# Optimizing a Trainium2 kernel written in Bass

```python
import jax
import jax.numpy as jnp
from jax import lax
import numpy as np

D_MODEL = 1024
BATCH = 1
SEQ = 512
DEPTH = 2
DEC_BATCH = 1
DEC_SEQ = 64
PAST_LEN = 512

CHUNK = 64
Q_BLOCK = 128
EPS = 1e-6
D_RNN = D_MODEL
LRU_BLOCKS = 16
LRU_BLOCK_W = D_RNN // LRU_BLOCKS
CONV_W = 4
LRU_C = 8.0
N_HEADS = 16
NOPE_DIM = 64
ROPE_DIM = 32
QK_DIM = NOPE_DIM + ROPE_DIM
V_DIM = D_MODEL // N_HEADS
Q_LORA = 384
KV_LORA = 256
ROPE_BASE = 10000.0
N_MEM = 256
MEM_HEADS = 4
MEM_HEAD_DIM = D_MODEL // MEM_HEADS
D_FF = 2816
N_EXPERTS = 8
TOP_K = 2
EXPERT_FF = 1024
N_DENSE = (DEPTH + 1) // 2
N_MOE = DEPTH // 2
SPLIT_POINTS = (D_RNN, 2 * D_RNN, 2 * D_RNN + Q_LORA, 2 * D_RNN + Q_LORA + KV_LORA,
                2 * D_RNN + Q_LORA + KV_LORA + ROPE_DIM, 2 * D_RNN + Q_LORA + KV_LORA + ROPE_DIM + D_MODEL)
IN_COLS = 2 * D_RNN + Q_LORA + KV_LORA + ROPE_DIM + 2 * D_MODEL

kernel_name = 'hybrid_rglru_mla_stream_step'

def rms_norm(x, g):
    xf = x.astype(jnp.float32)
    y = xf * lax.rsqrt(jnp.mean(xf * xf, axis=-1, keepdims=True) + EPS)
    return (y * g.astype(jnp.float32)).astype(x.dtype)

def apply_rope(x, pos):
    half = ROPE_DIM // 2
    inv_freq = ROPE_BASE ** (-jnp.arange(half, dtype=jnp.float32) / half)
    ang = pos.astype(jnp.float32)[:, None] * inv_freq[None, :]
    ang = ang.reshape((ang.shape[0],) + (1,) * (x.ndim - 3) + (half,))
    cos, sin = jnp.cos(ang), jnp.sin(ang)
    xf = x.astype(jnp.float32)
    x1, x2 = xf[..., :half], xf[..., half:]
    return jnp.concatenate([x1 * cos - x2 * sin, x1 * sin + x2 * cos], axis=-1).astype(x.dtype)

def causal_conv(x, prev, w, b):
    L = x.shape[1]
    xp = jnp.concatenate([prev, x], axis=1)
    y = b + w[CONV_W - 1] * x
    for j in range(CONV_W - 1):
        y = y + w[j] * xp[:, j:j + L]
    return y, xp[:, L:]

def rg_lru(x, h0, wa, ba, wi, bi, lam):
    B, L, C = x.shape
    xb = x.reshape(B, L, LRU_BLOCKS, LRU_BLOCK_W)
    gate_r = jnp.einsum('blni,nij->blnj', xb, wa).reshape(B, L, C) + ba
    gate_i = jnp.einsum('blni,nij->blnj', xb, wi).reshape(B, L, C) + bi
    r = jax.nn.sigmoid(gate_r.astype(jnp.float32))
    i = jax.nn.sigmoid(gate_i.astype(jnp.float32))
    log_a = -LRU_C * r * jax.nn.softplus(-lam.astype(jnp.float32))
    a = jnp.exp(log_a)
    u = jnp.sqrt(-jnp.expm1(2.0 * log_a)) * (i * x.astype(jnp.float32))

    def combine(left, right):
        return left[0] * right[0], right[0] * left[1] + right[1]

    a_cum, u_cum = lax.associative_scan(combine, (a, u), axis=1)
    h = a_cum * h0.astype(jnp.float32)[:, None, :] + u_cum
    return h.astype(x.dtype), h[:, -1].astype(x.dtype)

def chunk_causal_attention(q, k, v, q_pos, k_pos):
    s = jnp.einsum('bqhd,bkhd->bhqk', q, k).astype(jnp.float32) * (QK_DIM ** -0.5)
    visible = (k_pos[None, :] // CHUNK) <= (q_pos[:, None] // CHUNK)
    s = jnp.where(visible[None, None], s, -jnp.inf)
    p = jax.nn.softmax(s, axis=-1).astype(v.dtype)
    return jnp.einsum('bhqk,bkhd->bqhd', p, v)

def blocked_attention(q, k, v, q_pos, k_pos):
    B, L, H, Dq = q.shape
    if L <= Q_BLOCK or L % Q_BLOCK:
        return chunk_causal_attention(q, k, v, q_pos, k_pos)
    nb = L // Q_BLOCK
    qb = q.reshape(B, nb, Q_BLOCK, H, Dq).transpose(1, 0, 2, 3, 4)
    pb = q_pos.reshape(nb, Q_BLOCK)
    ob = lax.map(lambda blk: chunk_causal_attention(blk[0], k, v, blk[1], k_pos), (qb, pb))
    return ob.transpose(1, 0, 2, 3, 4).reshape(B, L, H, v.shape[-1])

def memory_kv(mem, g_in, w_k, w_v, g_k):
    B, M, _ = mem.shape
    m = rms_norm(mem, g_in)
    k = rms_norm((m @ w_k).reshape(B, M, MEM_HEADS, MEM_HEAD_DIM), g_k)
    v = (m @ w_v).reshape(B, M, MEM_HEADS, MEM_HEAD_DIM)
    return k, v

def memory_attention(h, mem_k, mem_v, w_q, g_q, w_o):
    B, L, _ = h.shape
    q = rms_norm((h @ w_q).reshape(B, L, MEM_HEADS, MEM_HEAD_DIM), g_q)
    s = jnp.einsum('blhd,bmhd->bhlm', q, mem_k).astype(jnp.float32) * (MEM_HEAD_DIM ** -0.5)
    p = jax.nn.softmax(s, axis=-1).astype(mem_v.dtype)
    o = jnp.einsum('bhlm,bmhd->blhd', p, mem_v).reshape(B, L, D_MODEL)
    return o @ w_o

def swiglu(h, w1, w3, w2):
    return (jax.nn.silu(h @ w1) * (h @ w3)) @ w2

def moe_swiglu(h, w_router, b_router, w1, w3, w2):
    logits = (h @ w_router).astype(jnp.float32) + b_router.astype(jnp.float32)
    probs = jax.nn.softmax(logits, axis=-1)
    top_p, top_i = lax.top_k(probs, TOP_K)
    top_p = top_p / jnp.sum(top_p, axis=-1, keepdims=True)
    gates = jnp.einsum('blk,blke->ble', top_p,
                       jax.nn.one_hot(top_i, N_EXPERTS, dtype=jnp.float32)).astype(h.dtype)
    out = jnp.zeros_like(h)
    for e in range(N_EXPERTS):
        out = out + gates[..., e:e + 1] * swiglu(h, w1[e], w3[e], w2[e])
    return out

def setup_inputs(seed: int = 0) -> dict:
    key = jax.random.key(seed)
    ks = iter(jax.random.split(key, 64))
    f32 = jnp.float32

    def nrm(shape, scale):
        return jax.random.normal(next(ks), shape, f32) * scale

    def gain(shape):
        return 1.0 + nrm(shape, 0.02)

    u = jax.random.uniform(next(ks), (DEPTH, D_RNN), f32, 0.9, 0.999)
    s = u ** (1.0 / LRU_C)
    lru_lambda = jnp.log(s) - jnp.log1p(-s)
    return {
        'x_prompt': nrm((BATCH, SEQ, D_MODEL), 1.0),
        'x_sample': nrm((DEC_BATCH, DEC_SEQ, D_MODEL), 1.0),
        'cache_ckv': nrm((DEPTH, DEC_BATCH, PAST_LEN, KV_LORA), 1.0),
        'cache_krope': nrm((DEPTH, DEC_BATCH, PAST_LEN, ROPE_DIM), 1.0),
        'cache_mem_k': nrm((DEPTH, DEC_BATCH, N_MEM, MEM_HEADS, MEM_HEAD_DIM), 1.0),
        'cache_mem_v': nrm((DEPTH, DEC_BATCH, N_MEM, MEM_HEADS, MEM_HEAD_DIM), 1.0),
        'state_lru': nrm((DEPTH, DEC_BATCH, D_RNN), 0.5),
        'state_conv': nrm((DEPTH, DEC_BATCH, CONV_W - 1, D_RNN), 1.0),
        'mem_prompt': nrm((BATCH, N_MEM, D_MODEL), 1.0),
        'norm_mix': gain((DEPTH, D_MODEL)),
        'w_in': nrm((DEPTH, D_MODEL, IN_COLS), D_MODEL ** -0.5),
        'conv_w': nrm((DEPTH, CONV_W, D_RNN), CONV_W ** -0.5),
        'conv_b': nrm((DEPTH, D_RNN), 0.01),
        'lru_wa': nrm((DEPTH, LRU_BLOCKS, LRU_BLOCK_W, LRU_BLOCK_W), LRU_BLOCK_W ** -0.5),
        'lru_ba': nrm((DEPTH, D_RNN), 0.01),
        'lru_wi': nrm((DEPTH, LRU_BLOCKS, LRU_BLOCK_W, LRU_BLOCK_W), LRU_BLOCK_W ** -0.5),
        'lru_bi': nrm((DEPTH, D_RNN), 0.01),
        'lru_lambda': lru_lambda,
        'q_lat_norm': gain((DEPTH, Q_LORA)),
        'w_uq': nrm((DEPTH, Q_LORA, N_HEADS * QK_DIM), Q_LORA ** -0.5),
        'kv_lat_norm': gain((DEPTH, KV_LORA)),
        'w_uk': nrm((DEPTH, KV_LORA, N_HEADS * NOPE_DIM), KV_LORA ** -0.5),
        'w_uv': nrm((DEPTH, KV_LORA, N_HEADS * V_DIM), KV_LORA ** -0.5),
        'q_head_norm': gain((DEPTH, QK_DIM)),
        'k_head_norm': gain((DEPTH, QK_DIM)),
        'w_out': nrm((DEPTH, D_MODEL, D_MODEL), D_MODEL ** -0.5),
        'norm_mem': gain((DEPTH, D_MODEL)),
        'mem_in_norm': gain((DEPTH, D_MODEL)),
        'w_mq': nrm((DEPTH, D_MODEL, D_MODEL), D_MODEL ** -0.5),
        'w_mk': nrm((DEPTH, D_MODEL, D_MODEL), D_MODEL ** -0.5),
        'w_mv': nrm((DEPTH, D_MODEL, D_MODEL), D_MODEL ** -0.5),
        'w_mo': nrm((DEPTH, D_MODEL, D_MODEL), D_MODEL ** -0.5),
        'mq_head_norm': gain((DEPTH, MEM_HEAD_DIM)),
        'mk_head_norm': gain((DEPTH, MEM_HEAD_DIM)),
        'norm_ffn': gain((DEPTH, D_MODEL)),
        'ffn_w1': nrm((N_DENSE, D_MODEL, D_FF), D_MODEL ** -0.5),
        'ffn_w3': nrm((N_DENSE, D_MODEL, D_FF), D_MODEL ** -0.5),
        'ffn_w2': nrm((N_DENSE, D_FF, D_MODEL), D_FF ** -0.5),
        'moe_router': nrm((N_MOE, D_MODEL, N_EXPERTS), D_MODEL ** -0.5),
        'moe_router_b': nrm((N_MOE, N_EXPERTS), 0.01),
        'moe_w1': nrm((N_MOE, N_EXPERTS, D_MODEL, EXPERT_FF), D_MODEL ** -0.5),
        'moe_w3': nrm((N_MOE, N_EXPERTS, D_MODEL, EXPERT_FF), D_MODEL ** -0.5),
        'moe_w2': nrm((N_MOE, N_EXPERTS, EXPERT_FF, D_MODEL), EXPERT_FF ** -0.5),
    }

def reference(x_prompt, x_sample, cache_ckv, cache_krope, cache_mem_k, cache_mem_v, state_lru, state_conv,
              mem_prompt, norm_mix, w_in, conv_w, conv_b, lru_wa, lru_ba, lru_wi, lru_bi, lru_lambda,
              q_lat_norm, w_uq, kv_lat_norm, w_uk, w_uv, q_head_norm, k_head_norm, w_out,
              norm_mem, mem_in_norm, w_mq, w_mk, w_mv, w_mo, mq_head_norm, mk_head_norm,
              norm_ffn, ffn_w1, ffn_w3, ffn_w2, moe_router, moe_router_b, moe_w1, moe_w3, moe_w2):

    def layer(l, x, pos, past_pos, conv_prev, h0, ckv_past, kr_past, mem_k, mem_v):
        B, L, _ = x.shape
        h = rms_norm(x, norm_mix[l])
        x_rec, x_gate, c_q, c_kv, k_rot, g_rec, g_att = jnp.split(h @ w_in[l], SPLIT_POINTS, axis=-1)
        x_conv, conv_state = causal_conv(x_rec, conv_prev, conv_w[l], conv_b[l])
        h_rec, h_last = rg_lru(x_conv, h0, lru_wa[l], lru_ba[l], lru_wi[l], lru_bi[l], lru_lambda[l])
        rec_out = jax.nn.gelu(x_gate) * h_rec
        c_kv = rms_norm(c_kv, kv_lat_norm[l])
        k_rot = apply_rope(k_rot, pos)
        ckv_all = jnp.concatenate([ckv_past, c_kv], axis=1)
        kr_all = jnp.concatenate([kr_past, k_rot], axis=1)
        k_pos = jnp.concatenate([past_pos, pos])
        T = ckv_all.shape[1]
        q = (rms_norm(c_q, q_lat_norm[l]) @ w_uq[l]).reshape(B, L, N_HEADS, QK_DIM)
        q = jnp.concatenate([q[..., :NOPE_DIM], apply_rope(q[..., NOPE_DIM:], pos)], axis=-1)
        q = rms_norm(q, q_head_norm[l])
        k_nope = (ckv_all @ w_uk[l]).reshape(B, T, N_HEADS, NOPE_DIM)
        k = jnp.concatenate([k_nope, jnp.broadcast_to(kr_all[:, :, None, :], (B, T, N_HEADS, ROPE_DIM))], axis=-1)
        k = rms_norm(k, k_head_norm[l])
        v = (ckv_all @ w_uv[l]).reshape(B, T, N_HEADS, V_DIM)
        att_out = blocked_attention(q, k, v, pos, k_pos).reshape(B, L, N_HEADS * V_DIM)
        mixed = jax.nn.sigmoid(g_rec) * rec_out + jax.nn.sigmoid(g_att) * att_out
        x = x + mixed @ w_out[l]
        x = x + memory_attention(rms_norm(x, norm_mem[l]), mem_k, mem_v, w_mq[l], mq_head_norm[l], w_mo[l])
        hf = rms_norm(x, norm_ffn[l])
        j = l // 2
        if l % 2 == 0:
            x = x + swiglu(hf, ffn_w1[j], ffn_w3[j], ffn_w2[j])
        else:
            x = x + moe_swiglu(hf, moe_router[j], moe_router_b[j], moe_w1[j], moe_w3[j], moe_w2[j])
        return x, conv_state, h_last, c_kv, k_rot

    Bp, Lp, _ = x_prompt.shape
    dt_p = x_prompt.dtype
    pos_p = jnp.arange(Lp, dtype=jnp.int32)
    no_pos = jnp.zeros((0,), jnp.int32)
    zero_conv = jnp.zeros((Bp, CONV_W - 1, D_RNN), dt_p)
    zero_h = jnp.zeros((Bp, D_RNN), dt_p)
    no_ckv = jnp.zeros((Bp, 0, KV_LORA), dt_p)
    no_kr = jnp.zeros((Bp, 0, ROPE_DIM), dt_p)
    x = x_prompt
    p_ckv, p_kr, p_lru, p_conv, p_mk, p_mv = [], [], [], [], [], []
    for l in range(DEPTH):
        mk, mv = memory_kv(mem_prompt, mem_in_norm[l], w_mk[l], w_mv[l], mk_head_norm[l])
        x, cs, hl, ckv, kr = layer(l, x, pos_p, no_pos, zero_conv, zero_h, no_ckv, no_kr, mk, mv)
        p_ckv.append(ckv)
        p_kr.append(kr)
        p_lru.append(hl)
        p_conv.append(cs)
        p_mk.append(mk)
        p_mv.append(mv)
    y_prompt = x

    Ls = x_sample.shape[1]
    T_past = cache_ckv.shape[2]
    past_pos_s = jnp.arange(T_past, dtype=jnp.int32)
    pos_s = T_past + jnp.arange(Ls, dtype=jnp.int32)
    x = x_sample
    s_ckv, s_kr, s_lru, s_conv = [], [], [], []
    for l in range(DEPTH):
        x, cs, hl, ckv, kr = layer(l, x, pos_s, past_pos_s, state_conv[l], state_lru[l],
                                   cache_ckv[l], cache_krope[l], cache_mem_k[l], cache_mem_v[l])
        s_ckv.append(ckv)
        s_kr.append(kr)
        s_lru.append(hl)
        s_conv.append(cs)
    y_sample = x

    new_ckv_p = jnp.stack(p_ckv)
    new_krope_p = jnp.stack(p_kr)
    new_lru_p = jnp.stack(p_lru)
    new_conv_p = jnp.stack(p_conv)
    new_mem_k_p = jnp.stack(p_mk)
    new_mem_v_p = jnp.stack(p_mv)
    new_ckv_s = jnp.stack(s_ckv)
    new_krope_s = jnp.stack(s_kr)
    new_lru_s = jnp.stack(s_lru)
    new_conv_s = jnp.stack(s_conv)
    return (y_prompt, y_sample, new_ckv_p, new_krope_p, new_lru_p, new_conv_p, new_mem_k_p, new_mem_v_p,
            new_ckv_s, new_krope_s, new_lru_s, new_conv_s)


_drawn_inputs = setup_inputs


def setup_inputs(seed=0):
    import zlib

    import numpy as np

    out = dict(_drawn_inputs(seed))
    spreads = {}
    factors = {'lru_ba': 8.0,
     'lru_bi': 5.704,
     'q_lat_norm': 4.231,
     'kv_lat_norm': 2.918,
     'q_head_norm': 5.63,
     'k_head_norm': 8.0,
     'norm_mem': 3.903,
     'mem_in_norm': 2.821,
     'mq_head_norm': 6.256,
     'mk_head_norm': 2.832,
     'moe_router_b': 3.53}
    for name, (base, spread) in spreads.items():
        noise = np.random.default_rng([zlib.crc32(name.encode()), seed]).standard_normal(out[name].shape)
        drawn = base * np.exp(spread * noise) if base else spread * noise
        out[name] = jnp.asarray(drawn.astype(out[name].dtype))
    for name, factor in factors.items():
        out[name] = (out[name] * factor).astype(out[name].dtype)
    return out
```

```python
from contextlib import ExitStack

import concourse.bass as bass
from concourse import mybir

F32 = mybir.dt.float32
F32R = mybir.dt.float32r
I32 = mybir.dt.int32
U32 = mybir.dt.uint32
ALU = mybir.AluOpType
ACT = mybir.ActivationFunctionType
AX_X = mybir.AxisListType.X

P = 128
D = 1024
C = D // P
SEQ, NEW, PAST = 512, 64, 512
T = SEQ + NEW
HALF = T // 2
TT = 5
KT = 9
KEYS = SEQ + NEW + PAST
DEPTH = 2
N_HEADS, NOPE, ROPE, QK = 16, 64, 32, 96
Q_LORA, KV_LORA = 384, 256
LAT = Q_LORA + KV_LORA + ROPE
N_MEM, MEM_HEADS, MEM_D = 256, 4, 256
D_FF, EXPERTS, EXPERT_FF = 2816, 8, 1024
EPS = 1e-6
UW = 256
UNIT = C * UW
CONV = 580
LANDED = 96
PARAM_DMAS = DEPTH * 19
MASKED = -1e30
GELU_C = 0.7978845608028654

(R_MIX, R_CW, R_CB, R_BA, R_BI, R_LAM, R_NMEM, R_NFFN, R_CONV, R_LRU, R_MEMIN, R_QLAT, R_MQ, R_QH, R_KH) = (
    0, 1, 5, 6, 7, 8, 9, 10, 11, 14, 15, 16, 17, 18, 19)
ROWS = 20


class Tally:

    def __init__(self, engine):
        self.engine, self.base, self.cur, self.per, self.i = engine, {}, {}, {}, None

    def loop(self, turns, **per):
        assert self.i is None and not any(self.cur.values())
        self.per = per
        with self.engine.Fori(0, turns) as i:
            self.i = i
            yield i
        for name in set(per) | set(self.cur):
            assert self.cur.get(name, 0) == per.get(name, 0), (name, "per turn", self.cur.get(name, 0))
            self.base[name] = self.base.get(name, 0) + turns * per[name]
        self.cur, self.i = {}, None

    def next(self, name):
        if self.i is None:
            self.base[name] = self.base.get(name, 0) + 1
            return Mark(self.base[name], self.base[name], None, 0)
        self.cur[name] = self.cur.get(name, 0) + 1
        k = self.base.get(name, 0) + self.cur[name]
        return Mark(k, k, self.i, self.per.get(name, 0))

    def last(self, name, plus=0):
        v = self.base.get(name, 0) + self.cur.get(name, 0) + plus
        return v if self.i is None else self.i * self.per.get(name, 0) + v

    def skip(self, name, n):
        for _ in range(n):
            self.next(name)


class Mark:
    def __init__(self, n, k, i, per):
        self.k, self.i, self.per = k, i, per

    def at(self, plus=0, each=1):
        v = (self.k + plus) * each
        return v if self.i is None else self.i * (self.per * each) + v

    @property
    def n(self):
        return self.at()

    def slot(self, ring):
        assert self.i is None or self.per % ring == 0, (self.per, ring)
        return (self.k - 1) % ring

    def use(self, ring, each):
        v = ((self.k - 1) // ring + 1) * each
        return v if self.i is None else self.i * (self.per // ring * each) + v
PER = {
    ('mix', 'pe'): dict(unit=4, acc=8, xc_lo=1, tp=8),
    ('att', 'pe'): dict(unit=2, acc=30, ka=2, tp=32, q_sq=4, q_lo=4, p1=8, p0=4),
    ('out', 'pe'): dict(unit=2, acc=4),
    ('mem', 'pe'): dict(unit=6, acc=16, mk=2, mc_in=2, tp=12, mq_sq=4, mq_lo=2, pm=2, pms=2),
    ('dense', 'pe'): dict(unit=12, acc=24, hidden=4),
    ('moe', 'pe'): dict(gate_row=1, tp=4, unit=12, acc=24, hidden=4),
    ('mix', 'act'): dict(acc=8, unit=4, xc=1, g_z=1, tp=8, g_gelu=1, lru_w=1),
    ('att', 'act'): dict(acc=30, unit=2, tp=32, s_max=12, mix_sum=2),
    ('out', 'act'): dict(acc=4, unit=2),
    ('mem', 'act'): dict(acc=16, unit=6, mc_in=2, tp=12, s_max=4, mem_place=2),
    ('dense', 'act'): dict(acc=24, unit=12, f_hid=4),
    ('moe', 'act'): dict(tp=4, acc=24, unit=12, f_hid=4),
    ('mix', 'dve'): dict(acc=8, dve_step=13, unit=4, bd_hi=1, xc_hi=1, g_sq=1, g_th=1, tp=8, lru_t=2, lru_a=2, lru_sqrt=1, grec=1, gatt=1),
    ('att', 'dve'): dict(acc=30, v_hi=10, unit=2, k_sq=2, dve_step=108, q_sq=4, q_hi=4, tp=32, tp_hi=28, p_exp=12, mix_hi=2),
    ('out', 'dve'): dict(acc=4, unit=2, x_hi=4, x_sq=4, sq_sum=4),
    ('mem', 'dve'): dict(acc=16, mem_place=2, unit=6, mk_sq=4, dve_step=64, vm_hi=4, mq_hi=4, tp=12, tp_hi=10, p_exp=4, acc_hi=4),
    ('dense', 'dve'): dict(acc=24, unit=12, f_th=4, dve_step=4, f_hi=4, hidden=4),
    ('moe', 'dve'): dict(tp=4, acc=24, unit=12, f_th=4, dve_step=4, f_hi=4, hidden=4),
}


def unit3(ap):
    return ap.rearrange("p (c n) -> p c n", n=UW)


def stream_step_kernel(nc, ins, outs):
    ctx = ExitStack()
    with ctx:
        top = [(nc.sbuf_base + 31) // 32 * 32]

        def at(name, shape, dt, offset):
            return nc.alloc_sbuf_tensor_at(name, shape, dt, offset=offset)

        def nbytes(shape):
            n = 4
            for k in shape[1:]:
                n *= k
            return (n + 31) // 32 * 32

        def fixed(name, shape, dt=F32):
            t = at(name, shape, dt, top[0])
            top[0] += nbytes(shape)
            return t

        X = fixed("X", [P, C, T])
        RAW = fixed("RAW", [P, 2, UNIT])
        WH = fixed("WH", [P, 2, UNIT], F32R)
        WL = fixed("WL", [P, 2, UNIT], F32R)
        PT = fixed("PT", [P, C, DEPTH * ROWS])
        ident = fixed("ident", [P, P])
        ones = fixed("ones", [P, P])
        MK = fixed("MK", [1, 2 * P], F32R)
        SQ = fixed("SQ", [P, T])
        SQT = fixed("SQT", [P, T])
        RSTD = fixed("RSTD", [P, T])
        rt = fixed("rt", [P, 8])
        nwt = fixed("nwt", [P, 6, 24])
        sm = fixed("sm", [P, 64])
        LAM = fixed("LAM", [P, C, 8])
        HB = fixed("HB", [P, C, 2])
        HBT = fixed("HBT", [P, 2, 2])
        OUTC = fixed("OUTC", [P, C, 8])
        rp = fixed("rp", [P, KT, ROPE])
        krs = fixed("krs", [P, KT])
        OPERAND = nbytes([P, C, T])
        A0 = top[0]
        B0 = A0 + 2 * OPERAND
        W0 = B0 + 2 * OPERAND
        END = nc.sbuf_usable_end
        ends = {}

        def region(start, end=END):
            o = [start]

            def put(name, shape, dt=F32):
                t = at(name, shape, dt, o[0])
                o[0] += nbytes(shape)
                assert o[0] <= end, (name, o[0], end)
                ends[name] = o[0]
                return t
            return put

        put = region(A0, B0)
        XH, XL = put("XH", [P, C, T], F32R), put("XL", [P, C, T], F32R)
        put = region(B0, W0)
        YH, YL = put("YH", [P, C, T], F32R), put("YL", [P, C, T], F32R)
        put = region(B0, W0)
        REC, TGA = put("REC", [P, C, T]), put("TGA", [P, C, T])
        put = region(B0, W0)
        TOK = put("TOK", [P, TT, D])
        put = region(W0)
        PST = put("PST", [DEPTH * ROWS, D])
        put = region(W0)
        XP = put("XP", [P, 2, CONV + 4])
        XC = put("XC", [P, 2, CONV])
        XCH, XCL = put("XCH", [P, 2, CONV], F32R), put("XCL", [P, 2, CONV], F32R)
        TR = put("TR", [P, 2, CONV])
        TI = put("TI", [P, 2, CONV])
        LA = put("LA", [P, 2, CONV])
        LU = put("LU", [P, 2, CONV])
        G = put("G", [P, 2, T])
        BD = put("BD", [P, 2, C, P])
        BDH, BDL = put("BDH", [P, 2, 2, P], F32R), put("BDL", [P, 2, 2, P], F32R)
        put = region(W0)
        CQH, CQL = put("CQH", [P, 3, T], F32R), put("CQL", [P, 3, T], F32R)
        CKH, CKL = put("CKH", [P, 2, KEYS], F32R), put("CKL", [P, 2, KEYS], F32R)
        rest = ends["CKL"]
        Z = put("Z", [P, TT, LAT])
        CKP = put("CKP", [P, 4, KV_LORA])
        RPT = put("RPT", [P, TT, 2, ROPE])
        GKV = put("GKV", [P, KV_LORA])
        put = region(A0, B0)
        ZQ = put("ZQ", [P, TT, Q_LORA])
        KR1, KR2 = put("KR1", [P, TT, ROPE]), put("KR2", [P, TT, ROPE])
        KRS = put("KRS", [P, KT, ROPE])
        put = region(rest)
        QTH, QTL = put("QTH", [P, T], F32R), put("QTL", [P, T], F32R)
        PTH, PTL = put("PTH", [P, 4, SEQ], F32R), put("PTL", [P, 4, SEQ], F32R)
        PSH, PSL = put("PSH", [P, TT, NEW], F32R), put("PSL", [P, TT, NEW], F32R)
        P1 = put("P1A", [P, 384]), put("P1B", [P, 512])
        put = region(A0, B0)
        KF = put("KF", [P, KT, 2, 64])
        VH, VL = put("VH", [P, KT, 2, 64], F32R), put("VL", [P, KT, 2, 64], F32R)
        KA = put("KA", [P, KT, 2, P])
        KTH, KTL = put("KTH", [P, KEYS], F32R), put("KTL", [P, KEYS], F32R)
        P0 = at("P0", [P, 2, 288], F32, ends["KTL"])
        QSQ = put("QSQ", [P, T])
        AO = put("AO", [P, T])
        put = region(W0)
        MTH, MTL = put("MTH", [P, C, N_MEM], F32R), put("MTL", [P, C, N_MEM], F32R)
        GMK = put("GMK", [P, MEM_D])
        QF = put("QF", [P, 2, T])
        PM = at("PM", [P, 4, N_MEM], F32, ends["GMK"])
        VMH, VML = put("VMH", [P, 2, 2, MEM_D], F32R), put("VML", [P, 2, 2, MEM_D], F32R)
        KMH, KML = put("KMH", [P, 2, 2, N_MEM], F32R), put("KML", [P, 2, 2, N_MEM], F32R)
        QMH, QML = put("QMH", [P, 2, T], F32R), put("QML", [P, 2, T], F32R)
        MEM = at("MEM", [P, 2, D], F32, ends["QML"])
        MC = at("MC", [P, 2, 2, MEM_D], F32, ends["QML"])
        MF = at("MF", [P, 2, MEM_D], F32, ends["QML"] + nbytes([P, 4, MEM_D]))
        MV = at("MV", [P, 2, MEM_D], F32, ends["QML"] + nbytes([P, 6, MEM_D]))
        PMH, PML = put("PMH", [P, 2, T], F32R), put("PML", [P, 2, T], F32R)
        put = region(W0)
        H1 = put("H1", [P, 2, T])
        TH = put("TH", [P, 2, T])
        GR = put("GR", [P, T])
        HF = put("HF", [P, T])
        RW = put("RW", [P, C, EXPERTS])
        RWH, RWL = put("RWH", [P, C, EXPERTS], F32R), put("RWL", [P, C, EXPERTS], F32R)
        RB = put("RB", [P, EXPERTS])
        LG = put("LG", [P, 8, TT, EXPERTS])
        LI = put("LI", [P, TT, EXPERTS], U32)
        IOT = put("IOT", [P, EXPERTS])
        GT = put("GT", [EXPERTS, T])
        GM = put("GM", [EXPERTS, T])
        YO = put("YO", [P, 2, D])

        ACC = ctx.enter_context(nc.psum_tensor("ACC", [P, 2, 2, 512], F32))
        TP = ctx.enter_context(nc.psum_tensor("TP", [P, 4, 512], F32))

        class Semaphores(dict):
            def __missing__(self, name):
                self[name] = ctx.enter_context(nc.semaphore(name))
                return self[name]
        s = Semaphores()

        def halves(bank_pair):
            return bank_pair[:, :, 0:HALF]

        def rows(tt):
            return NEW if tt == 4 else P

        def row_of(tensor, c):
            return tensor[:, c, :] if isinstance(c, int) else tensor[:, bass.ds(c, 1), :].rearrange("p o t -> p (o t)")

        def gain_of(c, row):
            return PT[:, c, row:row + 1] if isinstance(c, int) else PT[:, bass.ds(c, 1), row]

        def key_parts(pair):
            return [(h, 1, kt, rows(kt)) for h, kt in enumerate(pair)] if 4 in pair or len(pair) == 1 else [(0, 2, pair[0], P)]

        def key_col(kt):
            return kt * P if kt < 5 else SEQ + NEW + (kt - 5) * P

        block = ctx.enter_context(nc.Block())

        @block.tensor
        def _(pe):
            t = Tally(pe)

            def product(out, a, b, first=True, last=True):
                nc.tensor.matmul(out, a[0], b[0], start=first, stop=False)
                nc.tensor.matmul(out, a[0], b[1], start=False, stop=False)
                return nc.tensor.matmul(out, a[1], b[0], start=False, stop=last)

            def open_acc():
                m = t.next("acc")
                pe.wait_ge(s["acc_free"], m.n)
                return ACC[:, m.slot(2)]

            def open_tp():
                m = t.next("tp")
                pe.wait_ge(s["tp_free"], m.n)
                return TP[:, m.slot(4)]

            def weights():
                m = t.next("unit")
                pe.wait_ge(s["w_lo"], m.at(2))
                k = m.slot(2)
                return WH[:, k], WL[:, k]

            def features(source, chunks=C):
                wh, wl = (unit3(w) for w in weights())
                for m in range(2):
                    bank = open_acc()
                    for c in range(chunks):
                        for h in range(2):
                            cols = slice(h * HALF, (h + 1) * HALF)
                            mm = product(bank[:, h, 0:HALF], (wh[:, c, m * P:(m + 1) * P], wl[:, c, m * P:(m + 1) * P]),
                                         (source[0][:, c, cols], source[1][:, c, cols]), c == 0, c == chunks - 1)
                    mm.then_inc(s["acc_ready"], 1)

            def norm_statistics():
                t.skip("sq_sum", C - 1)
                pe.wait_ge(s["sq_sum"], t.next("sq_sum").n)
                bank = open_tp()
                for tt in range(TT):
                    mm = nc.tensor.matmul(bank[0:rows(tt), tt:tt + 1], SQ[:, tt * P:tt * P + rows(tt)], ones[:, 0:1],
                                          start=True, stop=True)
                mm.then_inc(s["tp_ready"], 1)
                bank = open_acc()
                pe.wait_ge(s["diag"], t.next("diag").n)
                for tt in range(TT):
                    n = rows(tt)
                    mm = nc.tensor.matmul(bank[:, tt // 4, (tt % 4) * P:(tt % 4) * P + n], ones[0:n, :],
                                          SQT[0:n, tt * P:tt * P + n], start=True, stop=True)
                mm.then_inc(s["acc_ready"], 1)

            pe.wait_ge(s["consts"], 4)
            pe.wait_ge(s["params_in"], PARAM_DMAS * 16)
            bank = open_tp()
            for c in range(C):
                mm = nc.tensor.transpose(bank[:, c * DEPTH * ROWS:(c + 1) * DEPTH * ROWS], PST[:, c * P:(c + 1) * P],
                                         ident[0:DEPTH * ROWS, 0:DEPTH * ROWS])
            mm.then_inc(s["tp_ready"], 1)
            pe.wait_ge(s["tokens_in"], 32)
            for c in range(C):
                bank = open_acc()
                for tt in range(TT):
                    n = rows(tt)
                    mm = nc.tensor.transpose(bank[:, tt // 4, (tt % 4) * P:(tt % 4) * P + n],
                                             TOK[0:n, tt, c * P:(c + 1) * P], ident[0:n, 0:n])
                mm.then_inc(s["acc_ready"], 1)

            for layer in range(DEPTH):
                norm_statistics()
                for i in t.loop(C // 2, **PER["mix", "pe"]):
                    features((XH, XL))
                    features((XH, XL))
                    pe.wait_ge(s["xc_lo"], t.next("xc_lo").n)
                    for f in range(2):
                        for gate in range(2):
                            for h in range(2):
                                bank = open_tp()
                                cols = slice(h * (CONV // 2), (h + 1) * (CONV // 2))
                                product(bank[:, 0:CONV // 2], (BDH[:, gate, f, :], BDL[:, gate, f, :]),
                                        (XCH[:, f, cols], XCL[:, f, cols])).then_inc(s["tp_ready"], 1)
                    features((XH, XL))
                    features((XH, XL))
                for n in (UW, UW, LAT - 2 * UW):
                    wh, wl = (unit3(w) for w in weights())
                    for pair in ((0, 1), (2, 3), (4,)):
                        bank = open_acc()
                        for h, tt in enumerate(pair):
                            cols = slice(tt * P, tt * P + rows(tt))
                            for c in range(C):
                                mm = product(bank[0:rows(tt), h, 0:n], (XH[:, c, cols], XL[:, c, cols]),
                                             (wh[:, c, 0:n], wl[:, c, 0:n]), c == 0, c == C - 1)
                        mm.then_inc(s["acc_ready"], 1)
                pe.wait_ge(s["zq"], t.next("zq").n)
                for c in range(3):
                    bank = open_acc()
                    for tt in range(TT):
                        n = rows(tt)
                        mm = nc.tensor.transpose(bank[:, tt // 4, (tt % 4) * P:(tt % 4) * P + n],
                                                 ZQ[0:n, tt, c * P:(c + 1) * P], ident[0:n, 0:n])
                    mm.then_inc(s["acc_ready"], 1)
                pe.wait_ge(s["zkv"], t.next("zkv").n)
                for c in range(2):
                    bank = open_acc()
                    for tt in range(TT):
                        n = rows(tt)
                        mm = nc.tensor.transpose(bank[:, tt // 4, (tt % 4) * P:(tt % 4) * P + n],
                                                 Z[0:n, tt, Q_LORA + c * P:Q_LORA + (c + 1) * P], ident[0:n, 0:n])
                    mm.then_inc(s["acc_ready"], 1)
                pe.wait_ge(s["past_in"], 32 * (layer + 1))
                for c in range(2):
                    bank = open_tp()
                    for k in range(4):
                        mm = nc.tensor.transpose(bank[:, k * P:(k + 1) * P], CKP[:, k, c * P:(c + 1) * P], ident[:, :])
                    mm.then_inc(s["tp_ready"], 1)

                pe.wait_ge(s["tp_free"], t.last("tp", 4))
                for i in t.loop(4, **PER["att", "pe"]):
                    for group in range(2):
                        wh, wl = weights()
                        wq = [w[:, 0:768].rearrange("p (c h n) -> p c h n", c=3, h=2) for w in (wh, wl)]
                        wkv = [w[:, 768:1280].rearrange("p (c n) -> p c n", c=2) for w in (wh, wl)]
                        for pair in ((0, 1), (2, 3), (4, 5), (6, 7), (8,)):
                            bank = open_acc()
                            for h, kt in enumerate(pair):
                                cols = slice(key_col(kt), key_col(kt) + rows(kt))
                                for c in range(2):
                                    mm = product(bank[0:rows(kt), h, 0:UW], (CKH[:, c, cols], CKL[:, c, cols]),
                                                 (wkv[0][:, c, :], wkv[1][:, c, :]), c == 0, c == 1)
                            mm.then_inc(s["acc_ready"], 1)
                        for head in range(2):
                            bank = open_acc()
                            for c in range(3):
                                for h in range(2):
                                    cols = slice(h * HALF, (h + 1) * HALF)
                                    mm = product(bank[:, h, 0:HALF], (wq[0][:, c, head, :], wq[1][:, c, head, :]),
                                                 (CQH[:, c, cols], CQL[:, c, cols]), c == 0, c == 2)
                            mm.then_inc(s["acc_ready"], 1)
                            if head == 0:
                                pe.wait_ge(s["ka"], t.next("ka").n)
                            for tiles in ((0, 1, 2, 3), (5, 6, 7, 4), (8,)):
                                bank = open_tp()
                                for kt in tiles:
                                    at0 = key_col(kt) - key_col(min(tiles))
                                    mm = nc.tensor.transpose(bank[:, at0:at0 + rows(kt)], KA[0:rows(kt), kt, head, :],
                                                             ident[0:rows(kt), 0:rows(kt)])
                                mm.then_inc(s["tp_ready"], 1)
                            keys_turned = t.last("tp", 4)
                            bank = open_tp()
                            pe.wait_ge(s["q_sq"], t.next("q_sq").n)
                            for tt in range(TT):
                                mm = nc.tensor.matmul(bank[0:rows(tt), tt:tt + 1], QSQ[0:QK, tt * P:tt * P + rows(tt)],
                                                      ones[0:QK, 0:1], start=True, stop=True)
                            mm.then_inc(s["tp_ready"], 1)

                            def prompt_scores(pair):
                                bank = open_acc()
                                for h, tt in enumerate(pair):
                                    cols, n = slice(tt * P, (tt + 1) * P), (tt + 1) * P
                                    product(bank[:, h, 0:n], (QTH[:, cols], QTL[:, cols]), (KTH[:, 0:n], KTL[:, 0:n]),
                                            True, False)
                                    mm = nc.tensor.matmul(bank[:, h, n - P:n], MK[0:1, 0:P], MK[0:1, P:2 * P],
                                                          start=False, stop=True)
                                mm.then_inc(s["acc_ready"], 1)

                            def turn_probabilities(blocks):
                                bank = open_tp()
                                for k, (src, n) in enumerate(blocks):
                                    mm = nc.tensor.transpose(bank[:, k * n:(k + 1) * n], src, ident[0:n, 0:n])
                                mm.then_inc(s["tp_ready"], 1)

                            pe.wait_ge(s["q_lo"], t.next("q_lo").n)
                            pe.wait_ge(s["tp_free"], keys_turned)
                            prompt_scores((0, 1))
                            prompt_scores((2, 3))
                            pe.wait_ge(s["p1"], t.next("p1").n)
                            turn_probabilities([(P1[0][:, 0:P], P), (P1[1][:, 0:P], P), (P1[1][:, P:2 * P], P)])
                            bank = open_acc()
                            for h in range(2):
                                cols = slice(SEQ + h * HALF, SEQ + (h + 1) * HALF)
                                mm = product(bank[0:NEW, h, 0:HALF], (QTH[:, SEQ:T], QTL[:, SEQ:T]), (KTH[:, cols], KTL[:, cols]))
                            mm.then_inc(s["acc_ready"], 1)
                            pe.wait_ge(s["p1"], t.next("p1").n)
                            turn_probabilities([(P1[0][:, k * P:(k + 1) * P], P) for k in range(3)])
                            turn_probabilities([(P1[1][:, k * P:(k + 1) * P], P) for k in range(4)])
                            pe.wait_ge(s["p0"], t.next("p0").n)
                            bank = open_tp()
                            ps = P0[:, :, :].rearrange("p a b -> p (a b)")
                            for k in (1, 2, 3, 4, 0):
                                kt = k + 4
                                a0 = key_col(kt) - SEQ
                                turn = nc.tensor.matmul if k == 1 else nc.tensor.transpose
                                mm = turn(bank[0:rows(kt), k * NEW:(k + 1) * NEW], ps[0:NEW, a0:a0 + rows(kt)], ident[0:NEW, 0:NEW])
                            mm.then_inc(s["tp_ready"], 1)
                            pe.wait_ge(s["tp_free"], t.last("tp", 4))
                            bank = open_acc()
                            for j in range(4):
                                product(bank[:, 0, j * P:SEQ], tuple(v[:, j, :, :].rearrange("p a b -> p (a b)") for v in (VH, VL)),
                                        (PTH[:, j, j * P:SEQ], PTL[:, j, j * P:SEQ]), j == 0, j == 3)
                            for k, kt in enumerate(range(4, KT)):
                                n = rows(kt)
                                mm = product(bank[:, 1, 0:NEW], tuple(v[0:n, kt, :, :].rearrange("p a b -> p (a b)") for v in (VH, VL)),
                                             (PSH[0:n, k, :], PSL[0:n, k, :]), k == 0, k == TT - 1)
                            mm.then_inc(s["acc_ready"], 1)

                pe.wait_ge(s["mixed"], 8 * (layer + 1))
                for i in t.loop(2, **PER["out", "pe"]):
                    features((YH, YL))
                    features((YH, YL))
                norm_statistics()

                pe.wait_ge(s["mem_normed"], t.next("mem_normed").n)
                for pair in range(4):
                    bank = open_tp()
                    for c in range(2):
                        for mt in range(2):
                            mm = nc.tensor.transpose(bank[:, (c * 2 + mt) * P:(c * 2 + mt + 1) * P],
                                                     MEM[:, mt, (pair * 2 + c) * P:(pair * 2 + c + 1) * P], ident[:, :])
                    mm.then_inc(s["tp_ready"], 1)
                pe.wait_ge(s["tp_free"], t.last("tp", 4))
                for i in t.loop(2, **PER["mem", "pe"]):
                    for head in range(2):
                        for kv in range(2):
                            wh, wl = (unit3(w) for w in weights())
                            bank = open_acc()
                            for mt in range(2):
                                cols = slice(mt * P, (mt + 1) * P)
                                for c in range(C):
                                    mm = product(bank[:, mt, 0:UW], (MTH[:, c, cols], MTL[:, c, cols]),
                                                 (wh[:, c, :], wl[:, c, :]), c == 0, c == C - 1)
                            mm.then_inc(s["acc_ready"], 1)
                        features((XH, XL))
                        pe.wait_ge(s["mk"], t.next("mk").n)
                        pe.wait_ge(s["mc_in"], t.next("mc_in").at(0, 32))
                        for src in (MF, MC[:, :, 0, :]):
                            bank = open_tp()
                            for dc in range(2):
                                for mt in range(2):
                                    mm = nc.tensor.transpose(bank[:, (dc * 2 + mt) * P:(dc * 2 + mt + 1) * P],
                                                             src[:, mt, dc * P:(dc + 1) * P], ident[:, :])
                            mm.then_inc(s["tp_ready"], 1)
                        bank = open_tp()
                        t.skip("mq_sq", 1)
                        pe.wait_ge(s["mq_sq"], t.next("mq_sq").n)
                        for tt in range(TT):
                            for dc in range(2):
                                mm = nc.tensor.matmul(bank[0:rows(tt), tt:tt + 1], (SQ, SQT)[dc][:, tt * P:tt * P + rows(tt)],
                                                      ones[:, 0:1], start=dc == 0, stop=dc == 1)
                        mm.then_inc(s["tp_ready"], 1)
                        pe.wait_ge(s["mq_lo"], t.next("mq_lo").n)
                        bank = open_acc()
                        for tt in range(4):
                            for dc in range(2):
                                cols = slice(tt * P, (tt + 1) * P)
                                mm = product(bank[:, tt // 2, (tt % 2) * N_MEM:(tt % 2 + 1) * N_MEM],
                                             (QMH[:, dc, cols], QML[:, dc, cols]), (KMH[:, 0, dc, :], KML[:, 0, dc, :]),
                                             dc == 0, dc == 1)
                        mm.then_inc(s["acc_ready"], 1)
                        bank = open_acc()
                        for dc in range(2):
                            mm = product(bank[0:NEW, 0, 0:N_MEM], (QMH[:, dc, SEQ:T], QML[:, dc, SEQ:T]),
                                         (KMH[:, 1, dc, :], KML[:, 1, dc, :]), dc == 0, dc == 1)
                        mm.then_inc(s["acc_ready"], 1)
                        pe.wait_ge(s["pm"], t.next("pm").n)
                        for mt in range(2):
                            bank = open_tp()
                            for tt in range(4):
                                mm = nc.tensor.transpose(bank[:, tt * P:(tt + 1) * P], PM[:, tt, mt * P:(mt + 1) * P], ident[:, :])
                            mm.then_inc(s["tp_ready"], 1)
                        pe.wait_ge(s["pms"], t.next("pms").n)
                        bank = open_tp()
                        for mt, turn in enumerate((nc.tensor.matmul, nc.tensor.transpose)):
                            mm = turn(bank[:, mt * NEW:(mt + 1) * NEW], SQT[0:NEW, mt * P:(mt + 1) * P], ident[0:NEW, 0:NEW])
                        mm.then_inc(s["tp_ready"], 1)
                        pe.wait_ge(s["tp_free"], t.last("tp", 4))
                        for dc in range(2):
                            bank = open_acc()
                            for which, (b, cols, n) in enumerate(((0, slice(0, SEQ), SEQ), (1, slice(SEQ, T), NEW))):
                                for mt in range(2):
                                    mm = product(bank[:, b, 0:n], (VMH[:, which, mt, dc * P:(dc + 1) * P], VML[:, which, mt, dc * P:(dc + 1) * P]),
                                                 (PMH[:, mt, cols], PML[:, mt, cols]), mt == 0, mt == 1)
                            mm.then_inc(s["acc_ready"], 1)
                pe.wait_ge(s["acc_free"], t.last("acc", 2))
                for i in t.loop(2, **PER["out", "pe"]):
                    features((YH, YL))
                    features((YH, YL))
                norm_statistics()

                def ffn_piece(tiles):
                    for pair in range(tiles // 2):
                        features((XH, XL))
                        features((XH, XL))
                    t.skip("hidden", tiles // 2 - 1)
                    pe.wait_ge(s["hidden"], t.next("hidden").n)
                    for k in range(4):
                        features((YH, YL), tiles)

                if layer == 0:
                    for i in t.loop(2, **PER["dense", "pe"]):
                        ffn_piece(8)
                    ffn_piece(6)
                else:
                    pe.wait_ge(s["router"], t.next("router").n)
                    bank = open_tp()
                    for tt in range(TT):
                        cols = slice(tt * P, tt * P + rows(tt))
                        for c in range(C):
                            mm = product(bank[0:rows(tt), tt * EXPERTS:(tt + 1) * EXPERTS], (XH[:, c, cols], XL[:, c, cols]),
                                         (RWH[:, c, :], RWL[:, c, :]), c == 0, c == C - 1)
                    mm.then_inc(s["tp_ready"], 1)
                    bank = open_acc()
                    pe.wait_ge(s["gates"], t.next("gates").n)
                    for tt in range(TT):
                        n = rows(tt)
                        mm = nc.tensor.transpose(bank[0:EXPERTS, tt // 4, (tt % 4) * P:(tt % 4) * P + n], LG[0:n, 7, tt, :], ident[0:n, 0:n])
                    mm.then_inc(s["acc_ready"], 1)
                    for i in t.loop(EXPERTS, **PER["moe", "pe"]):
                        pe.wait_ge(s["gate_row"], t.next("gate_row").n)
                        for k in range(4):
                            bank = open_tp()
                            nc.tensor.matmul(bank[:, 0:T // 4], ones[0:EXPERTS, :], GM[:, k * (T // 4):(k + 1) * (T // 4)],
                                             start=True, stop=True).then_inc(s["tp_ready"], 1)
                        ffn_piece(8)

                pe.wait_ge(s["outc"], t.next("outc").n)
                bank = open_acc()
                for c in range(C):
                    mm = nc.tensor.transpose(bank[0:8, c // 4, (c % 4) * P:(c % 4 + 1) * P], OUTC[:, c, :], ident[:, :])
                mm.then_inc(s["acc_ready"], 1)

            pe.wait_ge(s["y_done"], 1)
            for tt in range(TT):
                bank = open_acc()
                for c in range(C):
                    mm = nc.tensor.transpose(bank[0:rows(tt), c // 4, (c % 4) * P:(c % 4 + 1) * P], X[:, c, tt * P:tt * P + rows(tt)],
                                             ident[:, :])
                mm.then_inc(s["acc_ready"], 1)

        @block.scalar
        def _(act):
            t = Tally(act)
            fn = nc.scalar.activation

            def split_high():
                m = t.next("unit")
                k = m.slot(2)
                act.wait_ge(s["landed%d" % k], m.use(2, LANDED))
                fn(WH[:, k], RAW[:, k], ACT.Copy).then_inc(s["w_hi"], 1)

            def unit_tiles():
                a = t.next("acc")
                act.wait_ge(s["acc_ready"], a.n)
                split_high()
                return a, t.next("acc")

            def emptied(m):
                act.wait_ge(s["acc_free"], m.at(2))

            def prepare(m, c, row):
                emptied(m)
                fn(row_of(XH, c), row_of(X, c), ACT.Copy, scale=gain_of(c, row)).then_inc(s["x_hi"], 1)
                fn(SQT[:], row_of(X, c), ACT.Square).then_inc(s["x_sq"], 1)

            def turned(parts):
                m = t.next("tp")
                act.wait_ge(s["tp_ready"], m.n)
                todo = parts(TP[:, m.slot(4)])
                for k, (out, src, *gain) in enumerate(todo):
                    ins_ = fn(out, src, ACT.Copy, **({"scale": gain[0]} if gain else {}))
                    if k == len(todo) - 1:
                        ins_.then_inc(s["tp_hi"], 1)

            def turned_acc(parts):
                m = t.next("acc")
                act.wait_ge(s["acc_ready"], m.n)
                todo = parts(ACC[:, m.slot(2)])
                for k, (out, src, *gain) in enumerate(todo):
                    ins_ = fn(out, src, ACT.Copy, **({"scale": gain[0]} if gain else {}))
                    if k == len(todo) - 1:
                        ins_.then_inc(s["acc_hi"], 1)

            def output_projection(row):
                for i in t.loop(2, **PER["out", "act"]):
                    for u in range(2):
                        for f, m in enumerate(unit_tiles()):
                            prepare(m, i * 4 + (2 * u + f), row)
                t.skip("tp", 1)
                t.skip("acc", 1)

            split_high()
            t.skip("tp", 1)
            act.wait_ge(s["params"], 1)
            for c in range(C):
                prepare(t.next("acc"), c, R_MIX)

            for layer in range(DEPTH):
                base = layer * ROWS
                t.skip("tp", 1)
                t.skip("acc", 1)
                act.wait_ge(s["lam_abs"], layer + 1)
                fn(LAM[:, :, 2], LAM[:, :, 1], ACT.Exp, scale=-1.0).then_inc(s["lam_exp"], 1)
                act.wait_ge(s["lam"], layer + 1)
                act.wait_ge(s["blocks_in"], 64 * (layer + 1))
                for i in t.loop(C // 2, **PER["mix", "act"]):
                    unit_tiles()
                    fn(BDH[:], BD[:, :, bass.ds(i * 2, 2), :], ACT.Copy).then_inc(s["bd_hi"], 1)
                    act.wait_ge(s["xc"], t.next("xc").n)
                    fn(XCH[:], XC[:], ACT.Copy).then_inc(s["xc_hi"], 1)
                    emptied(unit_tiles()[1])
                    fn(LU[:, :, 0:T], G[:], ACT.Square).then_inc(s["g_sq"], 1)
                    act.wait_ge(s["g_z"], t.next("g_z").n)
                    fn(LU[:, :, 0:T], LU[:, :, 0:T], ACT.Tanh, scale=GELU_C).then_inc(s["g_th"], 1)
                    for f in range(2):
                        for gate, dst in enumerate((TR, TI)):
                            for h in range(2):
                                m = t.next("tp")
                                act.wait_ge(s["tp_ready"], m.n)
                                fn(dst[:, f, h * (CONV // 2):(h + 1) * (CONV // 2)], TP[:, m.slot(4), 0:CONV // 2], ACT.Tanh,
                                   bias=HBT[:, f, gate:gate + 1], scale=0.5).then_inc(s["tp_free"], 1)
                    act.wait_ge(s["tp_free"], m.at(4))
                    act.wait_ge(s["g_gelu"], t.next("g_gelu").n)
                    for f in range(2):
                        sp, neg = (LAM[:, bass.ds(i * 2 + f, 1), j] for j in (0, 3))
                        fn(LU[:, f, :], TR[:, f, :], ACT.Tanh, bias=sp, scale=sp).then_inc(s["lru_t"], 1)
                        fn(LA[:, f, :], TR[:, f, :], ACT.Exp, bias=neg, scale=neg).then_inc(s["lru_a"], 1)
                    act.wait_ge(s["lru_w"], t.next("lru_w").n)
                    fn(TR[:], TR[:], ACT.Sqrt).then_inc(s["lru_sqrt"], 1)
                    emptied(unit_tiles()[1])
                    fn(TR[:, :, 0:T], TR[:, :, 0:T], ACT.Tanh, scale=0.5).then_inc(s["grec"], 1)
                    emptied(unit_tiles()[1])
                    pair = TGA[:, bass.ds(i * 2, 2), :]
                    fn(pair, pair, ACT.Tanh, scale=0.5).then_inc(s["gatt"], 1)

                for n in range(3):
                    unit_tiles()
                    t.skip("acc", 1)
                q_gain = [PT[:, c, base + R_QLAT:base + R_QLAT + 1] for c in range(3)]
                for c in range(3):
                    turned_acc(lambda b: [(CQH[:, c, 0:SEQ], b[:, 0, :], q_gain[c]), (CQH[:, c, SEQ:T], b[:, 1, 0:NEW], q_gain[c])])
                for c in range(2):
                    turned_acc(lambda b: [(CKH[:, c, 0:SEQ], b[:, 0, :]), (CKH[:, c, SEQ:T], b[:, 1, 0:NEW])])
                for c in range(2):
                    turned(lambda b: [(CKH[:, c, T:KEYS], b)])
                act.wait_ge(s["latents_out"], 64 * (layer + 1))

                for i in t.loop(4, **PER["att", "act"]):
                    for group in range(2):
                        for n, pair in enumerate(((0, 1), (2, 3), (4, 5), (6, 7), (8,))):
                            m = t.next("acc")
                            act.wait_ge(s["acc_ready"], m.n)
                            bank = ACC[:, m.slot(2)]
                            parts = key_parts(pair)
                            for k, (h, w, kt, r) in enumerate(parts):
                                ins_ = fn(VH[0:r, kt:kt + w].rearrange("p t a b -> p t (a b)"), bank[0:r, h:h + w, P:2 * P], ACT.Copy)
                            ins_.then_inc(s["v_hi"], 1)
                            if n == 0:
                                split_high()
                        emptied(m)
                        fn(KA[:, :, :, 0:NOPE], KF[:], ACT.Square).then_inc(s["k_sq"], 1)
                        for head in range(2):
                            m = t.next("acc")
                            act.wait_ge(s["acc_ready"], m.n)
                            fn(QSQ[0:QK, :].rearrange("p (a b) -> p a b", a=2), halves(ACC[0:QK, m.slot(2)]), ACT.Square)\
                                .then_inc(s["q_sq"], 1)
                            emptied(m)
                            fn(QTH[:], SQ[:], ACT.Copy).then_inc(s["q_hi"], 1)
                            turned(lambda b: [(KTH[:, 0:SEQ], b)])
                            turned(lambda b: [(KTH[:, SEQ:SEQ + 448], b[:, 0:448])])
                            turned(lambda b: [(KTH[:, SEQ + 448:KEYS], b[:, 0:P])])
                            t.skip("tp", 1)

                            def exponentials(tiles, dst, r):
                                m = t.next("acc")
                                act.wait_ge(s["s_max"], t.next("s_max").n)
                                for k, (tt, n) in enumerate(tiles):
                                    ins_ = fn(dst[k][0:r, 0:n], ACC[0:r, m.slot(2), k, 0:n], ACT.Exp, bias=sm[0:r, 8 + tt:9 + tt],
                                              scale=sm[0:r, 24 + tt:25 + tt], accum_out=sm[0:r, 16 + tt:17 + tt])
                                ins_.then_inc(s["p_exp"], 1)

                            exponentials(((0, P), (1, 2 * P)), P1, P)
                            act.wait_ge(s["tp_ready"], t.last("tp", 1))
                            exponentials(((2, 3 * P), (3, 4 * P)), P1, P)
                            turned(lambda b: [(PTH[:, 0, 0:P], b[:, 0:P]),
                                              (PTH[:, 0:2, P:2 * P], b[:, P:3 * P].rearrange("p (a b) -> p a b", a=2))])
                            m = t.next("acc")
                            act.wait_ge(s["s_max"], t.next("s_max").n)
                            fn(P0[0:NEW], halves(ACC[0:NEW, m.slot(2)]), ACT.Exp, bias=sm[0:NEW, 12:13], scale=sm[0:NEW, 28:29],
                               accum_out=sm[0:NEW, 20:21]).then_inc(s["p_exp"], 1)
                            turned(lambda b: [(PTH[:, 0:3, 2 * P:3 * P], b[:, 0:3 * P].rearrange("p (a b) -> p a b", a=3))])
                            turned(lambda b: [(PTH[:, 0:4, 3 * P:4 * P], b.rearrange("p (a b) -> p a b", a=4))])
                            turned(lambda b: [(PSH[0:NEW, 0, :], b[0:NEW, 0:NEW]),
                                              (PSH[:, 1:TT, :], b[:, NEW:TT * NEW].rearrange("p (a b) -> p a b", a=4))])
                            t.skip("acc", 1)
                        act.wait_ge(s["mix_sum"], t.next("mix_sum").n)
                        fn(YH[:, bass.ds(i * 2 + group, 1), :], AO[:].rearrange("p (a b) -> p a b", a=1), ACT.Copy, scale=0.25)\
                            .then_inc(s["mix_hi"], 1)

                output_projection(base + R_NMEM)

                act.wait_ge(s["mem_in"], 32 * (layer + 1))
                for mt in range(2):
                    if mt:
                        act.wait_ge(s["mem_sq"], 2 * layer + 1)
                    fn(QF[:].rearrange("p a b -> p (a b)")[:, 0:D], MEM[:, mt, :], ACT.Square, accum_out=sm[:, mt:mt + 1])\
                        .then_inc(s["mem_sq"], 1)
                for p4 in range(4):
                    turned(lambda b: [(MTH[:, 2 * p4 + c, :], b[:, c * 2 * P:(c + 1) * 2 * P],
                                       PT[:, 2 * p4 + c, base + R_MEMIN:base + R_MEMIN + 1]) for c in range(2)])
                for i in t.loop(2, **PER["mem", "act"]):
                    for head in range(2):
                        m = t.next("acc")
                        act.wait_ge(s["acc_ready"], m.n)
                        split_high()
                        emptied(m)
                        for mt in range(2):
                            fn(QF[:, mt, 0:MEM_D], MF[:, mt, :], ACT.Square, accum_out=sm[:, mt:mt + 1]).then_inc(s["mk_sq"], 1)
                        m = t.next("acc")
                        act.wait_ge(s["acc_ready"], m.n)
                        split_high()
                        emptied(m)
                        fn(VMH[:, 0], MV[:], ACT.Copy).then_inc(s["vm_hi"], 1)
                        act.wait_ge(s["mc_in"], t.next("mc_in").at(0, 32))
                        fn(VMH[:, 1], MC[:, :, 1, :], ACT.Copy).then_inc(s["vm_hi"], 1)
                        for dc, m in enumerate(unit_tiles()):
                            emptied(m)
                            fn((SQ, SQT)[dc][:], QF[:, dc, :], ACT.Square).then_inc(s["mq_sq"], 1)
                            fn(QMH[:, dc, :], QF[:, dc, :], ACT.Copy, scale=PT[:, dc, base + R_MQ:base + R_MQ + 1])\
                                .then_inc(s["mq_hi"], 1)
                        for which in range(2):
                            turned(lambda b: [(KMH[:, which].rearrange("p a b -> p (a b)"), b)])
                        t.skip("tp", 1)
                        m = t.next("acc")
                        act.wait_ge(s["s_max"], t.next("s_max").n)
                        for tt in range(4):
                            ins_ = fn(PM[:, tt, :], ACC[:, m.slot(2), tt // 2, (tt % 2) * N_MEM:(tt % 2 + 1) * N_MEM], ACT.Exp,
                                      bias=sm[:, 8 + tt:9 + tt], scale=sm[:, 24 + tt:25 + tt], accum_out=sm[:, 16 + tt:17 + tt])
                        ins_.then_inc(s["p_exp"], 1)
                        m = t.next("acc")
                        act.wait_ge(s["s_max"], t.next("s_max").n)
                        fn(SQT[0:NEW, 0:N_MEM], ACC[0:NEW, m.slot(2), 0, 0:N_MEM], ACT.Exp, bias=sm[0:NEW, 12:13], scale=sm[0:NEW, 28:29],
                           accum_out=sm[0:NEW, 20:21]).then_inc(s["p_exp"], 1)
                        act.wait_ge(s["mem_place"], t.next("mem_place").at(1))
                        for mt in range(2):
                            turned(lambda b: [(PMH[:, mt, 0:SEQ], b)])
                        turned(lambda b: [(PMH[:, :, SEQ:T], b[:, 0:2 * NEW].rearrange("p (a b) -> p a b", a=2))])
                        for dc in range(2):
                            row = bass.ds(i * 4 + (2 * head + dc), 1)
                            turned_acc(lambda b: [(YH[:, row, 0:SEQ], b[:, 0:1, :]), (YH[:, row, SEQ:T], b[:, 1:2, 0:NEW])])
                output_projection(base + R_NFFN)

                def hidden_tiles(tiles):
                    for pair in range(tiles // 2):
                        emptied(unit_tiles()[1])
                        fn(TH[:], H1[:], ACT.Tanh, scale=0.5).then_inc(s["f_th"], 1)
                        unit_tiles()
                        act.wait_ge(s["f_hid"], t.next("f_hid").n)
                        fn(YH[:, 2 * pair:2 * pair + 2, :], H1[:], ACT.Copy).then_inc(s["f_hi"], 1)

                if layer == 0:
                    for i in t.loop(2, **PER["dense", "act"]):
                        hidden_tiles(8)
                        for k in range(4):
                            unit_tiles()
                    hidden_tiles(6)
                    for k in range(4):
                        for f, m in enumerate(unit_tiles()):
                            prepare(m, 2 * k + f, ROWS + R_MIX)
                else:
                    act.wait_ge(s["router_in"], 48)
                    fn(RWH[:], RW[:], ACT.Copy).then_inc(s["router_hi"], 1)
                    t.skip("tp", 1)
                    t.skip("acc", 1)
                    act.wait_ge(s["lg_shift"], 1)
                    fn(LG[:, 1], LG[:, 1], ACT.Exp).then_inc(s["lg_exp"], 1)
                    for i in t.loop(EXPERTS, **PER["moe", "act"]):
                        t.skip("tp", 4)
                        hidden_tiles(8)
                        for k in range(4):
                            unit_tiles()
                t.skip("acc", 1)

        @block.vector
        def _(dve):
            t = Tally(dve)
            v = nc.vector

            def step(ins_):
                ins_.then_inc(s["dve_step"], 1)
                dve.wait_ge(s["dve_step"], t.next("dve_step").n)

            def split_low():
                m = t.next("unit")
                k = m.slot(2)
                dve.wait_ge(s["w_hi"], m.n)
                v.tensor_tensor(WL[:, k], RAW[:, k], WH[:, k].bitcast(F32), ALU.subtract).then_inc(s["w_lo"], 1)

            def take_acc():
                m = t.next("acc")
                dve.wait_ge(s["acc_ready"], m.n)
                return ACC[:, m.slot(2)], m

            def take_tp():
                m = t.next("tp")
                dve.wait_ge(s["tp_ready"], m.n)
                return TP[:, m.slot(4)], m

            def turned(parts):
                bank, m = take_tp()
                dve.wait_ge(s["tp_hi"], t.next("tp_hi").n)
                lows(parts(bank)).then_inc(s["tp_free"], 1)

            def turned_acc(parts):
                bank, m = take_acc()
                dve.wait_ge(s["acc_hi"], t.next("acc_hi").n)
                lows(parts(bank)).then_inc(s["acc_free"], 1)

            def lows(todo):
                for out, src, high, *gain in todo:
                    if gain:
                        ins_ = v.scalar_tensor_tensor(out=out, in0=src, scalar=gain[0], in1=high.bitcast(F32), op0=ALU.mult, op1=ALU.subtract)
                    else:
                        ins_ = v.tensor_tensor(out, src, high.bitcast(F32), ALU.subtract)
                return ins_

            def rsqrt(n):
                x, b, y, q = (nwt[:, k, 0:n] for k in range(4))
                step(v.tensor_scalar(b.bitcast(U32), x.bitcast(U32), 1, None, ALU.logical_shift_right))
                step(v.tensor_scalar(y.bitcast(I32), b.bitcast(I32), -1.0, 1597463007.0, ALU.mult, ALU.add))
                for _ in range(4):
                    step(v.scalar_tensor_tensor(out=q, in0=x, scalar=-0.5, in1=y, op0=ALU.mult, op1=ALU.mult))
                    step(v.tensor_tensor(q, q, y, ALU.mult))
                    step(v.scalar_tensor_tensor(out=y, in0=q, scalar=1.5, in1=y, op0=ALU.add, op1=ALU.mult))

            def token_means(bank, m, width):
                v.tensor_scalar(nwt[:, 0, 0:4], bank[:, 0:4], 1.0 / width, EPS, ALU.mult, ALU.add)
                v.tensor_scalar(nwt[0:NEW, 0, 4:5], bank[0:NEW, 4:5], 1.0 / width, EPS, ALU.mult, ALU.add).then_inc(s["tp_free"], 1)
                dve.wait_ge(s["tp_free"], m.at(4))

            def norm_statistics():
                bank, m = take_tp()
                token_means(bank, m, D)
                rsqrt(TT)
                step(v.tensor_copy(rt[:, 0:TT], nwt[:, 2, 0:TT]))
                for tt in range(TT):
                    n = rows(tt)
                    ins_ = v.tensor_scalar(SQT[0:n, tt * P:tt * P + n], ident[0:n, 0:n], rt[0:n, tt:tt + 1], None, ALU.mult)
                ins_.then_inc(s["diag"], 1)
                bank, m = take_acc()
                v.tensor_copy(RSTD[:, 0:SEQ], bank[:, 0, :])
                v.tensor_copy(RSTD[:, SEQ:T], bank[:, 1, 0:NEW]).then_inc(s["acc_free"], 1)
                dve.wait_ge(s["acc_free"], m.at(2))

            def prepare(c, row):
                dve.wait_ge(s["x_hi"], t.next("x_hi").n)
                v.scalar_tensor_tensor(out=row_of(XL, c), in0=row_of(X, c), scalar=gain_of(c, row), in1=row_of(XH, c).bitcast(F32),
                                       op0=ALU.mult, op1=ALU.subtract)
                dve.wait_ge(s["x_sq"], t.next("x_sq").n)
                v.tensor_tensor(SQ[:], SQ[:], SQT[:], ALU.add).then_inc(s["sq_sum"], 1)
                dve.wait_ge(s["sq_sum"], t.next("sq_sum").n)

            def add_residual(bank, m, c):
                x = row_of(X, c).rearrange("p (a b) -> p a b", a=2)
                v.tensor_tensor(x, halves(bank), x, ALU.add).then_inc(s["acc_free"], 1)

            def scaled(out, bank, by):
                a2 = lambda ap: ap.rearrange("p o (a b) -> p (o a) b", a=2) if len(ap.shape) == 3 else ap.rearrange("p (a b) -> p a b", a=2)
                return v.tensor_tensor(a2(out), halves(bank), a2(by), ALU.mult).then_inc(s["acc_free"], 1)

            def output_projection(row):
                step(v.memset(SQ[:], 0.0))
                for i in t.loop(2, **PER["out", "dve"]):
                    for u in range(2):
                        for f in range(2):
                            bank, m = take_acc()
                            c = i * 4 + (2 * u + f)
                            add_residual(bank, m, c)
                            if f == 0:
                                split_low()
                            dve.wait_ge(s["acc_free"], m.at(2))
                            prepare(c, row)
                norm_statistics()

            def marker(name):
                k = ("w_free", "params", "lam_abs", "lam", "mc_free", "mq_lo", "y_done", "outc", "state_rows", "y_rows").index(name)
                return v.memset(nwt[:, 5, k:k + 1], 0.0)

            def w_region_free():
                marker("w_free").then_inc(s["w_free"], 1)

            v.memset(nwt[:], 1.0)
            v.memset(sm[:], 1.0)
            v.memset(rp[:], 0.0)
            v.memset(OUTC[:], 0.0)
            step(v.memset(SQ[:], 0.0))
            split_low()
            bank, m = take_tp()
            v.tensor_copy(PT[:], bank[:, 0:C * DEPTH * ROWS].rearrange("p (c r) -> p c r", c=C)).then_inc(s["tp_free"], 1)
            dve.wait_ge(s["tp_free"], m.at(4))
            marker("params").then_inc(s["params"], 1)
            for c in range(C):
                bank, m = take_acc()
                v.tensor_copy(X[:, c, 0:SEQ], bank[:, 0, :])
                v.tensor_copy(X[:, c, SEQ:T], bank[:, 1, 0:NEW]).then_inc(s["acc_free"], 1)
                dve.wait_ge(s["acc_free"], m.at(2))
                prepare(c, R_MIX)

            for layer in range(DEPTH):
                base = layer * ROWS
                w_region_free()
                lam = PT[:, :, base + R_LAM]
                L = [LAM[:, :, k] for k in range(8)]
                step(v.tensor_scalar(L[0], lam, -1.0, None, ALU.mult))
                step(v.tensor_tensor(L[1], L[0], lam, ALU.max))
                marker("lam_abs").then_inc(s["lam_abs"], 1)
                step(v.tensor_scalar(L[4], L[0], 0.0, 4.0, ALU.max, ALU.mult))
                dve.wait_ge(s["lam_exp"], layer + 1)
                step(v.tensor_scalar(L[5], L[2], 2.0, None, ALU.add))
                step(v.reciprocal(L[5], L[5]))
                step(v.tensor_tensor(L[5], L[5], L[2], ALU.mult))
                step(v.tensor_tensor(L[6], L[5], L[5], ALU.mult))
                step(v.tensor_scalar(L[7], L[6], 1.0 / 19, 1.0 / 17, ALU.mult, ALU.add))
                for k in (15, 13, 11, 9, 7, 5, 3, 1):
                    step(v.tensor_tensor(L[7], L[7], L[6], ALU.mult))
                    step(v.tensor_scalar(L[7], L[7], 1.0 / k, None, ALU.add))
                step(v.tensor_tensor(L[7], L[7], L[5], ALU.mult))
                step(v.scalar_tensor_tensor(out=L[0], in0=L[7], scalar=8.0, in1=L[4], op0=ALU.mult, op1=ALU.add))
                step(v.tensor_scalar(L[3], L[0], -1.0, None, ALU.mult))
                step(v.tensor_scalar(HB[:], PT[:, :, base + R_BA:base + R_BA + 2], 0.5, None, ALU.mult))
                if layer:
                    dve.wait_ge(s["state_out"], 64 * layer)
                v.memset(XP[:, :, 0:3], 0.0)
                step(v.memset(XP[:, :, CONV + 2:CONV + 4], 0.0))
                marker("lam").then_inc(s["lam"], 1)
                norm_statistics()
                dve.wait_ge(s["blocks_in"], 64 * (layer + 1))

                for i in t.loop(C // 2, **PER["mix", "dve"]):
                    pair = bass.ds(i * 2, 2)
                    for f in range(2):
                        bank, m = take_acc()
                        step(v.tensor_copy(XP[:, f:f + 1, SEQ + 3:SEQ + 6], PT[:, bass.ds(i * 2 + f, 1), base + R_CONV:base + R_CONV + 3]))
                        v.tensor_tensor(XP[:, f, 3:3 + HALF], bank[:, 0, 0:HALF], RSTD[:, 0:HALF], ALU.mult)
                        v.tensor_tensor(XP[:, f, 3 + HALF:3 + SEQ], bank[:, 1, 0:SEQ - HALF], RSTD[:, HALF:SEQ], ALU.mult)
                        v.tensor_tensor(XP[:, f, SEQ + 6:T + 6], bank[:, 1, SEQ - HALF:HALF], RSTD[:, SEQ:T], ALU.mult)\
                            .then_inc(s["acc_free"], 1)
                        if f == 0:
                            split_low()
                    v.tensor_copy(HBT[:], HB[:, pair, :])
                    dve.wait_ge(s["bd_hi"], t.next("bd_hi").n)
                    v.tensor_tensor(BDL[:], BD[:, :, pair, :], BDH[:].bitcast(F32), ALU.subtract)
                    dve.wait_ge(s["acc_free"], m.at(2))
                    v.tensor_copy(OUTC[:, pair, 0:3], XP[:, :, SEQ:SEQ + 3])
                    v.tensor_copy(OUTC[:, pair, 4:7], XP[:, :, T + 3:T + 6])
                    for j in range(4):
                        for f in range(2):
                            ch = bass.ds(i * 2 + f, 1)
                            w = PT[:, ch, base + R_CW + j]
                            if j == 0:
                                ins_ = v.tensor_scalar(XC[:, f, :], XP[:, f, 0:CONV], w, PT[:, ch, base + R_CB], ALU.mult, ALU.add)
                            else:
                                ins_ = v.scalar_tensor_tensor(out=XC[:, f, :], in0=XP[:, f, j:j + CONV], scalar=w, in1=XC[:, f, :],
                                                              op0=ALU.mult, op1=ALU.add)
                            if (j, f) == (3, 1):
                                ins_.then_inc(s["xc"], 1)
                            elif f == 1:
                                step(ins_)
                    dve.wait_ge(s["xc_hi"], t.next("xc_hi").n)
                    v.tensor_tensor(XCL[:], XC[:], XCH[:].bitcast(F32), ALU.subtract).then_inc(s["xc_lo"], 1)
                    for f in range(2):
                        bank, m = take_acc()
                        scaled(G[:, f, :], bank, RSTD[:])
                        if f == 0:
                            split_low()
                    dve.wait_ge(s["g_sq"], t.next("g_sq").n)
                    z = LU[:, :, 0:T]
                    step(v.tensor_scalar(z, z, 0.044715, 1.0, ALU.mult, ALU.add))
                    v.tensor_tensor(z, z, G[:], ALU.mult).then_inc(s["g_z"], 1)
                    dve.wait_ge(s["g_th"], t.next("g_th").n)
                    v.scalar_tensor_tensor(out=G[:], in0=z, scalar=1.0, in1=G[:], op0=ALU.add, op1=ALU.mult).then_inc(s["g_gelu"], 1)
                    t.skip("tp", 8)
                    dve.wait_ge(s["lru_t"], t.next("lru_t").at(1))
                    t.skip("lru_t", 1)
                    dve.wait_ge(s["lru_a"], t.next("lru_a").at(1))
                    t.skip("lru_a", 1)
                    step(v.tensor_scalar(TR[:], LU[:], 1.0, None, ALU.add))
                    step(v.reciprocal(TR[:], TR[:]))
                    step(v.tensor_tensor(TR[:], TR[:], LU[:], ALU.mult))
                    v.tensor_scalar(TR[:], TR[:], 0.5, 0.0, ALU.mult, ALU.max).then_inc(s["lru_w"], 1)
                    step(v.scalar_tensor_tensor(out=TI[:], in0=TI[:], scalar=1.0, in1=XC[:], op0=ALU.add, op1=ALU.mult))
                    dve.wait_ge(s["lru_sqrt"], t.next("lru_sqrt").n)
                    step(v.tensor_tensor(LU[:], TI[:], TR[:], ALU.mult))
                    for f in range(2):
                        v.tensor_tensor_scan(TI[:, f, 0:SEQ], LA[:, f, 0:SEQ], LU[:, f, 0:SEQ], 0.0, ALU.mult, ALU.add)
                        ins_ = v.tensor_tensor_scan(TI[:, f, SEQ + 3:T + 3], LA[:, f, SEQ + 3:T + 3], LU[:, f, SEQ + 3:T + 3],
                                                    PT[:, bass.ds(i * 2 + f, 1), base + R_LRU], ALU.mult, ALU.add)
                    step(ins_)
                    v.tensor_copy(OUTC[:, pair, 3:4], TI[:, :, SEQ - 1:SEQ])
                    v.tensor_copy(OUTC[:, pair, 7:8], TI[:, :, T + 2:T + 3])
                    v.tensor_tensor(G[:, :, 0:SEQ], G[:, :, 0:SEQ], TI[:, :, 0:SEQ], ALU.mult)
                    step(v.tensor_tensor(G[:, :, SEQ:T], G[:, :, SEQ:T], TI[:, :, SEQ + 3:T + 3], ALU.mult))
                    for f in range(2):
                        bank, m = take_acc()
                        scaled(TR[:, f, 0:T], bank, RSTD[:])
                        if f == 0:
                            split_low()
                    dve.wait_ge(s["grec"], t.next("grec").n)
                    v.scalar_tensor_tensor(out=REC[:, pair, :], in0=TR[:, :, 0:T], scalar=1.0, in1=G[:], op0=ALU.add, op1=ALU.mult)
                    for f in range(2):
                        bank, m = take_acc()
                        scaled(TGA[:, bass.ds(i * 2 + f, 1), :], bank, RSTD[:])
                        if f == 0:
                            split_low()
                    t.skip("gatt", 1)

                v.memset(RPT[NEW:P, 4], 0.0)
                w_region_free()
                for n, width in enumerate((UW, UW, LAT - 2 * UW)):
                    for k, pair in enumerate(((0, 1), (2, 3), (4,))):
                        bank, m = take_acc()
                        for h, tt in enumerate(pair):
                            r = rows(tt)
                            ins_ = v.tensor_scalar(Z[0:r, tt, n * UW:n * UW + width], bank[0:r, h, 0:width], rt[0:r, tt:tt + 1], None, ALU.mult)
                        ins_.then_inc(s["acc_free"], 1)
                        if k == 0:
                            split_low()
                step(v.memset(Z[NEW:P, 4, :], 1.0))
                dve.wait_ge(s["acc_free"], m.at(2))
                step(v.tensor_tensor(ZQ[:], Z[:, :, 0:Q_LORA], Z[:, :, 0:Q_LORA], ALU.mult))
                step(v.tensor_reduce(nwt[:, 4, 0:TT], ZQ[:], AX_X, ALU.add))
                step(v.tensor_scalar(nwt[:, 0, 0:TT], nwt[:, 4, 0:TT], 1.0 / Q_LORA, EPS, ALU.mult, ALU.add))
                step(v.tensor_tensor(ZQ[:, :, 0:KV_LORA], Z[:, :, Q_LORA:Q_LORA + KV_LORA], Z[:, :, Q_LORA:Q_LORA + KV_LORA], ALU.mult))
                step(v.tensor_reduce(nwt[:, 4, 0:TT], ZQ[:, :, 0:KV_LORA], AX_X, ALU.add))
                step(v.tensor_scalar(nwt[:, 0, TT:2 * TT], nwt[:, 4, 0:TT], 1.0 / KV_LORA, EPS, ALU.mult, ALU.add))
                rsqrt(2 * TT)
                for tt in range(TT):
                    ins_ = v.tensor_scalar(ZQ[:, tt, :], Z[:, tt, 0:Q_LORA], nwt[:, 2, tt:tt + 1], None, ALU.mult)
                ins_.then_inc(s["zq"], 1)
                dve.wait_ge(s["latents_in"], 48 * (layer + 1))
                zkv = Z[:, :, Q_LORA:Q_LORA + KV_LORA]
                for tt in range(TT):
                    ins_ = v.scalar_tensor_tensor(out=zkv[:, tt, :], in0=zkv[:, tt, :], scalar=nwt[:, 2, TT + tt:TT + tt + 1], in1=GKV[:],
                                                  op0=ALU.mult, op1=ALU.mult)
                ins_.then_inc(s["zkv"], 1)
                kr = Z[:, :, Q_LORA + KV_LORA:LAT]
                half = ROPE // 2
                v.tensor_tensor(KR1[:], kr, RPT[:, :, 0, :], ALU.mult)
                v.tensor_tensor(KR2[:, :, 0:half], kr[:, :, half:ROPE], RPT[:, :, 1, 0:half], ALU.mult)
                step(v.tensor_tensor(KR2[:, :, half:ROPE], kr[:, :, 0:half], RPT[:, :, 1, half:ROPE], ALU.mult))
                v.tensor_tensor(rp[:, 0:TT, :], KR1[:], KR2[:], ALU.add).then_inc(s["rotated"], 1)
                dve.wait_ge(s["rotated"], layer + 1)
                dve.wait_ge(s["past_in"], 32 * (layer + 1))
                v.tensor_tensor(KRS[:], rp[:], rp[:], ALU.mult).then_inc(s["krs"], 1)
                dve.wait_ge(s["krs"], layer + 1)
                step(v.tensor_reduce(krs[:], KRS[:], AX_X, ALU.add))
                q_gain = [PT[:, c, base + R_QLAT:base + R_QLAT + 1] for c in range(3)]
                for c in range(3):
                    turned_acc(lambda b: [(CQL[:, c, 0:SEQ], b[:, 0, :], CQH[:, c, 0:SEQ], q_gain[c]),
                                          (CQL[:, c, SEQ:T], b[:, 1, 0:NEW], CQH[:, c, SEQ:T], q_gain[c])])
                for c in range(2):
                    turned_acc(lambda b: [(CKL[:, c, 0:SEQ], b[:, 0, :], CKH[:, c, 0:SEQ]),
                                          (CKL[:, c, SEQ:T], b[:, 1, 0:NEW], CKH[:, c, SEQ:T])])
                for c in range(2):
                    turned(lambda b: [(CKL[:, c, T:KEYS], b, CKH[:, c, T:KEYS])])
                step(v.tensor_tensor(nwt[:, 4, 0:1], PT[:, 0, base + R_QH:base + R_QH + 1], PT[:, 0, base + R_KH:base + R_KH + 1], ALU.mult))
                dve.wait_ge(s["rope_in"], 16 * (layer + 1))
                step(v.tensor_scalar(RSTD[:], RSTD[:], nwt[:, 4, 0:1], None, ALU.mult))
                v.memset(KA[:], 0.0)
                step(v.memset(KF[:], 0.0))
                dve.wait_ge(s["gatt"], 4 * (layer + 1))
                dve.wait_ge(s["latents_out"], 64 * (layer + 1))

                for i in t.loop(4, **PER["att", "dve"]):
                    for group in range(2):
                        for n, pair in enumerate(((0, 1), (2, 3), (4, 5), (6, 7), (8,))):
                            bank, m = take_acc()
                            dve.wait_ge(s["v_hi"], t.next("v_hi").n)
                            parts = key_parts(pair)
                            for h, w, kt, r in parts:
                                tiles = slice(kt, kt + w)
                                v.tensor_copy(KF[0:r, tiles].rearrange("p t a b -> p t (a b)"), bank[0:r, h:h + w, 0:P])
                                ins_ = v.tensor_tensor(VL[0:r, tiles].rearrange("p t a b -> p t (a b)"), bank[0:r, h:h + w, P:2 * P],
                                                       VH[0:r, tiles].rearrange("p t a b -> p t (a b)").bitcast(F32), ALU.subtract)
                            ins_.then_inc(s["acc_free"], 1)
                            if n == 0:
                                split_low()
                        dve.wait_ge(s["k_sq"], t.next("k_sq").n)
                        step(v.tensor_reduce(nwt[:, 4, 0:2 * KT], KA[:, :, :, 0:NOPE], AX_X, ALU.add))
                        both = nwt[:, 4, 0:2 * KT].rearrange("p (t h) -> p t h", h=2)
                        step(v.tensor_tensor(both, both, krs[:, :].unsqueeze(2).to_broadcast([P, KT, 2]), ALU.add))
                        step(v.tensor_scalar(nwt[:, 0, 0:2 * KT], nwt[:, 4, 0:2 * KT], 1.0 / QK, EPS, ALU.mult, ALU.add))
                        rsqrt(2 * KT)
                        rk = nwt[:, 2, 0:2 * KT].rearrange("p (t h) -> p t h", h=2)
                        for head in range(2):
                            by = rk[:, :, head:head + 1]
                            v.tensor_tensor(KA[:, :, head, 0:NOPE], KF[:, :, head, :], by.to_broadcast([P, KT, NOPE]), ALU.mult)
                            v.tensor_tensor(KA[:, :, head, NOPE:QK], rp[:], by.to_broadcast([P, KT, ROPE]), ALU.mult)
                            v.tensor_tensor(KA[:, :, head, QK:QK + half], rp[:, :, half:ROPE], by.to_broadcast([P, KT, half]), ALU.mult)
                            ins_ = v.tensor_tensor(KA[:, :, head, QK + half:P], rp[:, :, 0:half], by.to_broadcast([P, KT, half]), ALU.mult)
                        ins_.then_inc(s["ka"], 1)
                        for head in range(2):
                            bank, m = take_acc()
                            dve.wait_ge(s["q_sq"], t.next("q_sq").n)
                            scaled(SQ[:], bank, RSTD[:])
                            dve.wait_ge(s["q_hi"], t.next("q_hi").n)
                            v.tensor_tensor(QTL[:], SQ[:], QTH[:].bitcast(F32), ALU.subtract).then_inc(s["q_lo"], 1)
                            turned(lambda b: [(KTL[:, 0:SEQ], b, KTH[:, 0:SEQ])])
                            turned(lambda b: [(KTL[:, SEQ:SEQ + 448], b[:, 0:448], KTH[:, SEQ:SEQ + 448])])
                            turned(lambda b: [(KTL[:, SEQ + 448:KEYS], b[:, 0:P], KTH[:, SEQ + 448:KEYS])])
                            bank, m = take_tp()
                            token_means(bank, m, QK)
                            rsqrt(TT)
                            step(v.tensor_scalar(sm[:, 24:24 + TT], nwt[:, 2, 0:TT], QK ** -0.5, None, ALU.mult))

                            def softmax(tiles, dst, r, done):
                                bank, m = take_acc()
                                for k, (tt, n) in enumerate(tiles):
                                    ins_ = v.reduce_max(sm[0:r, tt:tt + 1], bank[0:r, k, 0:n], AX_X)
                                step(ins_)
                                a, b = tiles[0][0], tiles[-1][0] + 1
                                v.scalar_tensor_tensor(out=sm[0:r, 8 + a:8 + b], in0=sm[0:r, a:b], scalar=-1.0, in1=sm[0:r, 24 + a:24 + b],
                                                       op0=ALU.mult, op1=ALU.mult).then_inc(s["s_max"], 1)

                                def divide():
                                    dve.wait_ge(s["p_exp"], t.next("p_exp").n)
                                    v.reciprocal(sm[0:r, 32 + a:32 + b], sm[0:r, 16 + a:16 + b]).then_inc(s["acc_free"], 1)
                                    dve.wait_ge(s["acc_free"], m.at(2))
                                    for k, (tt, n) in enumerate(tiles):
                                        ins_ = v.tensor_scalar(dst[k][0:r, 0:n], dst[k][0:r, 0:n], sm[0:r, 32 + tt:33 + tt], None, ALU.mult)
                                    ins_.then_inc(s[done], 1)
                                return divide

                            softmax(((0, P), (1, 2 * P)), P1, P, "p1")()
                            divide = softmax(((2, 3 * P), (3, 4 * P)), P1, P, "p1")
                            divide()
                            turned(lambda b: [(PTL[:, 0, 0:P], b[:, 0:P], PTH[:, 0, 0:P]),
                                              (PTL[:, 0:2, P:2 * P], b[:, P:3 * P].rearrange("p (a b) -> p a b", a=2), PTH[:, 0:2, P:2 * P])])
                            bank, m = take_acc()
                            step(v.tensor_reduce(sm[0:NEW, 4:5], halves(bank[0:NEW]), mybir.AxisListType.XY, ALU.max))
                            v.scalar_tensor_tensor(out=sm[0:NEW, 12:13], in0=sm[0:NEW, 4:5], scalar=-1.0, in1=sm[0:NEW, 28:29],
                                                   op0=ALU.mult, op1=ALU.mult).then_inc(s["s_max"], 1)
                            dve.wait_ge(s["p_exp"], t.next("p_exp").n)
                            v.reciprocal(sm[0:NEW, 36:37], sm[0:NEW, 20:21]).then_inc(s["acc_free"], 1)
                            dve.wait_ge(s["acc_free"], m.at(2))
                            v.tensor_scalar(P0[0:NEW], P0[0:NEW], sm[0:NEW, 36:37], None, ALU.mult).then_inc(s["p0"], 1)
                            turned(lambda b: [(PTL[:, 0:3, 2 * P:3 * P], b[:, 0:3 * P].rearrange("p (a b) -> p a b", a=3), PTH[:, 0:3, 2 * P:3 * P])])
                            turned(lambda b: [(PTL[:, 0:4, 3 * P:4 * P], b.rearrange("p (a b) -> p a b", a=4), PTH[:, 0:4, 3 * P:4 * P])])
                            turned(lambda b: [(PSL[0:NEW, 0, :], b[0:NEW, 0:NEW], PSH[0:NEW, 0, :]),
                                              (PSL[:, 1:TT, :], b[:, NEW:TT * NEW].rearrange("p (a b) -> p a b", a=4), PSH[:, 1:TT, :])])
                            bank, m = take_acc()
                            mine = slice(head * 64, head * 64 + 64)
                            v.tensor_copy(AO[mine, 0:SEQ], bank[mine, 0, :])
                            v.tensor_copy(AO[mine, SEQ:T], bank[mine, 1, 0:NEW]).then_inc(s["acc_free"], 1)
                        dve.wait_ge(s["acc_free"], m.at(2))
                        tile = bass.ds(i * 2 + group, 1)
                        ao = AO[:].rearrange("p (a b) -> p a b", a=1)
                        step(v.scalar_tensor_tensor(out=ao, in0=TGA[:, tile, :], scalar=1.0, in1=ao, op0=ALU.add, op1=ALU.mult))
                        v.scalar_tensor_tensor(out=ao, in0=ao, scalar=2.0, in1=REC[:, tile, :], op0=ALU.mult, op1=ALU.add)\
                            .then_inc(s["mix_sum"], 1)
                        dve.wait_ge(s["mix_hi"], t.next("mix_hi").n)
                        v.scalar_tensor_tensor(out=YL[:, tile, :], in0=ao, scalar=0.25, in1=YH[:, tile, :].bitcast(F32),
                                               op0=ALU.mult, op1=ALU.subtract).then_inc(s["mixed"], 1)

                w_region_free()
                output_projection(base + R_NMEM)

                dve.wait_ge(s["mem_in"], 32 * (layer + 1))
                dve.wait_ge(s["mem_sq"], 2 * (layer + 1))
                step(v.tensor_scalar(nwt[:, 0, 0:2], sm[:, 0:2], 1.0 / D, EPS, ALU.mult, ALU.add))
                rsqrt(2)
                for mt in range(2):
                    ins_ = v.tensor_scalar(MEM[:, mt, :], MEM[:, mt, :], nwt[:, 2, mt:mt + 1], None, ALU.mult)
                ins_.then_inc(s["mem_normed"], 1)
                for p4 in range(4):
                    turned(lambda b: [(MTL[:, 2 * p4 + c, :], b[:, c * 2 * P:(c + 1) * 2 * P], MTH[:, 2 * p4 + c, :],
                                       PT[:, 2 * p4 + c, base + R_MEMIN:base + R_MEMIN + 1]) for c in range(2)])
                marker("mc_free").then_inc(s["mc_free"], 1)
                for i in t.loop(2, **PER["mem", "dve"]):
                    for head in range(2):
                        bank, m = take_acc()
                        dve.wait_ge(s["mem_place"], t.next("mem_place").n)
                        v.tensor_copy(MF[:], bank[:, :, 0:MEM_D]).then_inc(s["acc_free"], 1)
                        split_low()
                        dve.wait_ge(s["mk_sq"], t.next("mk_sq").at(1))
                        t.skip("mk_sq", 1)
                        step(v.tensor_scalar(nwt[:, 0, 0:2], sm[:, 0:2], 1.0 / MEM_D, EPS, ALU.mult, ALU.add))
                        rsqrt(2)
                        for mt in range(2):
                            ins_ = v.scalar_tensor_tensor(out=MF[:, mt, :], in0=MF[:, mt, :], scalar=nwt[:, 2, mt:mt + 1], in1=GMK[:],
                                                          op0=ALU.mult, op1=ALU.mult)
                        ins_.then_inc(s["mk"], 1)
                        bank, m = take_acc()
                        v.tensor_copy(MV[:], bank[:, :, 0:MEM_D]).then_inc(s["acc_free"], 1)
                        split_low()
                        dve.wait_ge(s["vm_hi"], t.next("vm_hi").at(1))
                        t.skip("vm_hi", 1)
                        v.tensor_tensor(VML[:, 0], MV[:], VMH[:, 0].bitcast(F32), ALU.subtract).then_inc(s["mv"], 1)
                        v.tensor_tensor(VML[:, 1], MC[:, :, 1, :], VMH[:, 1].bitcast(F32), ALU.subtract)
                        for dc in range(2):
                            bank, m = take_acc()
                            scaled(QF[:, dc, :], bank, RSTD[:])
                            if dc == 0:
                                split_low()
                            dve.wait_ge(s["mq_hi"], t.next("mq_hi").n)
                            v.scalar_tensor_tensor(out=QML[:, dc, :], in0=QF[:, dc, :], scalar=PT[:, dc, base + R_MQ:base + R_MQ + 1],
                                                   in1=QMH[:, dc, :].bitcast(F32), op0=ALU.mult, op1=ALU.subtract)
                        for which in range(2):
                            turned(lambda b: [(KML[:, which].rearrange("p a b -> p (a b)"), b, KMH[:, which].rearrange("p a b -> p (a b)"))])
                        marker("mq_lo").then_inc(s["mq_lo"], 1)
                        bank, m = take_tp()
                        token_means(bank, m, MEM_D)
                        rsqrt(TT)
                        step(v.tensor_scalar(sm[:, 24:24 + TT], nwt[:, 2, 0:TT], MEM_D ** -0.5, None, ALU.mult))
                        bank, m = take_acc()
                        step(v.tensor_reduce(sm[:, 0:4], bank.rearrange("p a (b c) -> p (a b) c", b=2), AX_X, ALU.max))
                        v.scalar_tensor_tensor(out=sm[:, 8:12], in0=sm[:, 0:4], scalar=-1.0, in1=sm[:, 24:28], op0=ALU.mult, op1=ALU.mult)\
                            .then_inc(s["s_max"], 1)
                        dve.wait_ge(s["p_exp"], t.next("p_exp").n)
                        v.reciprocal(sm[:, 32:36], sm[:, 16:20]).then_inc(s["acc_free"], 1)
                        dve.wait_ge(s["acc_free"], m.at(2))
                        v.tensor_tensor(PM[:], PM[:], sm[:, 32:36].unsqueeze(2).to_broadcast([P, 4, N_MEM]), ALU.mult).then_inc(s["pm"], 1)
                        bank, m = take_acc()
                        step(v.reduce_max(sm[0:NEW, 4:5], bank[0:NEW, 0, 0:N_MEM], AX_X))
                        v.scalar_tensor_tensor(out=sm[0:NEW, 12:13], in0=sm[0:NEW, 4:5], scalar=-1.0, in1=sm[0:NEW, 28:29],
                                               op0=ALU.mult, op1=ALU.mult).then_inc(s["s_max"], 1)
                        dve.wait_ge(s["p_exp"], t.next("p_exp").n)
                        v.reciprocal(sm[0:NEW, 36:37], sm[0:NEW, 20:21]).then_inc(s["acc_free"], 1)
                        dve.wait_ge(s["acc_free"], m.at(2))
                        v.tensor_scalar(SQT[0:NEW, 0:N_MEM], SQT[0:NEW, 0:N_MEM], sm[0:NEW, 36:37], None, ALU.mult).then_inc(s["pms"], 1)
                        for mt in range(2):
                            turned(lambda b: [(PML[:, mt, 0:SEQ], b, PMH[:, mt, 0:SEQ])])
                        turned(lambda b: [(PML[:, :, SEQ:T], b[:, 0:2 * NEW].rearrange("p (a b) -> p a b", a=2), PMH[:, :, SEQ:T])])
                        for dc in range(2):
                            row = bass.ds(i * 4 + (2 * head + dc), 1)
                            turned_acc(lambda b: [(YL[:, row, 0:SEQ], b[:, 0:1, :], YH[:, row, 0:SEQ]),
                                                  (YL[:, row, SEQ:T], b[:, 1:2, 0:NEW], YH[:, row, SEQ:T])])
                        marker("mc_free").then_inc(s["mc_free"], 1)
                w_region_free()
                output_projection(base + R_NFFN)

                def hidden_tiles(tiles):
                    for pair in range(tiles // 2):
                        for f in range(2):
                            bank, m = take_acc()
                            scaled(H1[:, f, :], bank, RSTD[:])
                            if f == 0:
                                split_low()
                        dve.wait_ge(s["f_th"], t.next("f_th").n)
                        step(v.scalar_tensor_tensor(out=H1[:], in0=TH[:], scalar=1.0, in1=H1[:], op0=ALU.add, op1=ALU.mult))
                        for f in range(2):
                            bank, m = take_acc()
                            scaled(TH[:, f, :], bank, GR[:])
                            if f == 0:
                                split_low()
                        dve.wait_ge(s["acc_free"], m.at(2))
                        v.tensor_tensor(H1[:], H1[:], TH[:], ALU.mult).then_inc(s["f_hid"], 1)
                        dve.wait_ge(s["f_hi"], t.next("f_hi").n)
                        v.tensor_tensor(YL[:, 2 * pair:2 * pair + 2, :], H1[:], YH[:, 2 * pair:2 * pair + 2, :].bitcast(F32), ALU.subtract)\
                            .then_inc(s["hidden"], 1)
                        dve.wait_ge(s["hidden"], t.next("hidden").n)

                def add_tiles(row=None):
                    for k in range(C):
                        bank, m = take_acc()
                        add_residual(bank, m, k)
                        if k % 2 == 0:
                            split_low()
                        if row is not None:
                            dve.wait_ge(s["acc_free"], m.at(2))
                            prepare(k, row)
                    return m

                if layer == 0:
                    step(v.tensor_scalar(GR[:], RSTD[:], 0.5, None, ALU.mult))
                    for i in t.loop(2, **PER["dense", "dve"]):
                        hidden_tiles(8)
                        add_tiles()
                    step(v.memset(SQ[:], 0.0))
                    hidden_tiles(6)
                    add_tiles(ROWS + R_MIX)
                else:
                    dve.wait_ge(s["router_in"], 48)
                    step(v.memset(LG[:], 0.0))
                    dve.wait_ge(s["router_hi"], 1)
                    v.tensor_tensor(RWL[:], RW[:], RWH[:].bitcast(F32), ALU.subtract).then_inc(s["router"], 1)
                    bank, m = take_tp()
                    for tt in range(TT):
                        r = rows(tt)
                        ins_ = v.scalar_tensor_tensor(out=LG[0:r, 0, tt, :], in0=bank[0:r, tt * EXPERTS:(tt + 1) * EXPERTS],
                                                      scalar=rt[0:r, tt:tt + 1], in1=RB[0:r, :], op0=ALU.mult, op1=ALU.add)
                    ins_.then_inc(s["tp_free"], 1)
                    dve.wait_ge(s["tp_free"], m.at(4))
                    col = lambda k: nwt[:, k, 0:TT].unsqueeze(2).to_broadcast([P, TT, EXPERTS])
                    step(v.tensor_reduce(nwt[:, 0, 0:TT], LG[:, 0], AX_X, ALU.max))
                    v.tensor_tensor(LG[:, 1], LG[:, 0], col(0), ALU.subtract).then_inc(s["lg_shift"], 1)
                    dve.wait_ge(s["lg_exp"], 1)
                    step(v.tensor_reduce(nwt[:, 0, 0:TT], LG[:, 1], AX_X, ALU.add))
                    step(v.reciprocal(nwt[:, 1, 0:TT], nwt[:, 0, 0:TT]))
                    step(v.tensor_tensor(LG[:, 1], LG[:, 1], col(1), ALU.mult))
                    for tt in range(TT):
                        step(v.max(LG[:, 2, tt, :], LG[:, 1, tt, :]))
                        step(v.max_index(LI[:, tt, :], LG[:, 2, tt, :], LG[:, 1, tt, :]))
                    step(v.tensor_copy(LG[:, 3], LI[:]))
                    iota = IOT[:, :].unsqueeze(1).to_broadcast([P, TT, EXPERTS])
                    first, second = (LG[:, 3, :, k:k + 1].to_broadcast([P, TT, EXPERTS]) for k in range(2))
                    v.tensor_tensor(LG[:, 4], iota, first, ALU.is_equal)
                    step(v.tensor_tensor(LG[:, 5], iota, second, ALU.is_equal))
                    step(v.tensor_tensor(LG[:, 4], LG[:, 4], LG[:, 5], ALU.add))
                    step(v.tensor_tensor(LG[:, 4], LG[:, 4], LG[:, 1], ALU.mult))
                    step(v.tensor_reduce(nwt[:, 0, 0:TT], LG[:, 4], AX_X, ALU.add))
                    step(v.reciprocal(nwt[:, 1, 0:TT], nwt[:, 0, 0:TT]))
                    v.tensor_tensor(LG[:, 7], LG[:, 4], col(1), ALU.mult).then_inc(s["gates"], 1)
                    bank, m = take_acc()
                    v.tensor_copy(GT[:, 0:SEQ], bank[0:EXPERTS, 0, :])
                    v.tensor_copy(GT[:, SEQ:T], bank[0:EXPERTS, 1, 0:NEW]).then_inc(s["acc_free"], 1)
                    dve.wait_ge(s["acc_free"], m.at(2))
                    for i in t.loop(EXPERTS, **PER["moe", "dve"]):
                        v.tensor_scalar(GM[:], GT[:], ident[0:EXPERTS, bass.ds(i, 1)], None, ALU.mult).then_inc(s["gate_row"], 1)
                        for k in range(4):
                            bank, m = take_tp()
                            cols = slice(k * (T // 4), (k + 1) * (T // 4))
                            v.scalar_tensor_tensor(out=GR[:, cols], in0=bank[:, 0:T // 4], scalar=0.5, in1=RSTD[:, cols],
                                                   op0=ALU.mult, op1=ALU.mult).then_inc(s["tp_free"], 1)
                        dve.wait_ge(s["tp_free"], m.at(4))
                        hidden_tiles(8)
                        m = add_tiles()
                    dve.wait_ge(s["acc_free"], t.last("acc", 2))
                    marker("y_done").then_inc(s["y_done"], 1)
                marker("outc").then_inc(s["outc"], 1)
                bank, m = take_acc()
                v.tensor_copy(YO[0:8, 0, 0:512], bank[0:8, 0, :])
                v.tensor_copy(YO[0:8, 0, 512:D], bank[0:8, 1, :]).then_inc(s["acc_free"], 1)
                dve.wait_ge(s["acc_free"], m.at(2))
                marker("state_rows").then_inc(s["state_rows"], 1)

            dve.wait_ge(s["state_out"], 64 * DEPTH)
            for tt in range(TT):
                bank, m = take_acc()
                if tt >= 2:
                    dve.wait_ge(s["y_out%d" % (tt % 2)], 16 * (tt // 2))
                r = rows(tt)
                v.tensor_copy(YO[0:r, tt % 2, 0:512], bank[0:r, 0, :])
                v.tensor_copy(YO[0:r, tt % 2, 512:D], bank[0:r, 1, :]).then_inc(s["acc_free"], 1)
                dve.wait_ge(s["acc_free"], m.at(2))
                marker("y_rows").then_inc(s["y_rows"], 1)

        @block.gpsimd
        def _(pool):
            t = Tally(pool)
            load = pool.dma_start
            for name, n in (("acc_free", 2), ("tp_free", 4), ("w_lo", 2), ("mem_place", 1)):
                pool.sem_inc(s[name], n)
            nc.gpsimd.memset(ident[:], 0.0).then_inc(s["consts"], 1)
            nc.gpsimd.memset(PST[:], 0.0).then_inc(s["pst"], 1)
            nc.gpsimd.memset(MK[:, P:P + NEW].bitcast(F32), 0.0)
            nc.gpsimd.memset(ones[:], 1.0).then_inc(s["consts"], 1)
            pool.wait_ge(s["consts"], 2)
            nc.gpsimd.affine_select(out=ident[:], in_=ident[:], compare_op=ALU.not_equal, fill=1.0, base=0, pattern=[[-1, P]],
                                    channel_multiplier=1).then_inc(s["consts"], 1)
            nc.gpsimd.memset(MK[:, 0:NEW].bitcast(F32), 1.0)
            nc.gpsimd.memset(MK[:, NEW:P].bitcast(F32), 0.0)
            nc.gpsimd.memset(MK[:, P + NEW:2 * P].bitcast(F32), MASKED).then_inc(s["consts"], 1)
            pool.wait_ge(s["pst"], 1)
            n = 0
            for layer in range(DEPTH):
                r = layer * ROWS
                row = lambda ap: ap.rearrange("(o n) -> o n", o=1)
                for at0, count, width, src in (
                        (R_MIX, 1, D, row(ins["norm_mix"][layer])), (R_CW, 4, D, ins["conv_w"][layer]), (R_CB, 1, D, row(ins["conv_b"][layer])),
                        (R_BA, 1, D, row(ins["lru_ba"][layer])), (R_BI, 1, D, row(ins["lru_bi"][layer])),
                        (R_LAM, 1, D, row(ins["lru_lambda"][layer])), (R_NMEM, 1, D, row(ins["norm_mem"][layer])),
                        (R_NFFN, 1, D, row(ins["norm_ffn"][layer])), (R_CONV, 3, D, ins["state_conv"][layer, 0]),
                        (R_LRU, 1, D, ins["state_lru"][layer]), (R_MEMIN, 1, D, row(ins["mem_in_norm"][layer])),
                        (R_QLAT, 1, Q_LORA, row(ins["q_lat_norm"][layer])), (R_MQ, 1, MEM_D, row(ins["mq_head_norm"][layer])),
                        (R_QH, 1, QK, row(ins["q_head_norm"][layer])), (R_KH, 1, QK, row(ins["k_head_norm"][layer]))):
                    load(PST[r + at0:r + at0 + count, 0:width], src).then_inc(s["params_in"], 16)
                    n += 1
                for at0, name in ((R_QH, "q_head_norm"), (R_KH, "k_head_norm")):
                    g = row(ins[name][layer])
                    load(PST[r + at0:r + at0 + 1, 96:112], g[:, 80:96]).then_inc(s["params_in"], 16)
                    load(PST[r + at0:r + at0 + 1, 112:128], g[:, 64:80]).then_inc(s["params_in"], 16)
                    n += 2
            assert n == PARAM_DMAS
            load(TOK[:, 0:4, :], ins["x_prompt"][0].rearrange("(t p) d -> p t d", p=P)).then_inc(s["tokens_in"], 16)
            load(TOK[0:NEW, 4, :], ins["x_sample"][0]).then_inc(s["tokens_in"], 16)
            for layer in range(DEPTH):
                pool.wait_ge(s["w_free"], 4 * layer + 1)
                if layer:
                    pool.wait_ge(s["state_out"], 64 * layer)
                nc.gpsimd.memset(BD[:], 0.0).then_inc(s["bd_zero"], 1)
                pool.wait_ge(s["bd_zero"], layer + 1)
                for gate, name in enumerate(("lru_wa", "lru_wi")):
                    w = ins[name][layer].rearrange("(c two) i j -> two i c j", two=2)
                    for half in range(2):
                        load(BD[half * 64:half * 64 + 64, gate, :, half * 64:half * 64 + 64], w[half]).then_inc(s["blocks_in"], 16)
                pool.wait_ge(s["w_free"], 4 * layer + 2)
                load(CKP[:], ins["cache_ckv"][layer, 0].rearrange("(t p) d -> p t d", p=P)).then_inc(s["past_in"], 16)
                load(rp[:, TT:KT, :], ins["cache_krope"][layer, 0].rearrange("(t p) d -> p t d", p=P)).then_inc(s["past_in"], 16)
                load(RPT[:, 0:4], ins["rope_tok"][0:SEQ].rearrange("(t p) a d -> p t a d", p=P)).then_inc(s["latents_in"], 16)
                load(RPT[0:NEW, 4], ins["rope_tok"][SEQ:T]).then_inc(s["latents_in"], 16)
                load(GKV[:], ins["kv_lat_norm"][layer].partition_broadcast(P)).then_inc(s["latents_in"], 16)
                load(RSTD[:], ins["rope_rows"]).then_inc(s["rope_in"], 16)
                pool.wait_ge(s["zkv"], layer + 1)
                kv = slice(Q_LORA, Q_LORA + KV_LORA)
                load(outs["new_ckv_p"][layer, 0].rearrange("(t p) d -> p t d", p=P), Z[:, 0:4, kv]).then_inc(s["latents_out"], 16)
                load(outs["new_ckv_s"][layer, 0], Z[0:NEW, 4, kv]).then_inc(s["latents_out"], 16)
                pool.wait_ge(s["rotated"], layer + 1)
                load(outs["new_krope_p"][layer, 0].rearrange("(t p) d -> p t d", p=P), rp[:, 0:4, :]).then_inc(s["latents_out"], 16)
                load(outs["new_krope_s"][layer, 0], rp[0:NEW, 4, :]).then_inc(s["latents_out"], 16)
                pool.wait_ge(s["w_free"], 4 * layer + 3)
                load(MEM[:], ins["mem_prompt"][0].rearrange("(t p) d -> p t d", p=P)).then_inc(s["mem_in"], 16)
                load(GMK[:], ins["mk_head_norm"][layer].partition_broadcast(P)).then_inc(s["mem_in"], 16)
                for head in range(MEM_HEADS):
                    n = layer * MEM_HEADS + head
                    pool.wait_ge(s["mc_free"], 5 * layer + head + 1)
                    load(MC[:, :, 0, :], ins["cache_mem_k"][layer, 0, :, head, :].rearrange("(t p) d -> p t d", p=P)).then_inc(s["mc_in"], 16)
                    load(MC[:, :, 1, :], ins["cache_mem_v"][layer, 0, :, head, :].rearrange("(t p) d -> p t d", p=P)).then_inc(s["mc_in"], 16)
                    pool.wait_ge(s["mv"], n + 1)
                    load(outs["new_mem_k_p"][layer, 0, :, head, :].rearrange("(t p) d -> p t d", p=P), MF[:]).then_inc(s["mem_out"], 16)
                    load(outs["new_mem_v_p"][layer, 0, :, head, :].rearrange("(t p) d -> p t d", p=P), MV[:]).then_inc(s["mem_out"], 16)
                    pool.wait_ge(s["mem_out"], 32 * (n + 1))
                    pool.sem_inc(s["mem_place"], 1)
                pool.wait_ge(s["w_free"], 4 * layer + 4)
                if layer == 1:
                    load(RW[:], ins["moe_router"][0].rearrange("(c p) e -> p c e", p=P)).then_inc(s["router_in"], 16)
                    load(RB[:], ins["moe_router_b"][0].partition_broadcast(P)).then_inc(s["router_in"], 16)
                    load(IOT[:], ins["expert_numbers"]).then_inc(s["router_in"], 16)
                pool.wait_ge(s["state_rows"], layer + 1)
                load(outs["new_conv_p"][layer, 0], YO[0:3, 0, :]).then_inc(s["state_out"], 16)
                load(outs["new_lru_p"][layer], YO[3:4, 0, :]).then_inc(s["state_out"], 16)
                load(outs["new_conv_s"][layer, 0], YO[4:7, 0, :]).then_inc(s["state_out"], 16)
                load(outs["new_lru_s"][layer], YO[7:8, 0, :]).then_inc(s["state_out"], 16)
            pool.wait_ge(s["latents_out"], 64 * DEPTH)
            pool.wait_ge(s["mem_out"], 32 * MEM_HEADS * DEPTH)
            pool.wait_ge(s["state_out"], 64 * DEPTH)

        @block.sync
        def _(sp):
            t = Tally(sp)

            def unit(*pieces):
                m = t.next("unit")
                k = m.slot(2)
                sp.wait_ge(s["w_lo"], m.n)
                for dst, src in pieces:
                    sp.dma_start(dst(RAW[:, k]), src).then_inc(s["landed%d" % k], LANDED // len(pieces))

            def rows_of(w, tiles=C):
                return w.rearrange("(c p) n -> p c n", p=P)

            def columns(w, at0, n=UW, tiles=C):
                cols = slice(at0, at0 + n) if isinstance(at0, int) else bass.ds(at0, n)
                unit((lambda raw: unit3(raw)[:, 0:tiles, 0:n], rows_of(w)[:, :, cols]))

            GREC = 2 * D + LAT
            for layer in range(DEPTH):
                w_in = ins["w_in"][layer]
                for i in t.loop(4, unit=4):
                    for at0 in (0, D, GREC, GREC + D):
                        columns(w_in, i * UW + at0)
                for k, n in enumerate((UW, UW, LAT - 2 * UW)):
                    columns(w_in, 2 * D + k * UW, n)
                for i in t.loop(4, unit=2):
                    for group in range(2):
                        uq = ins["w_uq"][layer].rearrange("(c p) (h n) -> p c h n", p=P, n=QK)
                        q = lambda raw: raw[:, 0:768].rearrange("p (c h n) -> p c h n", c=3, h=2)
                        kv = lambda raw: raw[:, 768:1280].rearrange("p (c n) -> p c n", c=2)
                        m = t.next("unit")
                        k = m.slot(2)
                        sp.wait_ge(s["w_lo"], m.n)
                        heads = [bass.ds(i * 4 + group * 2 + h, 1) for h in range(2)]
                        for h in range(2):
                            sp.dma_start(q(RAW[:, k])[:, :, h:h + 1, 0:QK], uq[:, :, heads[h], :]).then_inc(s["landed%d" % k], 16)
                        for h in range(2):
                            sp.dma_start(q(RAW[:, k])[:, :, h:h + 1, QK:P], uq[:, :, heads[h], NOPE:QK]).then_inc(s["landed%d" % k], 16)
                        for j, name in enumerate(("w_uk", "w_uv")):
                            sp.dma_start(kv(RAW[:, k])[:, :, j * P:(j + 1) * P],
                                         rows_of(ins[name][layer])[:, :, bass.ds(i * 256 + group * P, P)]).then_inc(s["landed%d" % k], 16)
                for name in ("w_out",):
                    for i in t.loop(2, unit=2):
                        for u in range(2):
                            columns(ins[name][layer], i * 512 + u * UW)
                for i in t.loop(2, unit=6):
                    for head in range(2):
                        for name in ("w_mk", "w_mv", "w_mq"):
                            columns(ins[name][layer], i * 512 + head * UW)
                for i in t.loop(2, unit=2):
                    for u in range(2):
                        columns(ins["w_mo"][layer], i * 512 + u * UW)

                def ffn(w1, w3, w2, at0, tiles):
                    for pair in range(tiles // 2):
                        columns(w1, at0 + pair * UW)
                        columns(w3, at0 + pair * UW)
                    for k in range(4):
                        columns(w2, k * UW, tiles=tiles)

                if layer == 0:
                    w1, w3, w2 = (ins[n][0] for n in ("ffn_w1", "ffn_w3", "ffn_w2"))
                    for i in t.loop(2, unit=12):
                        ffn(w1, w3, w2[bass.ds(i * 1024, 1024), :], i * 1024, 8)
                    ffn(w1, w3, w2[2048:D_FF, :], 2048, 6)
                else:
                    for i in t.loop(EXPERTS, unit=12):
                        w1, w3, w2 = (ins[n][0, bass.ds(i, 1)].rearrange("o a b -> (o a) b") for n in ("moe_w1", "moe_w3", "moe_w2"))
                        ffn(w1, w3, w2, 0, 8)
            m = t.next("unit")
            sp.wait_ge(s["w_lo"], m.n)
            sp.sem_inc(s["landed%d" % m.slot(2)], LANDED)
            for tt in range(TT):
                sp.wait_ge(s["y_rows"], tt + 1)
                dst = outs["y_prompt"][0, tt * P:(tt + 1) * P, :] if tt < 4 else outs["y_sample"][0]
                sp.dma_start(dst, YO[0:rows(tt), tt % 2, :]).then_inc(s["y_out%d" % (tt % 2)], 16)
            sp.wait_ge(s["y_out0"], 48)
            sp.wait_ge(s["y_out1"], 32)


_INS = ['x_prompt', 'x_sample', 'cache_ckv', 'cache_krope', 'cache_mem_k', 'cache_mem_v', 'state_lru', 'state_conv',
        'mem_prompt', 'norm_mix', 'w_in', 'conv_w', 'conv_b', 'lru_wa', 'lru_ba', 'lru_wi', 'lru_bi', 'lru_lambda',
        'q_lat_norm', 'w_uq', 'kv_lat_norm', 'w_uk', 'w_uv', 'q_head_norm', 'k_head_norm', 'w_out',
        'norm_mem', 'mem_in_norm', 'w_mq', 'w_mk', 'w_mv', 'w_mo', 'mq_head_norm', 'mk_head_norm',
        'norm_ffn', 'ffn_w1', 'ffn_w3', 'ffn_w2', 'moe_router', 'moe_router_b', 'moe_w1', 'moe_w3', 'moe_w2']
_OUTS = [('y_prompt', (1, 512, 1024)), ('y_sample', (1, 64, 1024)), ('new_ckv_p', (2, 1, 512, 256)),
         ('new_krope_p', (2, 1, 512, 32)), ('new_lru_p', (2, 1, 1024)), ('new_conv_p', (2, 1, 3, 1024)),
         ('new_mem_k_p', (2, 1, 256, 4, 256)), ('new_mem_v_p', (2, 1, 256, 4, 256)),
         ('new_ckv_s', (2, 1, 64, 256)), ('new_krope_s', (2, 1, 64, 32)), ('new_lru_s', (2, 1, 1024)),
         ('new_conv_s', (2, 1, 3, 1024))]


def rope_tables():
    import numpy as _np
    half = 16
    inv_freq = (_np.float32(10000.0) ** (-_np.arange(half, dtype=_np.float32) / _np.float32(half))).astype(_np.float32)
    ang = _np.arange(576, dtype=_np.float32)[None, :] * inv_freq[:, None]
    cos, sin = _np.cos(ang), _np.sin(ang)
    tok = _np.stack([_np.concatenate([cos, cos]), _np.concatenate([-sin, sin])]).transpose(2, 0, 1)
    rows = _np.concatenate([_np.ones((64, 576)), cos, cos, sin, -sin])
    return _np.ascontiguousarray(tok, _np.float32), _np.ascontiguousarray(rows, _np.float32)


def kernel(**inputs):
    import numpy as _np
    import concourse.bacc as _bacc
    from concourse import mybir as _mybir
    from concourse.bass_utils import run_bass_kernel_spmd as _run

    nc = _bacc.Bacc("TRN2", target_bir_lowering=False, num_devices=1)
    arrays, ins, outs = {}, {}, {}
    tensors = {name: inputs[name] for name in _INS}
    tensors['rope_tok'], tensors['rope_rows'] = rope_tables()
    tensors['expert_numbers'] = _np.tile(_np.arange(8, dtype=_np.float32), (128, 1))
    for name, a in tensors.items():
        a = _np.ascontiguousarray(a)
        arrays[f"in_{name}_dram"] = a
        ins[name] = nc.dram_tensor(f"in_{name}_dram", a.shape, _mybir.dt.from_np(a.dtype), kind="ExternalInput").ap()
    for name, shape in _OUTS:
        outs[name] = nc.dram_tensor(f"out_{name}_dram", shape, _mybir.dt.float32, kind="ExternalOutput").ap()
    stream_step_kernel(nc, ins, outs)
    r = _run(nc, [arrays], core_ids=[0])
    return tuple(r.results[0][f"out_{name}_dram"] for name, _ in _OUTS)
```

```python
from contextlib import ExitStack

import concourse.bass as bass
from concourse import mybir

F32 = mybir.dt.float32
F32R = mybir.dt.float32r
I32 = mybir.dt.int32
U32 = mybir.dt.uint32
ALU = mybir.AluOpType
ACT = mybir.ActivationFunctionType
AX_X = mybir.AxisListType.X

P = 128
D = 1024
C = D // P
SEQ, NEW, PAST = 512, 64, 512
T = SEQ + NEW
HALF = T // 2
TT = 5
KT = 9
KEYS = SEQ + NEW + PAST
DEPTH = 2
N_HEADS, NOPE, ROPE, QK = 16, 64, 32, 96
Q_LORA, KV_LORA = 384, 256
LAT = Q_LORA + KV_LORA + ROPE
N_MEM, MEM_HEADS, MEM_D = 256, 4, 256
D_FF, EXPERTS, EXPERT_FF = 2816, 8, 1024
EPS = 1e-6
UW = 256
UNIT = C * UW
UA = (3 + 2) * UW
CONV = 580
LANDED = 96
PARAM_DMAS = DEPTH * 19
MASKED = -1e30
GELU_C = 0.7978845608028654

(R_MIX, R_CW, R_CB, R_BA, R_BI, R_LAM, R_NMEM, R_NFFN, R_CONV, R_LRU, R_MEMIN, R_QLAT, R_MQ, R_QH, R_KH) = (
    0, 1, 5, 6, 7, 8, 9, 10, 11, 14, 15, 16, 17, 18, 19)
ROWS = 20


class Tally:

    def __init__(self, engine):
        self.engine, self.base, self.cur, self.per, self.i = engine, {}, {}, {}, None

    def loop(self, turns, **per):
        assert self.i is None and not any(self.cur.values())
        self.per = per
        with self.engine.Fori(0, turns) as i:
            self.i = i
            yield i
        for name in set(per) | set(self.cur):
            assert self.cur.get(name, 0) == per.get(name, 0), (name, "per turn", self.cur.get(name, 0))
            self.base[name] = self.base.get(name, 0) + turns * per[name]
        self.cur, self.i = {}, None

    def next(self, name):
        if self.i is None:
            self.base[name] = self.base.get(name, 0) + 1
            return Mark(self.base[name], self.base[name], None, 0)
        self.cur[name] = self.cur.get(name, 0) + 1
        k = self.base.get(name, 0) + self.cur[name]
        return Mark(k, k, self.i, self.per.get(name, 0))

    def last(self, name, plus=0):
        v = self.base.get(name, 0) + self.cur.get(name, 0) + plus
        return v if self.i is None else self.i * self.per.get(name, 0) + v

    def skip(self, name, n):
        for _ in range(n):
            self.next(name)


class Mark:
    def __init__(self, n, k, i, per):
        self.k, self.i, self.per = k, i, per

    def at(self, plus=0, each=1):
        v = (self.k + plus) * each
        return v if self.i is None else self.i * (self.per * each) + v

    @property
    def n(self):
        return self.at()

    def slot(self, ring):
        assert self.i is None or self.per % ring == 0, (self.per, ring)
        return (self.k - 1) % ring

    def use(self, ring, each):
        v = ((self.k - 1) // ring + 1) * each
        return v if self.i is None else self.i * (self.per // ring * each) + v


PER = {
    ('mix', 'pe'): dict(unit=4, acc=8, xc_lo=1, tp=8),
    ('att', 'pe'): dict(q_lo=4, acc=18, v_lo=2, tp=40, p01=4, q_sq=4, p23=4, ka=2, unit=2),
    ('out', 'pe'): dict(unit=2, acc=4),
    ('mem', 'pe'): dict(unit=6, acc=16, mk=2, mc_in=2, tp=12, mq_sq=4, mq_lo=2, pm=2, pms=2),
    ('dense', 'pe'): dict(unit=12, acc=24, hidden=4),
    ('moe', 'pe'): dict(gate_row=1, tp=4, unit=12, acc=24, hidden=4),
    ('mix', 'act'): dict(acc=8, unit=4, xc=1, g_z=1, tp=8, g_gelu=1, lru_w=1),
    ('att', 'act'): dict(acc=18, s_max=8, tp=40, unit=2, mix_sum=2, v_lo=2),
    ('out', 'act'): dict(acc=4, unit=2),
    ('mem', 'act'): dict(unit=6, acc=16, mc_in=2, tp=12, s_max=4, mem_place=2),
    ('dense', 'act'): dict(acc=24, unit=12, f_hid=4),
    ('moe', 'act'): dict(tp=4, acc=24, unit=12, f_hid=4),
    ('mix', 'dve'): dict(acc=8, dve_step=14, unit=4, bd_hi=1, xc_hi=1, g_sq=1, g_th=1, gatt=1, tp=8, lru_t=2, lru_a=2, lru_sqrt=1, grec=1),
    ('att', 'dve'): dict(acc=18, dve_step=84, p_exp=8, tp=40, k_sum=2, q_sq=4, q_hi=4, tp_hi=28, unit=2, mix_hi=2),
    ('out', 'dve'): dict(acc=4, unit=2, x_hi=4, x_sq=4, sq_sum=4),
    ('mem', 'dve'): dict(unit=6, acc=16, mem_place=2, mk_sq=4, dve_step=48, vm_hi=4, mq_hi=4, tp=12, tp_hi=10, p_exp=4, acc_hi=4),
    ('dense', 'dve'): dict(acc=24, unit=12, f_th=4, dve_step=4, f_hi=4, hidden=4),
    ('moe', 'dve'): dict(tp=4, acc=24, unit=12, f_th=4, dve_step=4, f_hi=4, hidden=4),
}


def unit3(ap):
    return ap.rearrange("p (c n) -> p c n", n=UW)


def stream_step_kernel(nc, ins, outs):
    ctx = ExitStack()
    with ctx:
        top = [(nc.sbuf_base + 31) // 32 * 32]

        def at(name, shape, dt, offset):
            return nc.alloc_sbuf_tensor_at(name, shape, dt, offset=offset)

        def nbytes(shape):
            n = 4
            for k in shape[1:]:
                n *= k
            return (n + 31) // 32 * 32

        def fixed(name, shape, dt=F32):
            t = at(name, shape, dt, top[0])
            top[0] += nbytes(shape)
            return t

        X = fixed("X", [P, C, T])
        RAW = fixed("RAW", [P, 2, UNIT])
        WH = fixed("WH", [P, 2, UNIT], F32R)
        WL = fixed("WL", [P, 2, UNIT], F32R)
        VF = lambda kt, n, r=P: RAW[0:r, kt // 6, UA + kt % 6 * P:UA + (kt % 6 + n) * P]
        PT = fixed("PT", [P, C, DEPTH * ROWS])
        ident = fixed("ident", [P, P])
        ones = fixed("ones", [P, P])
        MK = fixed("MK", [1, 2 * P], F32R)
        SQ = fixed("SQ", [P, T])
        SQT = fixed("SQT", [P, T])
        RSTD = fixed("RSTD", [P, T])
        rt = fixed("rt", [P, 8])
        nwt = fixed("nwt", [P, 6, 24])
        RK = fixed("RK", [P, 3, 24])
        sm = fixed("sm", [P, 64])
        LAM = fixed("LAM", [P, C, 8])
        HB = fixed("HB", [P, C, 2])
        HBT = fixed("HBT", [P, 2, 2])
        OUTC = fixed("OUTC", [P, C, 8])
        rp = fixed("rp", [P, KT, ROPE])
        krs = fixed("krs", [P, KT])
        OPERAND = nbytes([P, C, T])
        A0 = top[0]
        B0 = A0 + 2 * OPERAND
        W0 = B0 + 2 * OPERAND
        END = nc.sbuf_usable_end
        ends = {}

        def region(start, end=END):
            o = [start]

            def put(name, shape, dt=F32):
                t = at(name, shape, dt, o[0])
                o[0] += nbytes(shape)
                assert o[0] <= end, (name, o[0], end)
                ends[name] = o[0]
                return t
            return put

        put = region(A0, B0)
        XH, XL = put("XH", [P, C, T], F32R), put("XL", [P, C, T], F32R)
        put = region(B0, W0)
        YH, YL = put("YH", [P, C, T], F32R), put("YL", [P, C, T], F32R)
        put = region(B0, W0)
        REC, TGA = put("REC", [P, C, T]), put("TGA", [P, C, T])
        put = region(B0, W0)
        TOK = put("TOK", [P, TT, D])
        put = region(W0)
        PST = put("PST", [DEPTH * ROWS, D])
        put = region(W0)
        XP = put("XP", [P, 2, CONV + 4])
        XC = put("XC", [P, 2, CONV])
        XCH, XCL = put("XCH", [P, 2, CONV], F32R), put("XCL", [P, 2, CONV], F32R)
        TR = put("TR", [P, 2, CONV])
        TI = put("TI", [P, 2, CONV])
        LA = put("LA", [P, 2, CONV])
        LU = put("LU", [P, 2, CONV])
        G = put("G", [P, 2, T])
        BD = put("BD", [P, 2, C, P])
        BDH, BDL = put("BDH", [P, 2, 2, P], F32R), put("BDL", [P, 2, 2, P], F32R)
        put = region(W0)
        CQH, CQL = put("CQH", [P, 3, T], F32R), put("CQL", [P, 3, T], F32R)
        CKH, CKL = put("CKH", [P, 2, KEYS], F32R), put("CKL", [P, 2, KEYS], F32R)
        rest = ends["CKL"]
        Z = put("Z", [P, TT, LAT])
        CKP = put("CKP", [P, 4, KV_LORA])
        RPT = put("RPT", [P, TT, 2, ROPE])
        GKV = put("GKV", [P, KV_LORA])
        put = region(A0, B0)
        ZQ = put("ZQ", [P, TT, Q_LORA])
        KR1, KR2 = put("KR1", [P, TT, ROPE]), put("KR2", [P, TT, ROPE])
        KRS = put("KRS", [P, KT, ROPE])
        put = region(rest)
        QTH, QTL = put("QTH", [P, T], F32R), put("QTL", [P, T], F32R)
        PTH, PTL = put("PTH", [P, 13, P], F32R), put("PTL", [P, 13, P], F32R)
        PSH, PSL = put("PSH", [P, TT, NEW], F32R), put("PSL", [P, TT, NEW], F32R)
        P23 = put("P2", [P, 3 * P]), put("P3", [P, 4 * P])
        P01 = SQT[:, 0:P], SQT[:, P:3 * P]
        P0 = put("P0", [NEW, T])
        put = region(A0, B0)
        KF = put("KF", [P, KT, 2, 64])
        VH, VL = put("VH", [P, KT, 2, 64], F32R), put("VL", [P, KT, 2, 64], F32R)
        KA = put("KA", [P, KT, 2, P])
        KTH, KTL = put("KTH", [P, KEYS], F32R), put("KTL", [P, KEYS], F32R)
        QSQ = put("QSQ", [P, T])
        AO = put("AO", [P, T])
        put = region(W0)
        MTH, MTL = put("MTH", [P, C, N_MEM], F32R), put("MTL", [P, C, N_MEM], F32R)
        GMK = put("GMK", [P, MEM_D])
        QF = put("QF", [P, 2, T])
        PM = at("PM", [P, 4, N_MEM], F32, ends["GMK"])
        VMH, VML = put("VMH", [P, 2, 2, MEM_D], F32R), put("VML", [P, 2, 2, MEM_D], F32R)
        KMH, KML = put("KMH", [P, 2, 2, N_MEM], F32R), put("KML", [P, 2, 2, N_MEM], F32R)
        QMH, QML = put("QMH", [P, 2, T], F32R), put("QML", [P, 2, T], F32R)
        MEM = at("MEM", [P, 2, D], F32, ends["QML"])
        MC = at("MC", [P, 2, 2, MEM_D], F32, ends["QML"])
        MF = at("MF", [P, 2, MEM_D], F32, ends["QML"] + nbytes([P, 4, MEM_D]))
        MV = at("MV", [P, 2, MEM_D], F32, ends["QML"] + nbytes([P, 6, MEM_D]))
        PMH, PML = put("PMH", [P, 2, T], F32R), put("PML", [P, 2, T], F32R)
        put = region(W0)
        H1 = put("H1", [P, 2, T])
        TH = put("TH", [P, 2, T])
        GR = put("GR", [P, T])
        HF = put("HF", [P, T])
        RW = put("RW", [P, C, EXPERTS])
        RWH, RWL = put("RWH", [P, C, EXPERTS], F32R), put("RWL", [P, C, EXPERTS], F32R)
        RB = put("RB", [P, EXPERTS])
        LG = put("LG", [P, 8, TT, EXPERTS])
        LI = put("LI", [P, TT, EXPERTS], U32)
        IOT = put("IOT", [P, EXPERTS])
        GT = put("GT", [EXPERTS, T])
        GM = put("GM", [EXPERTS, T])
        YO = put("YO", [P, 2, D])

        ACC = ctx.enter_context(nc.psum_tensor("ACC", [P, 2, 2, 512], F32))
        TP = ctx.enter_context(nc.psum_tensor("TP", [P, 4, 512], F32))

        class Semaphores(dict):
            def __missing__(self, name):
                self[name] = ctx.enter_context(nc.semaphore(name))
                return self[name]
        s = Semaphores()

        def halves(bank_pair):
            return bank_pair[:, :, 0:HALF]

        def rows(tt):
            return NEW if tt == 4 else P

        def row_of(tensor, c):
            return tensor[:, c, :] if isinstance(c, int) else tensor[:, bass.ds(c, 1), :].rearrange("p o t -> p (o t)")

        def gain_of(c, row):
            return PT[:, c, row:row + 1] if isinstance(c, int) else PT[:, bass.ds(c, 1), row]

        def key_tiles(tensor, kt, n=4, r=P):
            return tensor[0:r, kt:kt + n].rearrange("p t a b -> p (t a b)")

        def key_col(kt):
            return kt * P if kt < 5 else SEQ + NEW + (kt - 5) * P

        block = ctx.enter_context(nc.Block())

        @block.tensor
        def _(pe):
            t = Tally(pe)

            def product(out, a, b, first=True, last=True):
                nc.tensor.matmul(out, a[0], b[0], start=first, stop=False)
                nc.tensor.matmul(out, a[0], b[1], start=False, stop=False)
                return nc.tensor.matmul(out, a[1], b[0], start=False, stop=last)

            def open_acc():
                m = t.next("acc")
                pe.wait_ge(s["acc_free"], m.n)
                return ACC[:, m.slot(2)]

            def open_tp():
                m = t.next("tp")
                pe.wait_ge(s["tp_free"], m.n)
                return TP[:, m.slot(4)]

            def weights():
                m = t.next("unit")
                pe.wait_ge(s["w_lo"], m.at(2))
                k = m.slot(2)
                return WH[:, k], WL[:, k]

            def features(source, chunks=C):
                wh, wl = (unit3(w) for w in weights())
                for m in range(2):
                    bank = open_acc()
                    for c in range(chunks):
                        for h in range(2):
                            cols = slice(h * HALF, (h + 1) * HALF)
                            mm = product(bank[:, h, 0:HALF], (wh[:, c, m * P:(m + 1) * P], wl[:, c, m * P:(m + 1) * P]),
                                         (source[0][:, c, cols], source[1][:, c, cols]), c == 0, c == chunks - 1)
                    mm.then_inc(s["acc_ready"], 1)

            def norm_statistics():
                t.skip("sq_sum", C - 1)
                pe.wait_ge(s["sq_sum"], t.next("sq_sum").n)
                bank = open_tp()
                for tt in range(TT):
                    mm = nc.tensor.matmul(bank[0:rows(tt), tt:tt + 1], SQ[:, tt * P:tt * P + rows(tt)], ones[:, 0:1],
                                          start=True, stop=True)
                mm.then_inc(s["tp_ready"], 1)
                bank = open_acc()
                pe.wait_ge(s["diag"], t.next("diag").n)
                for tt in range(TT):
                    n = rows(tt)
                    mm = nc.tensor.matmul(bank[:, tt // 4, (tt % 4) * P:(tt % 4) * P + n], ones[0:n, :],
                                          SQT[0:n, tt * P:tt * P + n], start=True, stop=True)
                mm.then_inc(s["acc_ready"], 1)

            pe.wait_ge(s["consts"], 4)
            pe.wait_ge(s["params_in"], PARAM_DMAS * 16)
            bank = open_tp()
            for c in range(C):
                mm = nc.tensor.transpose(bank[:, c * DEPTH * ROWS:(c + 1) * DEPTH * ROWS], PST[:, c * P:(c + 1) * P],
                                         ident[0:DEPTH * ROWS, 0:DEPTH * ROWS])
            mm.then_inc(s["tp_ready"], 1)
            pe.wait_ge(s["tokens_in"], 32)
            for c in range(C):
                bank = open_acc()
                for tt in range(TT):
                    n = rows(tt)
                    mm = nc.tensor.transpose(bank[:, tt // 4, (tt % 4) * P:(tt % 4) * P + n],
                                             TOK[0:n, tt, c * P:(c + 1) * P], ident[0:n, 0:n])
                mm.then_inc(s["acc_ready"], 1)

            for layer in range(DEPTH):
                norm_statistics()
                for i in t.loop(C // 2, **PER["mix", "pe"]):
                    features((XH, XL))
                    features((XH, XL))
                    features((XH, XL))
                    pe.wait_ge(s["xc_lo"], t.next("xc_lo").n)
                    for f in range(2):
                        for gate in range(2):
                            for h in range(2):
                                bank = open_tp()
                                cols = slice(h * (CONV // 2), (h + 1) * (CONV // 2))
                                product(bank[:, 0:CONV // 2], (BDH[:, gate, f, :], BDL[:, gate, f, :]),
                                        (XCH[:, f, cols], XCL[:, f, cols])).then_inc(s["tp_ready"], 1)
                    features((XH, XL))
                for n in (UW, UW, LAT - 2 * UW):
                    wh, wl = (unit3(w) for w in weights())
                    for pair in ((0, 1), (2, 3), (4,)):
                        bank = open_acc()
                        for h, tt in enumerate(pair):
                            cols = slice(tt * P, tt * P + rows(tt))
                            for c in range(C):
                                mm = product(bank[0:rows(tt), h, 0:n], (XH[:, c, cols], XL[:, c, cols]),
                                             (wh[:, c, 0:n], wl[:, c, 0:n]), c == 0, c == C - 1)
                        mm.then_inc(s["acc_ready"], 1)
                pe.wait_ge(s["zq"], t.next("zq").n)
                for c in range(3):
                    bank = open_acc()
                    for tt in range(TT):
                        n = rows(tt)
                        mm = nc.tensor.transpose(bank[:, tt // 4, (tt % 4) * P:(tt % 4) * P + n],
                                                 ZQ[0:n, tt, c * P:(c + 1) * P], ident[0:n, 0:n])
                    mm.then_inc(s["acc_ready"], 1)
                pe.wait_ge(s["zkv"], t.next("zkv").n)
                for c in range(2):
                    bank = open_acc()
                    for tt in range(TT):
                        n = rows(tt)
                        mm = nc.tensor.transpose(bank[:, tt // 4, (tt % 4) * P:(tt % 4) * P + n],
                                                 Z[0:n, tt, Q_LORA + c * P:Q_LORA + (c + 1) * P], ident[0:n, 0:n])
                    mm.then_inc(s["acc_ready"], 1)
                pe.wait_ge(s["past_in"], 32 * (layer + 1))
                for c in range(2):
                    bank = open_tp()
                    for k in range(4):
                        mm = nc.tensor.transpose(bank[:, k * P:(k + 1) * P], CKP[:, k, c * P:(c + 1) * P], ident[:, :])
                    mm.then_inc(s["tp_ready"], 1)

                pe.wait_ge(s["tp_free"], t.last("tp", 4))
                def attention_weights():
                    w = weights()
                    return ([x[:, 0:768].rearrange("p (c h n) -> p c h n", c=3, h=2) for x in w],
                            [x[:, 768:1280].rearrange("p (c n) -> p c n", c=2) for x in w])

                def keys_and_values(wkv):
                    for tiles in ((0, 1, 2, 3), (5, 6, 7, 8), (4,)):
                        bank = open_acc()
                        for k, kt in enumerate(tiles):
                            cols, r = slice(key_col(kt), key_col(kt) + rows(kt)), rows(kt)
                            for c in range(2):
                                mm = product(bank[0:r, k // 2, (k % 2) * UW:(k % 2 + 1) * UW], (CKH[:, c, cols], CKL[:, c, cols]),
                                             (wkv[0][:, c, :], wkv[1][:, c, :]), c == 0, c == 1)
                        mm.then_inc(s["acc_ready"], 1)

                def queries(wq, head):
                    bank = open_acc()
                    for c in range(3):
                        for h in range(2):
                            cols = slice(h * HALF, (h + 1) * HALF)
                            mm = product(bank[:, h, 0:HALF], (wq[0][:, c, head, :], wq[1][:, c, head, :]),
                                         (CQH[:, c, cols], CQL[:, c, cols]), c == 0, c == 2)
                    mm.then_inc(s["acc_ready"], 1)

                def turn_keys(head):
                    if head == 0:
                        pe.wait_ge(s["ka"], t.next("ka").n)
                    for tiles in ((0, 1, 2, 3), (5, 6, 7, 4), (8,)):
                        bank = open_tp()
                        for kt in tiles:
                            at0 = key_col(kt) - key_col(min(tiles))
                            mm = nc.tensor.transpose(bank[:, at0:at0 + rows(kt)], KA[0:rows(kt), kt, head, :],
                                                     ident[0:rows(kt), 0:rows(kt)])
                        mm.then_inc(s["tp_ready"], 1)

                def query_squares():
                    bank = open_tp()
                    pe.wait_ge(s["q_sq"], t.next("q_sq").n)
                    for tt in range(TT):
                        mm = nc.tensor.matmul(bank[0:rows(tt), tt:tt + 1], QSQ[0:QK, tt * P:tt * P + rows(tt)],
                                              ones[0:QK, 0:1], start=True, stop=True)
                    mm.then_inc(s["tp_ready"], 1)

                def prompt_scores(bank, h, tt):
                    cols, n = slice(tt * P, (tt + 1) * P), (tt + 1) * P
                    product(bank[:, h, 0:n], (QTH[:, cols], QTL[:, cols]), (KTH[:, 0:n], KTL[:, 0:n]), True, False)
                    return nc.tensor.matmul(bank[:, h, n - P:n], MK[0:1, 0:P], MK[0:1, P:2 * P], start=False, stop=True)

                def turn_probabilities(blocks):
                    bank = open_tp()
                    for k, src in enumerate(blocks):
                        mm = nc.tensor.transpose(bank[:, k * P:(k + 1) * P], src, ident[:, :])
                    mm.then_inc(s["tp_ready"], 1)

                def weighted_values(head):
                    if head == 0:
                        pe.wait_ge(s["v_lo"], t.next("v_lo").n)
                    bank = open_tp()
                    for j in range(4):
                        mm = product(bank[:, j * P:SEQ], tuple(v[:, j, :, :].rearrange("p a b -> p (a b)") for v in (VH, VL)),
                                     tuple(p[:, 4 * j:3 * j + 4, :].rearrange("p a b -> p (a b)") for p in (PTH, PTL)), j == 0, j == 3)
                    mm.then_inc(s["tp_ready"], 1)
                    bank = open_tp()
                    for k in (1, 2, 3, 4, 0):
                        n = rows(k + 4)
                        mm = product(bank[:, 0:NEW], tuple(v[0:n, k + 4, :, :].rearrange("p a b -> p (a b)") for v in (VH, VL)),
                                     (PSH[0:n, k, :], PSL[0:n, k, :]), k == 1, k == 0)
                    mm.then_inc(s["tp_ready"], 1)

                def attend(head, w, first=False, last=False):
                    following = not (last and head == 1)
                    turned = t.last("tp", 4 if head == 1 else 1)
                    pe.wait_ge(s["q_lo"], t.next("q_lo").n)
                    pe.wait_ge(s["tp_free"], t.last("tp", 4 if head == 0 else -1))
                    bank = open_acc()
                    prompt_scores(bank, 0, 0)
                    prompt_scores(bank, 1, 1)
                    for h, at0, k0, n in ((0, P, SEQ, 3 * P), (1, 2 * P, SEQ + 3 * P, T - 3 * P)):
                        mm = product(bank[0:NEW, h, at0:at0 + n], (QTH[:, SEQ:T], QTL[:, SEQ:T]), (KTH[:, k0:k0 + n], KTL[:, k0:k0 + n]))
                    mm.then_inc(s["acc_ready"], 1)
                    bank = open_acc()
                    prompt_scores(bank, 0, 2)
                    prompt_scores(bank, 1, 3).then_inc(s["acc_ready"], 1)
                    if not first:
                        pe.wait_ge(s["tp_free"], turned)
                        weighted_values(1 - head)
                    if head == 0:
                        turn_keys(1)
                    if following:
                        queries(w[0], 1 - head)
                    pe.wait_ge(s["p01"], t.next("p01").n)
                    turn_probabilities([P01[0], P01[1][:, 0:P], P01[1][:, P:2 * P]])
                    if following:
                        query_squares()
                    bank = open_tp()
                    for k in (1, 2, 3, 4, 0):
                        kt = k + 4
                        a0 = key_col(kt) - SEQ
                        turn = nc.tensor.matmul if k == 1 else nc.tensor.transpose
                        mm = turn(bank[0:rows(kt), k * NEW:(k + 1) * NEW], P0[:, a0:a0 + rows(kt)], ident[0:NEW, 0:NEW])
                    mm.then_inc(s["tp_ready"], 1)
                    if head == 0 and not last:
                        w = attention_weights()
                        keys_and_values(w[1])
                    pe.wait_ge(s["p23"], t.next("p23").n)
                    turn_probabilities([P23[0][:, k * P:(k + 1) * P] for k in range(3)])
                    turn_probabilities([P23[1][:, k * P:(k + 1) * P] for k in range(4)])
                    if head == 1 and following:
                        turn_keys(0)
                    return w

                w = attention_weights()
                keys_and_values(w[1])
                queries(w[0], 0)
                turn_keys(0)
                query_squares()

                w = attend(0, w, first=True)
                for i in t.loop(3, **PER["att", "pe"]):
                    for pair in range(2):
                        w = attend(0, attend(1, w))
                w = attend(0, attend(1, w), last=True)
                attend(1, w, last=True)
                pe.wait_ge(s["tp_free"], t.last("tp", 4))
                weighted_values(1)

                pe.wait_ge(s["mixed"], 8 * (layer + 1))
                for i in t.loop(2, **PER["out", "pe"]):
                    features((YH, YL))
                    features((YH, YL))
                norm_statistics()

                pe.wait_ge(s["mem_normed"], t.next("mem_normed").n)
                for pair in range(4):
                    bank = open_tp()
                    for c in range(2):
                        for mt in range(2):
                            mm = nc.tensor.transpose(bank[:, (c * 2 + mt) * P:(c * 2 + mt + 1) * P],
                                                     MEM[:, mt, (pair * 2 + c) * P:(pair * 2 + c + 1) * P], ident[:, :])
                    mm.then_inc(s["tp_ready"], 1)
                pe.wait_ge(s["tp_free"], t.last("tp", 4))
                for i in t.loop(2, **PER["mem", "pe"]):
                    for head in range(2):
                        for kv in range(2):
                            wh, wl = (unit3(w) for w in weights())
                            bank = open_acc()
                            for mt in range(2):
                                cols = slice(mt * P, (mt + 1) * P)
                                for c in range(C):
                                    mm = product(bank[:, mt, 0:UW], (MTH[:, c, cols], MTL[:, c, cols]),
                                                 (wh[:, c, :], wl[:, c, :]), c == 0, c == C - 1)
                            mm.then_inc(s["acc_ready"], 1)
                        features((XH, XL))
                        pe.wait_ge(s["mk"], t.next("mk").n)
                        pe.wait_ge(s["mc_in"], t.next("mc_in").at(0, 32))
                        for src in (MF, MC[:, :, 0, :]):
                            bank = open_tp()
                            for dc in range(2):
                                for mt in range(2):
                                    mm = nc.tensor.transpose(bank[:, (dc * 2 + mt) * P:(dc * 2 + mt + 1) * P],
                                                             src[:, mt, dc * P:(dc + 1) * P], ident[:, :])
                            mm.then_inc(s["tp_ready"], 1)
                        bank = open_tp()
                        t.skip("mq_sq", 1)
                        pe.wait_ge(s["mq_sq"], t.next("mq_sq").n)
                        for tt in range(TT):
                            for dc in range(2):
                                mm = nc.tensor.matmul(bank[0:rows(tt), tt:tt + 1], (SQ, SQT)[dc][:, tt * P:tt * P + rows(tt)],
                                                      ones[:, 0:1], start=dc == 0, stop=dc == 1)
                        mm.then_inc(s["tp_ready"], 1)
                        pe.wait_ge(s["mq_lo"], t.next("mq_lo").n)
                        bank = open_acc()
                        for tt in range(4):
                            for dc in range(2):
                                cols = slice(tt * P, (tt + 1) * P)
                                mm = product(bank[:, tt // 2, (tt % 2) * N_MEM:(tt % 2 + 1) * N_MEM],
                                             (QMH[:, dc, cols], QML[:, dc, cols]), (KMH[:, 0, dc, :], KML[:, 0, dc, :]),
                                             dc == 0, dc == 1)
                        mm.then_inc(s["acc_ready"], 1)
                        bank = open_acc()
                        for dc in range(2):
                            mm = product(bank[0:NEW, 0, 0:N_MEM], (QMH[:, dc, SEQ:T], QML[:, dc, SEQ:T]),
                                         (KMH[:, 1, dc, :], KML[:, 1, dc, :]), dc == 0, dc == 1)
                        mm.then_inc(s["acc_ready"], 1)
                        pe.wait_ge(s["pm"], t.next("pm").n)
                        for mt in range(2):
                            bank = open_tp()
                            for tt in range(4):
                                mm = nc.tensor.transpose(bank[:, tt * P:(tt + 1) * P], PM[:, tt, mt * P:(mt + 1) * P], ident[:, :])
                            mm.then_inc(s["tp_ready"], 1)
                        pe.wait_ge(s["pms"], t.next("pms").n)
                        bank = open_tp()
                        for mt, turn in enumerate((nc.tensor.matmul, nc.tensor.transpose)):
                            mm = turn(bank[:, mt * NEW:(mt + 1) * NEW], SQT[0:NEW, mt * P:(mt + 1) * P], ident[0:NEW, 0:NEW])
                        mm.then_inc(s["tp_ready"], 1)
                        pe.wait_ge(s["tp_free"], t.last("tp", 4))
                        for dc in range(2):
                            bank = open_acc()
                            for which, (b, cols, n) in enumerate(((0, slice(0, SEQ), SEQ), (1, slice(SEQ, T), NEW))):
                                for mt in range(2):
                                    mm = product(bank[:, b, 0:n], (VMH[:, which, mt, dc * P:(dc + 1) * P], VML[:, which, mt, dc * P:(dc + 1) * P]),
                                                 (PMH[:, mt, cols], PML[:, mt, cols]), mt == 0, mt == 1)
                            mm.then_inc(s["acc_ready"], 1)
                pe.wait_ge(s["acc_free"], t.last("acc", 2))
                for i in t.loop(2, **PER["out", "pe"]):
                    features((YH, YL))
                    features((YH, YL))
                norm_statistics()

                def ffn_piece(tiles):
                    for pair in range(tiles // 2):
                        features((XH, XL))
                        features((XH, XL))
                    t.skip("hidden", tiles // 2 - 1)
                    pe.wait_ge(s["hidden"], t.next("hidden").n)
                    for k in range(4):
                        features((YH, YL), tiles)

                if layer == 0:
                    for i in t.loop(2, **PER["dense", "pe"]):
                        ffn_piece(8)
                    ffn_piece(6)
                else:
                    pe.wait_ge(s["router"], t.next("router").n)
                    bank = open_tp()
                    for tt in range(TT):
                        cols = slice(tt * P, tt * P + rows(tt))
                        for c in range(C):
                            mm = product(bank[0:rows(tt), tt * EXPERTS:(tt + 1) * EXPERTS], (XH[:, c, cols], XL[:, c, cols]),
                                         (RWH[:, c, :], RWL[:, c, :]), c == 0, c == C - 1)
                    mm.then_inc(s["tp_ready"], 1)
                    bank = open_acc()
                    pe.wait_ge(s["gates"], t.next("gates").n)
                    for tt in range(TT):
                        n = rows(tt)
                        mm = nc.tensor.transpose(bank[0:EXPERTS, tt // 4, (tt % 4) * P:(tt % 4) * P + n], LG[0:n, 7, tt, :], ident[0:n, 0:n])
                    mm.then_inc(s["acc_ready"], 1)
                    for i in t.loop(EXPERTS, **PER["moe", "pe"]):
                        pe.wait_ge(s["gate_row"], t.next("gate_row").n)
                        for k in range(4):
                            bank = open_tp()
                            nc.tensor.matmul(bank[:, 0:T // 4], ones[0:EXPERTS, :], GM[:, k * (T // 4):(k + 1) * (T // 4)],
                                             start=True, stop=True).then_inc(s["tp_ready"], 1)
                        ffn_piece(8)

                pe.wait_ge(s["outc"], t.next("outc").n)
                bank = open_acc()
                for c in range(C):
                    mm = nc.tensor.transpose(bank[0:8, c // 4, (c % 4) * P:(c % 4 + 1) * P], OUTC[:, c, :], ident[:, :])
                mm.then_inc(s["acc_ready"], 1)

            pe.wait_ge(s["y_done"], 1)
            for tt in range(TT):
                bank = open_acc()
                for c in range(C):
                    mm = nc.tensor.transpose(bank[0:rows(tt), c // 4, (c % 4) * P:(c % 4 + 1) * P], X[:, c, tt * P:tt * P + rows(tt)],
                                             ident[:, :])
                mm.then_inc(s["acc_ready"], 1)

        @block.scalar
        def _(act):
            t = Tally(act)
            fn = nc.scalar.activation

            def split_high(n=UNIT):
                m = t.next("unit")
                k = m.slot(2)
                act.wait_ge(s["landed%d" % k], m.use(2, LANDED))
                fn(WH[:, k, 0:n], RAW[:, k, 0:n], ACT.Copy).then_inc(s["w_hi"], 1)

            def unit_tiles():
                a = t.next("acc")
                act.wait_ge(s["acc_ready"], a.n)
                split_high()
                return a, t.next("acc")

            def emptied(m):
                act.wait_ge(s["acc_free"], m.at(2))

            def prepare(m, c, row):
                emptied(m)
                fn(row_of(XH, c), row_of(X, c), ACT.Copy, scale=gain_of(c, row)).then_inc(s["x_hi"], 1)
                fn(SQT[:], row_of(X, c), ACT.Square).then_inc(s["x_sq"], 1)

            def turned(parts):
                m = t.next("tp")
                act.wait_ge(s["tp_ready"], m.n)
                todo = parts(TP[:, m.slot(4)])
                for k, (out, src, *gain) in enumerate(todo):
                    ins_ = fn(out, src, ACT.Copy, **({"scale": gain[0]} if gain else {}))
                    if k == len(todo) - 1:
                        ins_.then_inc(s["tp_hi"], 1)

            def turned_acc(parts):
                m = t.next("acc")
                act.wait_ge(s["acc_ready"], m.n)
                todo = parts(ACC[:, m.slot(2)])
                for k, (out, src, *gain) in enumerate(todo):
                    ins_ = fn(out, src, ACT.Copy, **({"scale": gain[0]} if gain else {}))
                    if k == len(todo) - 1:
                        ins_.then_inc(s["acc_hi"], 1)

            def output_projection(row):
                for i in t.loop(2, **PER["out", "act"]):
                    for u in range(2):
                        for f, m in enumerate(unit_tiles()):
                            prepare(m, i * 4 + (2 * u + f), row)
                t.skip("tp", 1)
                t.skip("acc", 1)

            split_high()
            t.skip("tp", 1)
            act.wait_ge(s["params"], 1)
            for c in range(C):
                prepare(t.next("acc"), c, R_MIX)

            for layer in range(DEPTH):
                base = layer * ROWS
                t.skip("tp", 1)
                t.skip("acc", 1)
                act.wait_ge(s["lam_abs"], layer + 1)
                fn(LAM[:, :, 2], LAM[:, :, 1], ACT.Exp, scale=-1.0).then_inc(s["lam_exp"], 1)
                act.wait_ge(s["lam"], layer + 1)
                act.wait_ge(s["blocks_in"], 64 * (layer + 1))
                for i in t.loop(C // 2, **PER["mix", "act"]):
                    unit_tiles()
                    fn(BDH[:], BD[:, :, bass.ds(i * 2, 2), :], ACT.Copy).then_inc(s["bd_hi"], 1)
                    act.wait_ge(s["xc"], t.next("xc").n)
                    fn(XCH[:], XC[:], ACT.Copy).then_inc(s["xc_hi"], 1)
                    emptied(unit_tiles()[1])
                    fn(LU[:, :, 0:T], G[:], ACT.Square).then_inc(s["g_sq"], 1)
                    act.wait_ge(s["g_z"], t.next("g_z").n)
                    fn(LU[:, :, 0:T], LU[:, :, 0:T], ACT.Tanh, scale=GELU_C).then_inc(s["g_th"], 1)
                    emptied(unit_tiles()[1])
                    pair = TGA[:, bass.ds(i * 2, 2), :]
                    fn(pair, pair, ACT.Tanh, scale=0.5).then_inc(s["gatt"], 1)
                    for f in range(2):
                        for gate, dst in enumerate((TR, TI)):
                            for h in range(2):
                                m = t.next("tp")
                                act.wait_ge(s["tp_ready"], m.n)
                                fn(dst[:, f, h * (CONV // 2):(h + 1) * (CONV // 2)], TP[:, m.slot(4), 0:CONV // 2], ACT.Tanh,
                                   bias=HBT[:, f, gate:gate + 1], scale=0.5).then_inc(s["tp_free"], 1)
                    act.wait_ge(s["tp_free"], m.at(4))
                    act.wait_ge(s["g_gelu"], t.next("g_gelu").n)
                    for f in range(2):
                        sp, neg = (LAM[:, bass.ds(i * 2 + f, 1), j] for j in (0, 3))
                        fn(LU[:, f, :], TR[:, f, :], ACT.Tanh, bias=sp, scale=sp).then_inc(s["lru_t"], 1)
                        fn(LA[:, f, :], TR[:, f, :], ACT.Exp, bias=neg, scale=neg).then_inc(s["lru_a"], 1)
                    split_high()
                    act.wait_ge(s["lru_w"], t.next("lru_w").n)
                    fn(TR[:], TR[:], ACT.Sqrt).then_inc(s["lru_sqrt"], 1)
                    t.skip("acc", 1)
                    emptied(t.next("acc"))
                    fn(XP[:, :, 3:3 + T], XP[:, :, 3:3 + T], ACT.Tanh, scale=0.5).then_inc(s["grec"], 1)

                for n in range(3):
                    unit_tiles()
                    t.skip("acc", 1)
                q_gain = [PT[:, c, base + R_QLAT:base + R_QLAT + 1] for c in range(3)]
                for c in range(3):
                    turned_acc(lambda b: [(CQH[:, c, 0:SEQ], b[:, 0, :], q_gain[c]), (CQH[:, c, SEQ:T], b[:, 1, 0:NEW], q_gain[c])])
                for c in range(2):
                    turned_acc(lambda b: [(CKH[:, c, 0:SEQ], b[:, 0, :]), (CKH[:, c, SEQ:T], b[:, 1, 0:NEW])])
                for c in range(2):
                    turned(lambda b: [(CKH[:, c, T:KEYS], b)])
                act.wait_ge(s["latents_out"], 64 * (layer + 1))

                def values_high(first):
                    if not first:
                        act.wait_ge(s["tp_ready"], t.last("tp"))
                    fn(key_tiles(VH, 0, 6), VF(0, 6), ACT.Copy)
                    fn(key_tiles(VH, 6, 3), VF(6, 3), ACT.Copy).then_inc(s["v_hi"], 1)

                def keys_out(first=False):
                    if not first:
                        act.wait_ge(s["v_lo"], t.next("v_lo").n)
                    for n, kt in enumerate((0, 5, 4)):
                        m = t.next("acc")
                        if n == 0:
                            act.wait_ge(s["acc_free"], m.at(1))
                        act.wait_ge(s["acc_ready"], m.n)
                        bank = ACC[:, m.slot(2)]
                        if kt == 4:
                            fn(VF(4, 1, NEW), bank[0:NEW, 0, P:2 * P], ACT.Copy)
                            fn(key_tiles(KF, 4, 1, NEW), bank[0:NEW, 0, 0:P], ACT.Copy).then_inc(s["acc_free"], 1)
                        else:
                            kv = bank.rearrange("p h (t n) -> p (h t) n", n=UW)
                            if kt == 0:
                                fn(VF(0, 4).rearrange("p (t n) -> p t n", n=P), kv[:, :, P:UW], ACT.Copy)
                            else:
                                fn(VF(5, 1), kv[:, 0, P:UW], ACT.Copy)
                                fn(VF(6, 3).rearrange("p (t n) -> p t n", n=P), kv[:, 1:4, P:UW], ACT.Copy)
                            fn(KF[:, kt:kt + 4].rearrange("p t a b -> p t (a b)"), kv[:, :, 0:P], ACT.Copy).then_inc(s["acc_free"], 1)
                    act.wait_ge(s["acc_free"], m.at(2))
                    fn(KA[:, :, :, 0:NOPE], KF[:], ACT.Square).then_inc(s["k_sq"], 1)

                def queries_high():
                    m = t.next("acc")
                    act.wait_ge(s["acc_ready"], m.n)
                    fn(QSQ[0:QK, :].rearrange("p (a b) -> p a b", a=2), halves(ACC[0:QK, m.slot(2)]), ACT.Square)\
                        .then_inc(s["q_sq"], 1)
                    emptied(m)
                    fn(QTH[:], SQ[:], ACT.Copy).then_inc(s["q_hi"], 1)

                def keys_high():
                    turned(lambda b: [(KTH[:, 0:SEQ], b)])
                    turned(lambda b: [(KTH[:, SEQ:SEQ + 448], b[:, 0:448])])
                    turned(lambda b: [(KTH[:, SEQ + 448:KEYS], b[:, 0:P])])

                def exponentials(parts):
                    m = t.next("acc")
                    bank = ACC[:, m.slot(2)]
                    act.wait_ge(s["s_max"], t.next("s_max").n)
                    for out, h, at0, n, tt, total in parts:
                        r = NEW if tt == 4 else P
                        ins_ = fn(out, bank[0:r, h, at0:at0 + n], ACT.Exp, bias=sm[0:r, 8 + tt:9 + tt],
                                  scale=sm[0:r, 24 + tt:25 + tt], accum_out=sm[0:r, total:total + 1])
                    ins_.then_inc(s["p_exp"], 1)

                def mixed_high(tile):
                    act.wait_ge(s["mix_sum"], t.next("mix_sum").n)
                    fn(YH[:, bass.ds(tile, 1), :], AO[:].rearrange("p (a b) -> p a b", a=1), ACT.Copy, scale=0.25)\
                        .then_inc(s["mix_hi"], 1)

                def attend(head, tile=None, first=False, last=False, split=UA):
                    following = not (last and head == 1)
                    exponentials([(P01[0], 0, 0, P, 0, 16), (P01[1], 1, 0, 2 * P, 1, 17),
                                  (P0[:, 0:3 * P], 0, P, 3 * P, 4, 20), (P0[:, 3 * P:T], 1, 2 * P, T - 3 * P, 4, 21)])
                    exponentials([(P23[0][:], 0, 0, 3 * P, 2, 18), (P23[1][:], 1, 0, 4 * P, 3, 19)])
                    if not first:
                        t.skip("tp", 2)
                    if head == 0:
                        keys_high()
                    if following:
                        queries_high()
                    if head == 0:
                        values_high(first)
                    turned(lambda b: [(PTH[:, 0, :], b[:, 0:P]),
                                      (PTH[:, 1:5:3, :], b[:, P:3 * P].rearrange("p (a b) -> p a b", a=2))])
                    if following:
                        t.skip("tp", 1)
                    turned(lambda b: [(PSH[0:NEW, 0, :], b[0:NEW, 0:NEW]),
                                      (PSH[:, 1:TT, :], b[:, NEW:TT * NEW].rearrange("p (a b) -> p a b", a=4))])
                    if tile is not None:
                        mixed_high(tile)
                    if head == 0 and not last:
                        keys_out()
                    turned(lambda b: [(PTH[:, 2:9:3, :], b[:, 0:3 * P].rearrange("p (a b) -> p a b", a=3))])
                    turned(lambda b: [(PTH[:, 3:13:3, :], b.rearrange("p (a b) -> p a b", a=4))])
                    if head == 1 and following:
                        keys_high()
                    if head == 1 and split and not last:
                        split_high(split)

                act.wait_ge(s["acc_ready"], t.last("acc", 1))
                split_high(UA)
                act.wait_ge(s["keys_clear"], layer + 1)
                keys_out(first=True)
                queries_high()
                keys_high()
                t.skip("tp", 1)
                attend(0, first=True)
                for i in t.loop(3, **PER["att", "act"]):
                    for pair in range(2):
                        attend(1)
                        attend(0, tile=i * 2 + pair)
                attend(1, split=0)
                attend(0, tile=6, last=True)
                attend(1, last=True)
                split_high()
                t.skip("tp", 2)
                t.skip("v_lo", 1)
                mixed_high(7)

                output_projection(base + R_NMEM)

                act.wait_ge(s["mem_in"], 32 * (layer + 1))
                for mt in range(2):
                    if mt:
                        act.wait_ge(s["mem_sq"], 2 * layer + 1)
                    fn(QF[:].rearrange("p a b -> p (a b)")[:, 0:D], MEM[:, mt, :], ACT.Square, accum_out=sm[:, mt:mt + 1])\
                        .then_inc(s["mem_sq"], 1)
                for p4 in range(4):
                    turned(lambda b: [(MTH[:, 2 * p4 + c, :], b[:, c * 2 * P:(c + 1) * 2 * P],
                                       PT[:, 2 * p4 + c, base + R_MEMIN:base + R_MEMIN + 1]) for c in range(2)])
                for i in t.loop(2, **PER["mem", "act"]):
                    for head in range(2):
                        split_high()
                        m = t.next("acc")
                        act.wait_ge(s["acc_ready"], m.n)
                        split_high()
                        emptied(m)
                        for mt in range(2):
                            fn(QF[:, mt, 0:MEM_D], MF[:, mt, :], ACT.Square, accum_out=sm[:, mt:mt + 1]).then_inc(s["mk_sq"], 1)
                        m = t.next("acc")
                        act.wait_ge(s["acc_ready"], m.n)
                        split_high()
                        emptied(m)
                        fn(VMH[:, 0], MV[:], ACT.Copy).then_inc(s["vm_hi"], 1)
                        act.wait_ge(s["mc_in"], t.next("mc_in").at(0, 32))
                        fn(VMH[:, 1], MC[:, :, 1, :], ACT.Copy).then_inc(s["vm_hi"], 1)
                        for dc in range(2):
                            emptied(t.next("acc"))
                            fn((SQ, SQT)[dc][:], QF[:, dc, :], ACT.Square).then_inc(s["mq_sq"], 1)
                            fn(QMH[:, dc, :], QF[:, dc, :], ACT.Copy, scale=PT[:, dc, base + R_MQ:base + R_MQ + 1])\
                                .then_inc(s["mq_hi"], 1)
                        for which in range(2):
                            turned(lambda b: [(KMH[:, which].rearrange("p a b -> p (a b)"), b)])
                        t.skip("tp", 1)
                        m = t.next("acc")
                        act.wait_ge(s["s_max"], t.next("s_max").n)
                        for tt in range(4):
                            ins_ = fn(PM[:, tt, :], ACC[:, m.slot(2), tt // 2, (tt % 2) * N_MEM:(tt % 2 + 1) * N_MEM], ACT.Exp,
                                      bias=sm[:, 8 + tt:9 + tt], scale=sm[:, 24 + tt:25 + tt], accum_out=sm[:, 16 + tt:17 + tt])
                        ins_.then_inc(s["p_exp"], 1)
                        m = t.next("acc")
                        act.wait_ge(s["s_max"], t.next("s_max").n)
                        fn(SQT[0:NEW, 0:N_MEM], ACC[0:NEW, m.slot(2), 0, 0:N_MEM], ACT.Exp, bias=sm[0:NEW, 12:13], scale=sm[0:NEW, 28:29],
                           accum_out=sm[0:NEW, 20:21]).then_inc(s["p_exp"], 1)
                        act.wait_ge(s["mem_place"], t.next("mem_place").at(1))
                        for mt in range(2):
                            turned(lambda b: [(PMH[:, mt, 0:SEQ], b)])
                        turned(lambda b: [(PMH[:, :, SEQ:T], b[:, 0:2 * NEW].rearrange("p (a b) -> p a b", a=2))])
                        for dc in range(2):
                            row = bass.ds(i * 4 + (2 * head + dc), 1)
                            turned_acc(lambda b: [(YH[:, row, 0:SEQ], b[:, 0:1, :]), (YH[:, row, SEQ:T], b[:, 1:2, 0:NEW])])
                output_projection(base + R_NFFN)

                def hidden_tiles(tiles):
                    for pair in range(tiles // 2):
                        emptied(unit_tiles()[1])
                        fn(TH[:], H1[:], ACT.Tanh, scale=0.5).then_inc(s["f_th"], 1)
                        unit_tiles()
                        act.wait_ge(s["f_hid"], t.next("f_hid").n)
                        fn(YH[:, 2 * pair:2 * pair + 2, :], H1[:], ACT.Copy).then_inc(s["f_hi"], 1)

                if layer == 0:
                    for i in t.loop(2, **PER["dense", "act"]):
                        hidden_tiles(8)
                        for k in range(4):
                            unit_tiles()
                    hidden_tiles(6)
                    for k in range(4):
                        for f, m in enumerate(unit_tiles()):
                            prepare(m, 2 * k + f, ROWS + R_MIX)
                else:
                    act.wait_ge(s["router_in"], 48)
                    fn(RWH[:], RW[:], ACT.Copy).then_inc(s["router_hi"], 1)
                    t.skip("tp", 1)
                    t.skip("acc", 1)
                    act.wait_ge(s["lg_shift"], 1)
                    fn(LG[:, 1], LG[:, 1], ACT.Exp).then_inc(s["lg_exp"], 1)
                    for i in t.loop(EXPERTS, **PER["moe", "act"]):
                        t.skip("tp", 4)
                        hidden_tiles(8)
                        for k in range(4):
                            unit_tiles()
                t.skip("acc", 1)

        @block.vector
        def _(dve):
            t = Tally(dve)
            v = nc.vector

            def step(ins_):
                ins_.then_inc(s["dve_step"], 1)
                dve.wait_ge(s["dve_step"], t.next("dve_step").n)

            def split_low(n=UNIT):
                m = t.next("unit")
                k = m.slot(2)
                dve.wait_ge(s["w_hi"], m.n)
                v.tensor_tensor(WL[:, k, 0:n], RAW[:, k, 0:n], WH[:, k, 0:n].bitcast(F32), ALU.subtract).then_inc(s["w_lo"], 1)

            def take_acc():
                m = t.next("acc")
                dve.wait_ge(s["acc_ready"], m.n)
                return ACC[:, m.slot(2)], m

            def take_tp():
                m = t.next("tp")
                dve.wait_ge(s["tp_ready"], m.n)
                return TP[:, m.slot(4)], m

            def turned(parts):
                bank, m = take_tp()
                dve.wait_ge(s["tp_hi"], t.next("tp_hi").n)
                lows(parts(bank)).then_inc(s["tp_free"], 1)

            def turned_acc(parts):
                bank, m = take_acc()
                dve.wait_ge(s["acc_hi"], t.next("acc_hi").n)
                lows(parts(bank)).then_inc(s["acc_free"], 1)

            def lows(todo):
                for out, src, high, *gain in todo:
                    if gain:
                        ins_ = v.scalar_tensor_tensor(out=out, in0=src, scalar=gain[0], in1=high.bitcast(F32), op0=ALU.mult, op1=ALU.subtract)
                    else:
                        ins_ = v.tensor_tensor(out, src, high.bitcast(F32), ALU.subtract)
                return ins_

            def rsqrt(n, buffer=nwt):
                x, y, q = (buffer[:, k, 0:n] for k in (0, 2, 1))
                step(v.tensor_scalar(y.bitcast(I32), x.bitcast(I32), -0.5, 1597463007.0, ALU.mult, ALU.add))
                for _ in range(3):
                    step(v.scalar_tensor_tensor(out=q, in0=x, scalar=-0.5, in1=y, op0=ALU.mult, op1=ALU.mult))
                    step(v.tensor_tensor(q, q, y, ALU.mult))
                    step(v.scalar_tensor_tensor(out=y, in0=q, scalar=1.5, in1=y, op0=ALU.add, op1=ALU.mult))

            def token_means(bank, m, width):
                v.tensor_scalar(nwt[:, 0, 0:4], bank[:, 0:4], 1.0 / width, EPS, ALU.mult, ALU.add)
                v.tensor_scalar(nwt[0:NEW, 0, 4:5], bank[0:NEW, 4:5], 1.0 / width, EPS, ALU.mult, ALU.add).then_inc(s["tp_free"], 1)
                dve.wait_ge(s["tp_free"], m.at(4))

            def norm_statistics():
                bank, m = take_tp()
                token_means(bank, m, D)
                rsqrt(TT)
                step(v.tensor_copy(rt[:, 0:TT], nwt[:, 2, 0:TT]))
                for tt in range(TT):
                    n = rows(tt)
                    ins_ = v.tensor_scalar(SQT[0:n, tt * P:tt * P + n], ident[0:n, 0:n], rt[0:n, tt:tt + 1], None, ALU.mult)
                ins_.then_inc(s["diag"], 1)
                bank, m = take_acc()
                v.tensor_copy(RSTD[:, 0:SEQ], bank[:, 0, :])
                v.tensor_copy(RSTD[:, SEQ:T], bank[:, 1, 0:NEW]).then_inc(s["acc_free"], 1)
                dve.wait_ge(s["acc_free"], m.at(2))

            def prepare(c, row):
                dve.wait_ge(s["x_hi"], t.next("x_hi").n)
                v.scalar_tensor_tensor(out=row_of(XL, c), in0=row_of(X, c), scalar=gain_of(c, row), in1=row_of(XH, c).bitcast(F32),
                                       op0=ALU.mult, op1=ALU.subtract)
                dve.wait_ge(s["x_sq"], t.next("x_sq").n)
                v.tensor_tensor(SQ[:], SQ[:], SQT[:], ALU.add).then_inc(s["sq_sum"], 1)
                dve.wait_ge(s["sq_sum"], t.next("sq_sum").n)

            def add_residual(bank, m, c):
                x = row_of(X, c).rearrange("p (a b) -> p a b", a=2)
                v.tensor_tensor(x, halves(bank), x, ALU.add).then_inc(s["acc_free"], 1)

            def scaled(out, bank, by):
                a2 = lambda ap: ap.rearrange("p o (a b) -> p (o a) b", a=2) if len(ap.shape) == 3 else ap.rearrange("p (a b) -> p a b", a=2)
                return v.tensor_tensor(a2(out), halves(bank), a2(by), ALU.mult).then_inc(s["acc_free"], 1)

            def output_projection(row):
                step(v.memset(SQ[:], 0.0))
                for i in t.loop(2, **PER["out", "dve"]):
                    for u in range(2):
                        for f in range(2):
                            bank, m = take_acc()
                            c = i * 4 + (2 * u + f)
                            add_residual(bank, m, c)
                            if f == 0:
                                split_low()
                            dve.wait_ge(s["acc_free"], m.at(2))
                            prepare(c, row)
                norm_statistics()

            def marker(name):
                k = ("w_free", "params", "lam_abs", "lam", "mc_free", "mq_lo", "y_done", "outc", "state_rows", "y_rows", "rk").index(name)
                return v.memset(nwt[:, 5, k:k + 1], 0.0)

            def w_region_free():
                marker("w_free").then_inc(s["w_free"], 1)

            v.memset(nwt[:], 1.0)
            v.memset(sm[:], 1.0)
            v.memset(rp[:], 0.0)
            v.memset(OUTC[:], 0.0)
            step(v.memset(SQ[:], 0.0))
            split_low()
            bank, m = take_tp()
            v.tensor_copy(PT[:], bank[:, 0:C * DEPTH * ROWS].rearrange("p (c r) -> p c r", c=C)).then_inc(s["tp_free"], 1)
            dve.wait_ge(s["tp_free"], m.at(4))
            marker("params").then_inc(s["params"], 1)
            for c in range(C):
                bank, m = take_acc()
                v.tensor_copy(X[:, c, 0:SEQ], bank[:, 0, :])
                v.tensor_copy(X[:, c, SEQ:T], bank[:, 1, 0:NEW]).then_inc(s["acc_free"], 1)
                dve.wait_ge(s["acc_free"], m.at(2))
                prepare(c, R_MIX)

            for layer in range(DEPTH):
                base = layer * ROWS
                w_region_free()
                lam = PT[:, :, base + R_LAM]
                L = [LAM[:, :, k] for k in range(8)]
                step(v.tensor_scalar(L[0], lam, -1.0, None, ALU.mult))
                step(v.tensor_tensor(L[1], L[0], lam, ALU.max))
                marker("lam_abs").then_inc(s["lam_abs"], 1)
                step(v.tensor_scalar(L[4], L[0], 0.0, 4.0, ALU.max, ALU.mult))
                dve.wait_ge(s["lam_exp"], layer + 1)
                step(v.tensor_scalar(L[5], L[2], 2.0, None, ALU.add))
                step(v.reciprocal(L[5], L[5]))
                step(v.tensor_tensor(L[5], L[5], L[2], ALU.mult))
                step(v.tensor_tensor(L[6], L[5], L[5], ALU.mult))
                step(v.tensor_scalar(L[7], L[6], 1.0 / 19, 1.0 / 17, ALU.mult, ALU.add))
                for k in (15, 13, 11, 9, 7, 5, 3, 1):
                    step(v.tensor_tensor(L[7], L[7], L[6], ALU.mult))
                    step(v.tensor_scalar(L[7], L[7], 1.0 / k, None, ALU.add))
                step(v.tensor_tensor(L[7], L[7], L[5], ALU.mult))
                step(v.scalar_tensor_tensor(out=L[0], in0=L[7], scalar=8.0, in1=L[4], op0=ALU.mult, op1=ALU.add))
                step(v.tensor_scalar(L[3], L[0], -1.0, None, ALU.mult))
                step(v.tensor_scalar(HB[:], PT[:, :, base + R_BA:base + R_BA + 2], 0.5, None, ALU.mult))
                if layer:
                    dve.wait_ge(s["state_out"], 64 * layer)
                v.memset(XP[:, :, 0:3], 0.0)
                step(v.memset(XP[:, :, CONV + 2:CONV + 4], 0.0))
                marker("lam").then_inc(s["lam"], 1)
                norm_statistics()
                dve.wait_ge(s["blocks_in"], 64 * (layer + 1))

                for i in t.loop(C // 2, **PER["mix", "dve"]):
                    pair = bass.ds(i * 2, 2)
                    for f in range(2):
                        bank, m = take_acc()
                        step(v.tensor_copy(XP[:, f:f + 1, SEQ + 3:SEQ + 6], PT[:, bass.ds(i * 2 + f, 1), base + R_CONV:base + R_CONV + 3]))
                        v.tensor_tensor(XP[:, f, 3:3 + HALF], bank[:, 0, 0:HALF], RSTD[:, 0:HALF], ALU.mult)
                        v.tensor_tensor(XP[:, f, 3 + HALF:3 + SEQ], bank[:, 1, 0:SEQ - HALF], RSTD[:, HALF:SEQ], ALU.mult)
                        v.tensor_tensor(XP[:, f, SEQ + 6:T + 6], bank[:, 1, SEQ - HALF:HALF], RSTD[:, SEQ:T], ALU.mult)\
                            .then_inc(s["acc_free"], 1)
                        if f == 0:
                            split_low()
                    v.tensor_copy(HBT[:], HB[:, pair, :])
                    dve.wait_ge(s["bd_hi"], t.next("bd_hi").n)
                    v.tensor_tensor(BDL[:], BD[:, :, pair, :], BDH[:].bitcast(F32), ALU.subtract)
                    dve.wait_ge(s["acc_free"], m.at(2))
                    v.tensor_copy(OUTC[:, pair, 0:3], XP[:, :, SEQ:SEQ + 3])
                    v.tensor_copy(OUTC[:, pair, 4:7], XP[:, :, T + 3:T + 6])
                    for j in range(4):
                        for f in range(2):
                            ch = bass.ds(i * 2 + f, 1)
                            w = PT[:, ch, base + R_CW + j]
                            if j == 0:
                                ins_ = v.tensor_scalar(XC[:, f, :], XP[:, f, 0:CONV], w, PT[:, ch, base + R_CB], ALU.mult, ALU.add)
                            else:
                                ins_ = v.scalar_tensor_tensor(out=XC[:, f, :], in0=XP[:, f, j:j + CONV], scalar=w, in1=XC[:, f, :],
                                                              op0=ALU.mult, op1=ALU.add)
                            if (j, f) == (3, 1):
                                ins_.then_inc(s["xc"], 1)
                            elif f == 1:
                                step(ins_)
                    dve.wait_ge(s["xc_hi"], t.next("xc_hi").n)
                    v.tensor_tensor(XCL[:], XC[:], XCH[:].bitcast(F32), ALU.subtract).then_inc(s["xc_lo"], 1)
                    for f in range(2):
                        bank, m = take_acc()
                        scaled(G[:, f, :], bank, RSTD[:])
                        if f == 0:
                            split_low()
                    dve.wait_ge(s["g_sq"], t.next("g_sq").n)
                    z = LU[:, :, 0:T]
                    step(v.tensor_scalar(z, z, 0.044715, 1.0, ALU.mult, ALU.add))
                    v.tensor_tensor(z, z, G[:], ALU.mult).then_inc(s["g_z"], 1)
                    dve.wait_ge(s["g_th"], t.next("g_th").n)
                    v.scalar_tensor_tensor(out=G[:], in0=z, scalar=1.0, in1=G[:], op0=ALU.add, op1=ALU.mult).then_inc(s["g_gelu"], 1)
                    for f in range(2):
                        bank, m = take_acc()
                        scaled(TGA[:, bass.ds(i * 2 + f, 1), :], bank, RSTD[:])
                        if f == 0:
                            split_low()
                    t.skip("gatt", 1)
                    t.skip("tp", 8)
                    dve.wait_ge(s["lru_t"], t.next("lru_t").at(1))
                    t.skip("lru_t", 1)
                    dve.wait_ge(s["lru_a"], t.next("lru_a").at(1))
                    t.skip("lru_a", 1)
                    step(v.tensor_scalar(TR[:], LU[:], 1.0, None, ALU.add))
                    step(v.reciprocal(TR[:], TR[:]))
                    step(v.tensor_tensor(TR[:], TR[:], LU[:], ALU.mult))
                    v.tensor_scalar(TR[:], TR[:], 0.5, 0.0, ALU.mult, ALU.max).then_inc(s["lru_w"], 1)
                    step(v.scalar_tensor_tensor(out=TI[:], in0=TI[:], scalar=1.0, in1=XC[:], op0=ALU.add, op1=ALU.mult))
                    split_low()
                    for f in range(2):
                        bank, m = take_acc()
                        scaled(XP[:, f, 3:3 + T], bank, RSTD[:])
                    dve.wait_ge(s["lru_sqrt"], t.next("lru_sqrt").n)
                    step(v.tensor_tensor(LU[:], TI[:], TR[:], ALU.mult))
                    for f in range(2):
                        v.tensor_tensor_scan(TI[:, f, 0:SEQ], LA[:, f, 0:SEQ], LU[:, f, 0:SEQ], 0.0, ALU.mult, ALU.add)
                        ins_ = v.tensor_tensor_scan(TI[:, f, SEQ + 3:T + 3], LA[:, f, SEQ + 3:T + 3], LU[:, f, SEQ + 3:T + 3],
                                                    PT[:, bass.ds(i * 2 + f, 1), base + R_LRU], ALU.mult, ALU.add)
                    step(ins_)
                    v.tensor_copy(OUTC[:, pair, 3:4], TI[:, :, SEQ - 1:SEQ])
                    v.tensor_copy(OUTC[:, pair, 7:8], TI[:, :, T + 2:T + 3])
                    v.tensor_tensor(G[:, :, 0:SEQ], G[:, :, 0:SEQ], TI[:, :, 0:SEQ], ALU.mult)
                    step(v.tensor_tensor(G[:, :, SEQ:T], G[:, :, SEQ:T], TI[:, :, SEQ + 3:T + 3], ALU.mult))
                    dve.wait_ge(s["grec"], t.next("grec").n)
                    step(v.scalar_tensor_tensor(out=REC[:, pair, :], in0=XP[:, :, 3:3 + T], scalar=1.0, in1=G[:], op0=ALU.add, op1=ALU.mult))

                v.memset(RPT[NEW:P, 4], 0.0)
                w_region_free()
                for n, width in enumerate((UW, UW, LAT - 2 * UW)):
                    for k, pair in enumerate(((0, 1), (2, 3), (4,))):
                        bank, m = take_acc()
                        for h, tt in enumerate(pair):
                            r = rows(tt)
                            ins_ = v.tensor_scalar(Z[0:r, tt, n * UW:n * UW + width], bank[0:r, h, 0:width], rt[0:r, tt:tt + 1], None, ALU.mult)
                        ins_.then_inc(s["acc_free"], 1)
                        if k == 0:
                            split_low()
                step(v.memset(Z[NEW:P, 4, :], 1.0))
                dve.wait_ge(s["acc_free"], m.at(2))
                step(v.tensor_tensor(ZQ[:], Z[:, :, 0:Q_LORA], Z[:, :, 0:Q_LORA], ALU.mult))
                step(v.tensor_reduce(nwt[:, 4, 0:TT], ZQ[:], AX_X, ALU.add))
                step(v.tensor_scalar(nwt[:, 0, 0:TT], nwt[:, 4, 0:TT], 1.0 / Q_LORA, EPS, ALU.mult, ALU.add))
                step(v.tensor_tensor(ZQ[:, :, 0:KV_LORA], Z[:, :, Q_LORA:Q_LORA + KV_LORA], Z[:, :, Q_LORA:Q_LORA + KV_LORA], ALU.mult))
                step(v.tensor_reduce(nwt[:, 4, 0:TT], ZQ[:, :, 0:KV_LORA], AX_X, ALU.add))
                step(v.tensor_scalar(nwt[:, 0, TT:2 * TT], nwt[:, 4, 0:TT], 1.0 / KV_LORA, EPS, ALU.mult, ALU.add))
                rsqrt(2 * TT)
                for tt in range(TT):
                    ins_ = v.tensor_scalar(ZQ[:, tt, :], Z[:, tt, 0:Q_LORA], nwt[:, 2, tt:tt + 1], None, ALU.mult)
                ins_.then_inc(s["zq"], 1)
                dve.wait_ge(s["latents_in"], 48 * (layer + 1))
                zkv = Z[:, :, Q_LORA:Q_LORA + KV_LORA]
                for tt in range(TT):
                    ins_ = v.scalar_tensor_tensor(out=zkv[:, tt, :], in0=zkv[:, tt, :], scalar=nwt[:, 2, TT + tt:TT + tt + 1], in1=GKV[:],
                                                  op0=ALU.mult, op1=ALU.mult)
                ins_.then_inc(s["zkv"], 1)
                kr = Z[:, :, Q_LORA + KV_LORA:LAT]
                half = ROPE // 2
                v.tensor_tensor(KR1[:], kr, RPT[:, :, 0, :], ALU.mult)
                v.tensor_tensor(KR2[:, :, 0:half], kr[:, :, half:ROPE], RPT[:, :, 1, 0:half], ALU.mult)
                step(v.tensor_tensor(KR2[:, :, half:ROPE], kr[:, :, 0:half], RPT[:, :, 1, half:ROPE], ALU.mult))
                v.tensor_tensor(rp[:, 0:TT, :], KR1[:], KR2[:], ALU.add).then_inc(s["rotated"], 1)
                dve.wait_ge(s["rotated"], layer + 1)
                dve.wait_ge(s["past_in"], 32 * (layer + 1))
                v.tensor_tensor(KRS[:], rp[:], rp[:], ALU.mult).then_inc(s["krs"], 1)
                dve.wait_ge(s["krs"], layer + 1)
                step(v.tensor_reduce(krs[:], KRS[:], AX_X, ALU.add))
                q_gain = [PT[:, c, base + R_QLAT:base + R_QLAT + 1] for c in range(3)]
                for c in range(3):
                    turned_acc(lambda b: [(CQL[:, c, 0:SEQ], b[:, 0, :], CQH[:, c, 0:SEQ], q_gain[c]),
                                          (CQL[:, c, SEQ:T], b[:, 1, 0:NEW], CQH[:, c, SEQ:T], q_gain[c])])
                for c in range(2):
                    turned_acc(lambda b: [(CKL[:, c, 0:SEQ], b[:, 0, :], CKH[:, c, 0:SEQ]),
                                          (CKL[:, c, SEQ:T], b[:, 1, 0:NEW], CKH[:, c, SEQ:T])])
                for c in range(2):
                    turned(lambda b: [(CKL[:, c, T:KEYS], b, CKH[:, c, T:KEYS])])
                step(v.tensor_tensor(nwt[:, 4, 0:1], PT[:, 0, base + R_QH:base + R_QH + 1], PT[:, 0, base + R_KH:base + R_KH + 1], ALU.mult))
                dve.wait_ge(s["rope_in"], 16 * (layer + 1))
                step(v.tensor_scalar(RSTD[:], RSTD[:], nwt[:, 4, 0:1], None, ALU.mult))
                v.memset(RK[:], 1.0)
                v.memset(KA[:], 0.0)
                v.memset(VF(4, 1), 0.0)
                v.memset(KF[:], 0.0).then_inc(s["keys_clear"], 1)
                dve.wait_ge(s["gatt"], 4 * (layer + 1))
                dve.wait_ge(s["latents_out"], 64 * (layer + 1))

                def key_roots():
                    dve.wait_ge(s["k_sum"], t.next("k_sum").n)
                    step(v.tensor_scalar(RK[:, 0, 0:2 * KT], RK[:, 0, 0:2 * KT], 1.0 / QK, EPS, ALU.mult, ALU.add))
                    rsqrt(2 * KT, RK)
                    marker("rk").then_inc(s["rk"], 1)

                def queries_low():
                    bank, m = take_acc()
                    dve.wait_ge(s["q_sq"], t.next("q_sq").n)
                    scaled(SQ[:], bank, RSTD[:])
                    dve.wait_ge(s["q_hi"], t.next("q_hi").n)
                    v.tensor_tensor(QTL[:], SQ[:], QTH[:].bitcast(F32), ALU.subtract).then_inc(s["q_lo"], 1)

                def keys_low():
                    turned(lambda b: [(KTL[:, 0:SEQ], b, KTH[:, 0:SEQ])])
                    turned(lambda b: [(KTL[:, SEQ:SEQ + 448], b[:, 0:448], KTH[:, SEQ:SEQ + 448])])
                    turned(lambda b: [(KTL[:, SEQ + 448:KEYS], b[:, 0:P], KTH[:, SEQ + 448:KEYS])])

                def query_means():
                    bank, m = take_tp()
                    token_means(bank, m, QK)

                def query_scales():
                    rsqrt(TT)
                    step(v.tensor_scalar(sm[:, 24:24 + TT], nwt[:, 2, 0:TT], QK ** -0.5, None, ALU.mult))

                def negative_max(r, a, b):
                    return v.scalar_tensor_tensor(out=sm[0:r, 8 + a:8 + b], in0=sm[0:r, a:b], scalar=-1.0, in1=sm[0:r, 24 + a:24 + b],
                                                  op0=ALU.mult, op1=ALU.mult)

                def head_output(head):
                    mine = slice(head * 64, head * 64 + 64)
                    bank, m = take_tp()
                    v.tensor_copy(AO[mine, 0:SEQ], bank[mine, :]).then_inc(s["tp_free"], 1)
                    bank, m = take_tp()
                    v.tensor_copy(AO[mine, SEQ:T], bank[mine, 0:NEW]).then_inc(s["tp_free"], 1)
                    return m

                def gated_sum(tile, m):
                    dve.wait_ge(s["tp_free"], m.at(4))
                    tile = bass.ds(tile, 1)
                    ao = AO[:].rearrange("p (a b) -> p a b", a=1)
                    step(v.scalar_tensor_tensor(out=ao, in0=TGA[:, tile, :], scalar=1.0, in1=ao, op0=ALU.add, op1=ALU.mult))
                    v.scalar_tensor_tensor(out=ao, in0=ao, scalar=2.0, in1=REC[:, tile, :], op0=ALU.mult, op1=ALU.add)\
                        .then_inc(s["mix_sum"], 1)

                def mixed_low(tile):
                    tile = bass.ds(tile, 1)
                    dve.wait_ge(s["mix_hi"], t.next("mix_hi").n)
                    v.scalar_tensor_tensor(out=YL[:, tile, :], in0=AO[:].rearrange("p (a b) -> p a b", a=1), scalar=0.25,
                                           in1=YH[:, tile, :].bitcast(F32), op0=ALU.mult, op1=ALU.subtract).then_inc(s["mixed"], 1)

                def attend(head, tile=None, first=False, last=False, split=UA):
                    following = not (last and head == 1)
                    bank, m01 = take_acc()
                    v.reduce_max(sm[:, 0:1], bank[:, 0, 0:P], AX_X)
                    v.reduce_max(sm[:, 1:2], bank[:, 1, 0:2 * P], AX_X)
                    v.reduce_max(sm[0:NEW, 4:5], bank[0:NEW, 0, P:4 * P], AX_X)
                    step(v.reduce_max(sm[0:NEW, 5:6], bank[0:NEW, 1, 2 * P:T - P], AX_X))
                    step(v.tensor_tensor(sm[0:NEW, 4:5], sm[0:NEW, 4:5], sm[0:NEW, 5:6], ALU.max))
                    negative_max(P, 0, 2)
                    negative_max(NEW, 4, 5).then_inc(s["s_max"], 1)
                    bank, m23 = take_acc()
                    v.reduce_max(sm[:, 2:3], bank[:, 0, 0:3 * P], AX_X)
                    step(v.reduce_max(sm[:, 3:4], bank[:, 1, 0:4 * P], AX_X))
                    negative_max(P, 2, 4).then_inc(s["s_max"], 1)
                    dve.wait_ge(s["p_exp"], t.next("p_exp").n)
                    v.reciprocal(sm[:, 32:34], sm[:, 16:18])
                    step(v.tensor_tensor(sm[0:NEW, 20:21], sm[0:NEW, 20:21], sm[0:NEW, 21:22], ALU.add))
                    v.reciprocal(sm[0:NEW, 36:37], sm[0:NEW, 20:21]).then_inc(s["acc_free"], 1)
                    dve.wait_ge(s["acc_free"], m01.at(2))
                    for k in range(2):
                        v.tensor_scalar(P01[k], P01[k], sm[:, 32 + k:33 + k], None, ALU.mult)
                    v.tensor_scalar(P0[:], P0[:], sm[0:NEW, 36:37], None, ALU.mult).then_inc(s["p01"], 1)
                    if not first:
                        m = head_output(1 - head)
                    if head == 1 and following:
                        key_roots()
                    dve.wait_ge(s["p_exp"], t.next("p_exp").n)
                    v.reciprocal(sm[:, 34:36], sm[:, 18:20]).then_inc(s["acc_free"], 1)
                    dve.wait_ge(s["acc_free"], m23.at(2))
                    v.tensor_scalar(P23[0][:], P23[0][:], sm[:, 34:35], None, ALU.mult)
                    v.tensor_scalar(P23[1][:], P23[1][:], sm[:, 35:36], None, ALU.mult).then_inc(s["p23"], 1)
                    if head == 0:
                        keys_low()
                    if following:
                        queries_low()
                    if tile is not None:
                        gated_sum(tile, m)
                    turned(lambda b: [(PTL[:, 0, :], b[:, 0:P], PTH[:, 0, :]),
                                      (PTL[:, 1:5:3, :], b[:, P:3 * P].rearrange("p (a b) -> p a b", a=2), PTH[:, 1:5:3, :])])
                    if following:
                        query_means()
                    turned(lambda b: [(PSL[0:NEW, 0, :], b[0:NEW, 0:NEW], PSH[0:NEW, 0, :]),
                                      (PSL[:, 1:TT, :], b[:, NEW:TT * NEW].rearrange("p (a b) -> p a b", a=4), PSH[:, 1:TT, :])])
                    if tile is not None:
                        mixed_low(tile)
                    if head == 0 and not last:
                        t.skip("acc", 3)
                    turned(lambda b: [(PTL[:, 2:9:3, :], b[:, 0:3 * P].rearrange("p (a b) -> p a b", a=3), PTH[:, 2:9:3, :])])
                    turned(lambda b: [(PTL[:, 3:13:3, :], b.rearrange("p (a b) -> p a b", a=4), PTH[:, 3:13:3, :])])
                    if following:
                        query_scales()
                    if head == 1 and following:
                        keys_low()
                    if head == 1 and split and not last:
                        split_low(split)

                split_low(UA)
                t.skip("acc", 3)
                key_roots()
                queries_low()
                keys_low()
                query_means()
                query_scales()
                attend(0, first=True)
                for i in t.loop(3, **PER["att", "dve"]):
                    for pair in range(2):
                        attend(1)
                        attend(0, tile=i * 2 + pair)
                attend(1, split=0)
                attend(0, tile=6, last=True)
                attend(1, last=True)
                split_low()
                gated_sum(7, head_output(1))
                mixed_low(7)

                w_region_free()
                output_projection(base + R_NMEM)

                dve.wait_ge(s["mem_in"], 32 * (layer + 1))
                dve.wait_ge(s["mem_sq"], 2 * (layer + 1))
                step(v.tensor_scalar(nwt[:, 0, 0:2], sm[:, 0:2], 1.0 / D, EPS, ALU.mult, ALU.add))
                rsqrt(2)
                for mt in range(2):
                    ins_ = v.tensor_scalar(MEM[:, mt, :], MEM[:, mt, :], nwt[:, 2, mt:mt + 1], None, ALU.mult)
                ins_.then_inc(s["mem_normed"], 1)
                for p4 in range(4):
                    turned(lambda b: [(MTL[:, 2 * p4 + c, :], b[:, c * 2 * P:(c + 1) * 2 * P], MTH[:, 2 * p4 + c, :],
                                       PT[:, 2 * p4 + c, base + R_MEMIN:base + R_MEMIN + 1]) for c in range(2)])
                marker("mc_free").then_inc(s["mc_free"], 1)
                for i in t.loop(2, **PER["mem", "dve"]):
                    for head in range(2):
                        split_low()
                        bank, m = take_acc()
                        dve.wait_ge(s["mem_place"], t.next("mem_place").n)
                        v.tensor_copy(MF[:], bank[:, :, 0:MEM_D]).then_inc(s["acc_free"], 1)
                        split_low()
                        dve.wait_ge(s["mk_sq"], t.next("mk_sq").at(1))
                        t.skip("mk_sq", 1)
                        step(v.tensor_scalar(nwt[:, 0, 0:2], sm[:, 0:2], 1.0 / MEM_D, EPS, ALU.mult, ALU.add))
                        rsqrt(2)
                        for mt in range(2):
                            ins_ = v.scalar_tensor_tensor(out=MF[:, mt, :], in0=MF[:, mt, :], scalar=nwt[:, 2, mt:mt + 1], in1=GMK[:],
                                                          op0=ALU.mult, op1=ALU.mult)
                        ins_.then_inc(s["mk"], 1)
                        bank, m = take_acc()
                        v.tensor_copy(MV[:], bank[:, :, 0:MEM_D]).then_inc(s["acc_free"], 1)
                        split_low()
                        dve.wait_ge(s["vm_hi"], t.next("vm_hi").at(1))
                        t.skip("vm_hi", 1)
                        v.tensor_tensor(VML[:, 0], MV[:], VMH[:, 0].bitcast(F32), ALU.subtract).then_inc(s["mv"], 1)
                        v.tensor_tensor(VML[:, 1], MC[:, :, 1, :], VMH[:, 1].bitcast(F32), ALU.subtract)
                        for dc in range(2):
                            bank, m = take_acc()
                            scaled(QF[:, dc, :], bank, RSTD[:])
                            dve.wait_ge(s["mq_hi"], t.next("mq_hi").n)
                            v.scalar_tensor_tensor(out=QML[:, dc, :], in0=QF[:, dc, :], scalar=PT[:, dc, base + R_MQ:base + R_MQ + 1],
                                                   in1=QMH[:, dc, :].bitcast(F32), op0=ALU.mult, op1=ALU.subtract)
                        for which in range(2):
                            turned(lambda b: [(KML[:, which].rearrange("p a b -> p (a b)"), b, KMH[:, which].rearrange("p a b -> p (a b)"))])
                        marker("mq_lo").then_inc(s["mq_lo"], 1)
                        bank, m = take_tp()
                        token_means(bank, m, MEM_D)
                        rsqrt(TT)
                        step(v.tensor_scalar(sm[:, 24:24 + TT], nwt[:, 2, 0:TT], MEM_D ** -0.5, None, ALU.mult))
                        bank, m = take_acc()
                        step(v.tensor_reduce(sm[:, 0:4], bank.rearrange("p a (b c) -> p (a b) c", b=2), AX_X, ALU.max))
                        v.scalar_tensor_tensor(out=sm[:, 8:12], in0=sm[:, 0:4], scalar=-1.0, in1=sm[:, 24:28], op0=ALU.mult, op1=ALU.mult)\
                            .then_inc(s["s_max"], 1)
                        dve.wait_ge(s["p_exp"], t.next("p_exp").n)
                        v.reciprocal(sm[:, 32:36], sm[:, 16:20]).then_inc(s["acc_free"], 1)
                        dve.wait_ge(s["acc_free"], m.at(2))
                        v.tensor_tensor(PM[:], PM[:], sm[:, 32:36].unsqueeze(2).to_broadcast([P, 4, N_MEM]), ALU.mult).then_inc(s["pm"], 1)
                        bank, m = take_acc()
                        step(v.reduce_max(sm[0:NEW, 4:5], bank[0:NEW, 0, 0:N_MEM], AX_X))
                        v.scalar_tensor_tensor(out=sm[0:NEW, 12:13], in0=sm[0:NEW, 4:5], scalar=-1.0, in1=sm[0:NEW, 28:29],
                                               op0=ALU.mult, op1=ALU.mult).then_inc(s["s_max"], 1)
                        dve.wait_ge(s["p_exp"], t.next("p_exp").n)
                        v.reciprocal(sm[0:NEW, 36:37], sm[0:NEW, 20:21]).then_inc(s["acc_free"], 1)
                        dve.wait_ge(s["acc_free"], m.at(2))
                        v.tensor_scalar(SQT[0:NEW, 0:N_MEM], SQT[0:NEW, 0:N_MEM], sm[0:NEW, 36:37], None, ALU.mult).then_inc(s["pms"], 1)
                        for mt in range(2):
                            turned(lambda b: [(PML[:, mt, 0:SEQ], b, PMH[:, mt, 0:SEQ])])
                        turned(lambda b: [(PML[:, :, SEQ:T], b[:, 0:2 * NEW].rearrange("p (a b) -> p a b", a=2), PMH[:, :, SEQ:T])])
                        for dc in range(2):
                            row = bass.ds(i * 4 + (2 * head + dc), 1)
                            turned_acc(lambda b: [(YL[:, row, 0:SEQ], b[:, 0:1, :], YH[:, row, 0:SEQ]),
                                                  (YL[:, row, SEQ:T], b[:, 1:2, 0:NEW], YH[:, row, SEQ:T])])
                        marker("mc_free").then_inc(s["mc_free"], 1)
                w_region_free()
                output_projection(base + R_NFFN)

                def hidden_tiles(tiles):
                    for pair in range(tiles // 2):
                        for f in range(2):
                            bank, m = take_acc()
                            scaled(H1[:, f, :], bank, RSTD[:])
                            if f == 0:
                                split_low()
                        dve.wait_ge(s["f_th"], t.next("f_th").n)
                        step(v.scalar_tensor_tensor(out=H1[:], in0=TH[:], scalar=1.0, in1=H1[:], op0=ALU.add, op1=ALU.mult))
                        for f in range(2):
                            bank, m = take_acc()
                            scaled(TH[:, f, :], bank, GR[:])
                            if f == 0:
                                split_low()
                        dve.wait_ge(s["acc_free"], m.at(2))
                        v.tensor_tensor(H1[:], H1[:], TH[:], ALU.mult).then_inc(s["f_hid"], 1)
                        dve.wait_ge(s["f_hi"], t.next("f_hi").n)
                        v.tensor_tensor(YL[:, 2 * pair:2 * pair + 2, :], H1[:], YH[:, 2 * pair:2 * pair + 2, :].bitcast(F32), ALU.subtract)\
                            .then_inc(s["hidden"], 1)
                        dve.wait_ge(s["hidden"], t.next("hidden").n)

                def add_tiles(row=None):
                    for k in range(C):
                        bank, m = take_acc()
                        add_residual(bank, m, k)
                        if k % 2 == 0:
                            split_low()
                        if row is not None:
                            dve.wait_ge(s["acc_free"], m.at(2))
                            prepare(k, row)
                    return m

                if layer == 0:
                    step(v.tensor_scalar(GR[:], RSTD[:], 0.5, None, ALU.mult))
                    for i in t.loop(2, **PER["dense", "dve"]):
                        hidden_tiles(8)
                        add_tiles()
                    step(v.memset(SQ[:], 0.0))
                    hidden_tiles(6)
                    add_tiles(ROWS + R_MIX)
                else:
                    dve.wait_ge(s["router_in"], 48)
                    step(v.memset(LG[:], 0.0))
                    dve.wait_ge(s["router_hi"], 1)
                    v.tensor_tensor(RWL[:], RW[:], RWH[:].bitcast(F32), ALU.subtract).then_inc(s["router"], 1)
                    bank, m = take_tp()
                    for tt in range(TT):
                        r = rows(tt)
                        ins_ = v.scalar_tensor_tensor(out=LG[0:r, 0, tt, :], in0=bank[0:r, tt * EXPERTS:(tt + 1) * EXPERTS],
                                                      scalar=rt[0:r, tt:tt + 1], in1=RB[0:r, :], op0=ALU.mult, op1=ALU.add)
                    ins_.then_inc(s["tp_free"], 1)
                    dve.wait_ge(s["tp_free"], m.at(4))
                    col = lambda k: nwt[:, k, 0:TT].unsqueeze(2).to_broadcast([P, TT, EXPERTS])
                    step(v.tensor_reduce(nwt[:, 0, 0:TT], LG[:, 0], AX_X, ALU.max))
                    v.tensor_tensor(LG[:, 1], LG[:, 0], col(0), ALU.subtract).then_inc(s["lg_shift"], 1)
                    dve.wait_ge(s["lg_exp"], 1)
                    step(v.tensor_reduce(nwt[:, 0, 0:TT], LG[:, 1], AX_X, ALU.add))
                    step(v.reciprocal(nwt[:, 1, 0:TT], nwt[:, 0, 0:TT]))
                    step(v.tensor_tensor(LG[:, 1], LG[:, 1], col(1), ALU.mult))
                    for tt in range(TT):
                        step(v.max(LG[:, 2, tt, :], LG[:, 1, tt, :]))
                        step(v.max_index(LI[:, tt, :], LG[:, 2, tt, :], LG[:, 1, tt, :]))
                    step(v.tensor_copy(LG[:, 3], LI[:]))
                    iota = IOT[:, :].unsqueeze(1).to_broadcast([P, TT, EXPERTS])
                    first, second = (LG[:, 3, :, k:k + 1].to_broadcast([P, TT, EXPERTS]) for k in range(2))
                    v.tensor_tensor(LG[:, 4], iota, first, ALU.is_equal)
                    step(v.tensor_tensor(LG[:, 5], iota, second, ALU.is_equal))
                    step(v.tensor_tensor(LG[:, 4], LG[:, 4], LG[:, 5], ALU.add))
                    step(v.tensor_tensor(LG[:, 4], LG[:, 4], LG[:, 1], ALU.mult))
                    step(v.tensor_reduce(nwt[:, 0, 0:TT], LG[:, 4], AX_X, ALU.add))
                    step(v.reciprocal(nwt[:, 1, 0:TT], nwt[:, 0, 0:TT]))
                    v.tensor_tensor(LG[:, 7], LG[:, 4], col(1), ALU.mult).then_inc(s["gates"], 1)
                    bank, m = take_acc()
                    v.tensor_copy(GT[:, 0:SEQ], bank[0:EXPERTS, 0, :])
                    v.tensor_copy(GT[:, SEQ:T], bank[0:EXPERTS, 1, 0:NEW]).then_inc(s["acc_free"], 1)
                    dve.wait_ge(s["acc_free"], m.at(2))
                    for i in t.loop(EXPERTS, **PER["moe", "dve"]):
                        v.tensor_scalar(GM[:], GT[:], ident[0:EXPERTS, bass.ds(i, 1)], None, ALU.mult).then_inc(s["gate_row"], 1)
                        for k in range(4):
                            bank, m = take_tp()
                            cols = slice(k * (T // 4), (k + 1) * (T // 4))
                            v.scalar_tensor_tensor(out=GR[:, cols], in0=bank[:, 0:T // 4], scalar=0.5, in1=RSTD[:, cols],
                                                   op0=ALU.mult, op1=ALU.mult).then_inc(s["tp_free"], 1)
                        dve.wait_ge(s["tp_free"], m.at(4))
                        hidden_tiles(8)
                        m = add_tiles()
                    dve.wait_ge(s["acc_free"], t.last("acc", 2))
                    marker("y_done").then_inc(s["y_done"], 1)
                marker("outc").then_inc(s["outc"], 1)
                bank, m = take_acc()
                v.tensor_copy(YO[0:8, 0, 0:512], bank[0:8, 0, :])
                v.tensor_copy(YO[0:8, 0, 512:D], bank[0:8, 1, :]).then_inc(s["acc_free"], 1)
                dve.wait_ge(s["acc_free"], m.at(2))
                marker("state_rows").then_inc(s["state_rows"], 1)

            dve.wait_ge(s["state_out"], 64 * DEPTH)
            for tt in range(TT):
                bank, m = take_acc()
                if tt >= 2:
                    dve.wait_ge(s["y_out%d" % (tt % 2)], 16 * (tt // 2))
                r = rows(tt)
                v.tensor_copy(YO[0:r, tt % 2, 0:512], bank[0:r, 0, :])
                v.tensor_copy(YO[0:r, tt % 2, 512:D], bank[0:r, 1, :]).then_inc(s["acc_free"], 1)
                dve.wait_ge(s["acc_free"], m.at(2))
                marker("y_rows").then_inc(s["y_rows"], 1)

        @block.gpsimd
        def _(pool):
            t = Tally(pool)
            load = pool.dma_start
            for name, n in (("acc_free", 2), ("tp_free", 4), ("w_lo", 2), ("mem_place", 1)):
                pool.sem_inc(s[name], n)
            nc.gpsimd.memset(ident[:], 0.0).then_inc(s["consts"], 1)
            nc.gpsimd.memset(PST[:], 0.0).then_inc(s["pst"], 1)
            nc.gpsimd.memset(MK[:, P:P + NEW].bitcast(F32), 0.0)
            nc.gpsimd.memset(ones[:], 1.0).then_inc(s["consts"], 1)
            pool.wait_ge(s["consts"], 2)
            nc.gpsimd.affine_select(out=ident[:], in_=ident[:], compare_op=ALU.not_equal, fill=1.0, base=0, pattern=[[-1, P]],
                                    channel_multiplier=1).then_inc(s["consts"], 1)
            nc.gpsimd.memset(MK[:, 0:NEW].bitcast(F32), 1.0)
            nc.gpsimd.memset(MK[:, NEW:P].bitcast(F32), 0.0)
            nc.gpsimd.memset(MK[:, P + NEW:2 * P].bitcast(F32), MASKED).then_inc(s["consts"], 1)
            pool.wait_ge(s["pst"], 1)
            n = 0
            for layer in range(DEPTH):
                r = layer * ROWS
                row = lambda ap: ap.rearrange("(o n) -> o n", o=1)
                for at0, count, width, src in (
                        (R_MIX, 1, D, row(ins["norm_mix"][layer])), (R_CW, 4, D, ins["conv_w"][layer]), (R_CB, 1, D, row(ins["conv_b"][layer])),
                        (R_BA, 1, D, row(ins["lru_ba"][layer])), (R_BI, 1, D, row(ins["lru_bi"][layer])),
                        (R_LAM, 1, D, row(ins["lru_lambda"][layer])), (R_NMEM, 1, D, row(ins["norm_mem"][layer])),
                        (R_NFFN, 1, D, row(ins["norm_ffn"][layer])), (R_CONV, 3, D, ins["state_conv"][layer, 0]),
                        (R_LRU, 1, D, ins["state_lru"][layer]), (R_MEMIN, 1, D, row(ins["mem_in_norm"][layer])),
                        (R_QLAT, 1, Q_LORA, row(ins["q_lat_norm"][layer])), (R_MQ, 1, MEM_D, row(ins["mq_head_norm"][layer])),
                        (R_QH, 1, QK, row(ins["q_head_norm"][layer])), (R_KH, 1, QK, row(ins["k_head_norm"][layer]))):
                    load(PST[r + at0:r + at0 + count, 0:width], src).then_inc(s["params_in"], 16)
                    n += 1
                for at0, name in ((R_QH, "q_head_norm"), (R_KH, "k_head_norm")):
                    g = row(ins[name][layer])
                    load(PST[r + at0:r + at0 + 1, 96:112], g[:, 80:96]).then_inc(s["params_in"], 16)
                    load(PST[r + at0:r + at0 + 1, 112:128], g[:, 64:80]).then_inc(s["params_in"], 16)
                    n += 2
            assert n == PARAM_DMAS
            load(TOK[:, 0:4, :], ins["x_prompt"][0].rearrange("(t p) d -> p t d", p=P)).then_inc(s["tokens_in"], 16)
            load(TOK[0:NEW, 4, :], ins["x_sample"][0]).then_inc(s["tokens_in"], 16)
            for layer in range(DEPTH):
                pool.wait_ge(s["w_free"], 4 * layer + 1)
                if layer:
                    pool.wait_ge(s["state_out"], 64 * layer)
                nc.gpsimd.memset(BD[:], 0.0).then_inc(s["bd_zero"], 1)
                pool.wait_ge(s["bd_zero"], layer + 1)
                for gate, name in enumerate(("lru_wa", "lru_wi")):
                    w = ins[name][layer].rearrange("(c two) i j -> two i c j", two=2)
                    for half in range(2):
                        load(BD[half * 64:half * 64 + 64, gate, :, half * 64:half * 64 + 64], w[half]).then_inc(s["blocks_in"], 16)
                pool.wait_ge(s["w_free"], 4 * layer + 2)
                load(CKP[:], ins["cache_ckv"][layer, 0].rearrange("(t p) d -> p t d", p=P)).then_inc(s["past_in"], 16)
                load(rp[:, TT:KT, :], ins["cache_krope"][layer, 0].rearrange("(t p) d -> p t d", p=P)).then_inc(s["past_in"], 16)
                load(RPT[:, 0:4], ins["rope_tok"][0:SEQ].rearrange("(t p) a d -> p t a d", p=P)).then_inc(s["latents_in"], 16)
                load(RPT[0:NEW, 4], ins["rope_tok"][SEQ:T]).then_inc(s["latents_in"], 16)
                load(GKV[:], ins["kv_lat_norm"][layer].partition_broadcast(P)).then_inc(s["latents_in"], 16)
                load(RSTD[:], ins["rope_rows"]).then_inc(s["rope_in"], 16)
                pool.wait_ge(s["zkv"], layer + 1)
                kv = slice(Q_LORA, Q_LORA + KV_LORA)
                load(outs["new_ckv_p"][layer, 0].rearrange("(t p) d -> p t d", p=P), Z[:, 0:4, kv]).then_inc(s["latents_out"], 16)
                load(outs["new_ckv_s"][layer, 0], Z[0:NEW, 4, kv]).then_inc(s["latents_out"], 16)
                pool.wait_ge(s["rotated"], layer + 1)
                load(outs["new_krope_p"][layer, 0].rearrange("(t p) d -> p t d", p=P), rp[:, 0:4, :]).then_inc(s["latents_out"], 16)
                load(outs["new_krope_s"][layer, 0], rp[0:NEW, 4, :]).then_inc(s["latents_out"], 16)
                tt_ = nc.gpsimd.tensor_tensor

                def step(ins_):
                    ins_.then_inc(s["pool_step"], 1)
                    pool.wait_ge(s["pool_step"], t.next("pool_step").n)

                def assemble_keys():
                    pool.wait_ge(s["k_sq"], t.next("k_sq").n)
                    v, n, half = nc.gpsimd, 2 * KT, ROPE // 2
                    x, y = (RK[:, k, 0:n] for k in (0, 2))
                    step(v.tensor_tensor(KA[:, :, :, 0:32], KA[:, :, :, 0:32], KA[:, :, :, 32:64], ALU.add))
                    step(v.tensor_tensor(KA[:, :, :, 0:16], KA[:, :, :, 0:16], KA[:, :, :, 16:32], ALU.add))
                    step(v.tensor_tensor(KA[:, :, :, 0:8], KA[:, :, :, 0:8], KA[:, :, :, 8:16], ALU.add))
                    step(v.tensor_tensor(KA[:, :, :, 0:4], KA[:, :, :, 0:4], KA[:, :, :, 4:8], ALU.add))
                    step(v.tensor_tensor(KA[:, :, :, 0:2], KA[:, :, :, 0:2], KA[:, :, :, 2:4], ALU.add))
                    both = x.rearrange("p (t h o) -> p t h o", h=2, o=1)
                    step(v.tensor_tensor(both, KA[:, :, :, 0:1], KA[:, :, :, 1:2], ALU.add))
                    both = x.rearrange("p (t h) -> p t h", h=2)
                    v.tensor_tensor(both, both, krs[:, :].unsqueeze(2).to_broadcast([P, KT, 2]), ALU.add).then_inc(s["k_sum"], 1)
                    pool.wait_ge(s["rk"], t.next("rk").n)
                    for head in range(2):
                        by = lambda n: y.rearrange("p (t h) -> p t h", h=2)[:, :, head:head + 1].to_broadcast([P, KT, n])
                        tt_(KA[:, :, head, 0:NOPE], KF[:, :, head, :], by(NOPE), ALU.mult)
                        tt_(KA[:, :, head, NOPE:QK], rp[:], by(ROPE), ALU.mult)
                        tt_(KA[:, :, head, QK:QK + half], rp[:, :, half:ROPE], by(half), ALU.mult)
                        ins_ = tt_(KA[:, :, head, QK + half:P], rp[:, :, 0:half], by(half), ALU.mult)
                    ins_.then_inc(s["ka"], 1)

                def values_low():
                    pool.wait_ge(s["v_hi"], t.next("v_hi").n)
                    tt_(key_tiles(VL, 0, 6), VF(0, 6), key_tiles(VH, 0, 6).bitcast(F32), ALU.subtract)
                    tt_(key_tiles(VL, 6, 3), VF(6, 3), key_tiles(VH, 6, 3).bitcast(F32), ALU.subtract).then_inc(s["v_lo"], 1)

                assemble_keys()
                for i in t.loop(N_HEADS // 2 - 1, v_hi=1, k_sq=1, pool_step=6, rk=1):
                    values_low()
                    assemble_keys()
                values_low()
                pool.wait_ge(s["w_free"], 4 * layer + 3)
                load(MEM[:], ins["mem_prompt"][0].rearrange("(t p) d -> p t d", p=P)).then_inc(s["mem_in"], 16)
                load(GMK[:], ins["mk_head_norm"][layer].partition_broadcast(P)).then_inc(s["mem_in"], 16)
                for head in range(MEM_HEADS):
                    n = layer * MEM_HEADS + head
                    pool.wait_ge(s["mc_free"], 5 * layer + head + 1)
                    load(MC[:, :, 0, :], ins["cache_mem_k"][layer, 0, :, head, :].rearrange("(t p) d -> p t d", p=P)).then_inc(s["mc_in"], 16)
                    load(MC[:, :, 1, :], ins["cache_mem_v"][layer, 0, :, head, :].rearrange("(t p) d -> p t d", p=P)).then_inc(s["mc_in"], 16)
                    pool.wait_ge(s["mv"], n + 1)
                    load(outs["new_mem_k_p"][layer, 0, :, head, :].rearrange("(t p) d -> p t d", p=P), MF[:]).then_inc(s["mem_out"], 16)
                    load(outs["new_mem_v_p"][layer, 0, :, head, :].rearrange("(t p) d -> p t d", p=P), MV[:]).then_inc(s["mem_out"], 16)
                    pool.wait_ge(s["mem_out"], 32 * (n + 1))
                    pool.sem_inc(s["mem_place"], 1)
                pool.wait_ge(s["w_free"], 4 * layer + 4)
                if layer == 1:
                    load(RW[:], ins["moe_router"][0].rearrange("(c p) e -> p c e", p=P)).then_inc(s["router_in"], 16)
                    load(RB[:], ins["moe_router_b"][0].partition_broadcast(P)).then_inc(s["router_in"], 16)
                    load(IOT[:], ins["expert_numbers"]).then_inc(s["router_in"], 16)
                pool.wait_ge(s["state_rows"], layer + 1)
                load(outs["new_conv_p"][layer, 0], YO[0:3, 0, :]).then_inc(s["state_out"], 16)
                load(outs["new_lru_p"][layer], YO[3:4, 0, :]).then_inc(s["state_out"], 16)
                load(outs["new_conv_s"][layer, 0], YO[4:7, 0, :]).then_inc(s["state_out"], 16)
                load(outs["new_lru_s"][layer], YO[7:8, 0, :]).then_inc(s["state_out"], 16)
            pool.wait_ge(s["latents_out"], 64 * DEPTH)
            pool.wait_ge(s["mem_out"], 32 * MEM_HEADS * DEPTH)
            pool.wait_ge(s["state_out"], 64 * DEPTH)

        @block.sync
        def _(sp):
            t = Tally(sp)

            def unit(*pieces):
                m = t.next("unit")
                k = m.slot(2)
                sp.wait_ge(s["w_lo"], m.n)
                for dst, src in pieces:
                    sp.dma_start(dst(RAW[:, k]), src).then_inc(s["landed%d" % k], LANDED // len(pieces))

            def rows_of(w, tiles=C):
                return w.rearrange("(c p) n -> p c n", p=P)

            def columns(w, at0, n=UW, tiles=C):
                cols = slice(at0, at0 + n) if isinstance(at0, int) else bass.ds(at0, n)
                unit((lambda raw: unit3(raw)[:, 0:tiles, 0:n], rows_of(w)[:, :, cols]))

            GREC = 2 * D + LAT
            for layer in range(DEPTH):
                w_in = ins["w_in"][layer]
                for i in t.loop(4, unit=4):
                    for at0 in (0, D, GREC + D, GREC):
                        columns(w_in, i * UW + at0)
                for k, n in enumerate((UW, UW, LAT - 2 * UW)):
                    columns(w_in, 2 * D + k * UW, n)
                for i in t.loop(4, unit=2):
                    for group in range(2):
                        uq = ins["w_uq"][layer].rearrange("(c p) (h n) -> p c h n", p=P, n=QK)
                        q = lambda raw: raw[:, 0:768].rearrange("p (c h n) -> p c h n", c=3, h=2)
                        kv = lambda raw: raw[:, 768:1280].rearrange("p (c n) -> p c n", c=2)
                        m = t.next("unit")
                        k = m.slot(2)
                        sp.wait_ge(s["w_lo"], m.n)
                        heads = [bass.ds(i * 4 + group * 2 + h, 1) for h in range(2)]
                        for h in range(2):
                            sp.dma_start(q(RAW[:, k])[:, :, h:h + 1, 0:QK], uq[:, :, heads[h], :]).then_inc(s["landed%d" % k], 16)
                        for h in range(2):
                            sp.dma_start(q(RAW[:, k])[:, :, h:h + 1, QK:P], uq[:, :, heads[h], NOPE:QK]).then_inc(s["landed%d" % k], 16)
                        for j, name in enumerate(("w_uk", "w_uv")):
                            sp.dma_start(kv(RAW[:, k])[:, :, j * P:(j + 1) * P],
                                         rows_of(ins[name][layer])[:, :, bass.ds(i * 256 + group * P, P)]).then_inc(s["landed%d" % k], 16)
                sp.wait_ge(s["v_lo"], 8 * (layer + 1))
                for i in t.loop(2, unit=2):
                    for u in range(2):
                        columns(ins["w_out"][layer], i * 512 + u * UW)
                for i in t.loop(2, unit=6):
                    for head in range(2):
                        for name in ("w_mk", "w_mv", "w_mq"):
                            columns(ins[name][layer], i * 512 + head * UW)
                for i in t.loop(2, unit=2):
                    for u in range(2):
                        columns(ins["w_mo"][layer], i * 512 + u * UW)

                def ffn(w1, w3, w2, at0, tiles):
                    for pair in range(tiles // 2):
                        columns(w1, at0 + pair * UW)
                        columns(w3, at0 + pair * UW)
                    for k in range(4):
                        columns(w2, k * UW, tiles=tiles)

                if layer == 0:
                    w1, w3, w2 = (ins[n][0] for n in ("ffn_w1", "ffn_w3", "ffn_w2"))
                    for i in t.loop(2, unit=12):
                        ffn(w1, w3, w2[bass.ds(i * 1024, 1024), :], i * 1024, 8)
                    ffn(w1, w3, w2[2048:D_FF, :], 2048, 6)
                else:
                    for i in t.loop(EXPERTS, unit=12):
                        w1, w3, w2 = (ins[n][0, bass.ds(i, 1)].rearrange("o a b -> (o a) b") for n in ("moe_w1", "moe_w3", "moe_w2"))
                        ffn(w1, w3, w2, 0, 8)
            m = t.next("unit")
            sp.wait_ge(s["w_lo"], m.n)
            sp.sem_inc(s["landed%d" % m.slot(2)], LANDED)
            for tt in range(TT):
                sp.wait_ge(s["y_rows"], tt + 1)
                dst = outs["y_prompt"][0, tt * P:(tt + 1) * P, :] if tt < 4 else outs["y_sample"][0]
                sp.dma_start(dst, YO[0:rows(tt), tt % 2, :]).then_inc(s["y_out%d" % (tt % 2)], 16)
            sp.wait_ge(s["y_out0"], 48)
            sp.wait_ge(s["y_out1"], 32)


_INS = ['x_prompt', 'x_sample', 'cache_ckv', 'cache_krope', 'cache_mem_k', 'cache_mem_v', 'state_lru', 'state_conv',
        'mem_prompt', 'norm_mix', 'w_in', 'conv_w', 'conv_b', 'lru_wa', 'lru_ba', 'lru_wi', 'lru_bi', 'lru_lambda',
        'q_lat_norm', 'w_uq', 'kv_lat_norm', 'w_uk', 'w_uv', 'q_head_norm', 'k_head_norm', 'w_out',
        'norm_mem', 'mem_in_norm', 'w_mq', 'w_mk', 'w_mv', 'w_mo', 'mq_head_norm', 'mk_head_norm',
        'norm_ffn', 'ffn_w1', 'ffn_w3', 'ffn_w2', 'moe_router', 'moe_router_b', 'moe_w1', 'moe_w3', 'moe_w2']
_OUTS = [('y_prompt', (1, 512, 1024)), ('y_sample', (1, 64, 1024)), ('new_ckv_p', (2, 1, 512, 256)),
         ('new_krope_p', (2, 1, 512, 32)), ('new_lru_p', (2, 1, 1024)), ('new_conv_p', (2, 1, 3, 1024)),
         ('new_mem_k_p', (2, 1, 256, 4, 256)), ('new_mem_v_p', (2, 1, 256, 4, 256)),
         ('new_ckv_s', (2, 1, 64, 256)), ('new_krope_s', (2, 1, 64, 32)), ('new_lru_s', (2, 1, 1024)),
         ('new_conv_s', (2, 1, 3, 1024))]


def rope_tables():
    import numpy as _np
    half = 16
    inv_freq = (_np.float32(10000.0) ** (-_np.arange(half, dtype=_np.float32) / _np.float32(half))).astype(_np.float32)
    ang = _np.arange(576, dtype=_np.float32)[None, :] * inv_freq[:, None]
    cos, sin = _np.cos(ang), _np.sin(ang)
    tok = _np.stack([_np.concatenate([cos, cos]), _np.concatenate([-sin, sin])]).transpose(2, 0, 1)
    rows = _np.concatenate([_np.ones((64, 576)), cos, cos, sin, -sin])
    return _np.ascontiguousarray(tok, _np.float32), _np.ascontiguousarray(rows, _np.float32)


def kernel(**inputs):
    import numpy as _np
    import concourse.bacc as _bacc
    from concourse import mybir as _mybir
    from concourse.bass_utils import run_bass_kernel_spmd as _run

    nc = _bacc.Bacc("TRN2", target_bir_lowering=False, num_devices=1)
    arrays, ins, outs = {}, {}, {}
    tensors = {name: inputs[name] for name in _INS}
    tensors['rope_tok'], tensors['rope_rows'] = rope_tables()
    tensors['expert_numbers'] = _np.tile(_np.arange(8, dtype=_np.float32), (128, 1))
    for name, a in tensors.items():
        a = _np.ascontiguousarray(a)
        arrays[f"in_{name}_dram"] = a
        ins[name] = nc.dram_tensor(f"in_{name}_dram", a.shape, _mybir.dt.from_np(a.dtype), kind="ExternalInput").ap()
    for name, shape in _OUTS:
        outs[name] = nc.dram_tensor(f"out_{name}_dram", shape, _mybir.dt.float32, kind="ExternalOutput").ap()
    stream_step_kernel(nc, ins, outs)
    r = _run(nc, [arrays], core_ids=[0])
    return tuple(r.results[0][f"out_{name}_dram"] for name, _ in _OUTS)
```
